# Optimizing a Trainium2 kernel written in Bass

```python
import math
import jax
import jax.numpy as jnp
from jax import lax
import numpy as np
import jax, jax.numpy as jnp

D_MODEL = 1024
BATCH = 1
SEQ = 256
DEPTH = 2

GRID_W = 64
CTX_LEN = 256
N_EVEN = (DEPTH + 1) // 2
N_ODD = DEPTH // 2
NORM_EPS = 1e-6
ROPE_THETA = 10000.0
N_MOD = 6

ML_HEADS = 4
ML_DQK = 64
ML_DV = 128
ML_CHUNK = 64
ML_CONV = 3
ML_W = ML_HEADS * ML_DV

DA_HEADS = 4
DA_DQK = 64
DA_DV = 128
DA_W = DA_HEADS * DA_DV
Q_BLOCK = 128

EVEN_SIZES = (2 * ML_HEADS * ML_DQK, ML_W, ML_W, 4 * ML_HEADS,
              DA_HEADS * 2 * DA_DQK, DA_HEADS * 2 * DA_DQK, DA_W)
EVEN_IN = sum(EVEN_SIZES)
EVEN_SPLITS = tuple(sum(EVEN_SIZES[:i + 1]) for i in range(len(EVEN_SIZES) - 1))
MIX_W = ML_W + DA_W

WA_HEADS = 16
WA_KV_HEADS = 4
WA_GROUP = WA_HEADS // WA_KV_HEADS
WA_DH = 64
WINDOW = 128
W_BLOCK = WINDOW
WA_W = WA_HEADS * WA_DH
WA_KV_W = WA_KV_HEADS * WA_DH
ODD_IN = WA_W + 2 * WA_KV_W
ODD_SPLITS = (WA_W, WA_W + WA_KV_W)

PEER_HEADS = 8
PEER_NKEYS = 128
PEER_EXPERTS = PEER_NKEYS * PEER_NKEYS
PEER_DQ = 256
PEER_DHALF = PEER_DQ // 2
PEER_TOPK = 16
PEER_TOK_BLOCK = 128


def _rmsnorm(x, g):
    xf = x.astype(jnp.float32)
    y = xf * lax.rsqrt(jnp.mean(xf * xf, axis=-1, keepdims=True) + NORM_EPS)
    return (y * g.astype(jnp.float32)).astype(x.dtype)

def _headnorm(x, g):
    xf = x.astype(jnp.float32)
    y = xf * lax.rsqrt(jnp.mean(xf * xf, axis=-1, keepdims=True) + NORM_EPS)
    y = y * g.astype(jnp.float32).reshape(x.shape[-2:])
    return y.reshape(x.shape[:-2] + (-1,))

def _axial_rope_tables(n_tok, dim):
    rows = n_tok // GRID_W
    r = jnp.repeat(jnp.arange(rows, dtype=jnp.float32), GRID_W)
    col = jnp.broadcast_to(jnp.arange(GRID_W, dtype=jnp.float32), (rows, GRID_W)).reshape(-1)
    nf = dim // 4
    inv = ROPE_THETA ** (-jnp.arange(nf, dtype=jnp.float32) / nf)
    ang = jnp.concatenate([r[:, None] * inv, col[:, None] * inv], axis=-1)
    return jnp.cos(ang), jnp.sin(ang)

def _apply_rope(x, cos, sin):
    shp = (x.shape[1],) + (1,) * (x.ndim - 3) + (cos.shape[-1],)
    cs = cos.reshape(shp)
    sn = sin.reshape(shp)
    xf = x.astype(jnp.float32)
    x1, x2 = jnp.split(xf, 2, axis=-1)
    return jnp.concatenate([x1 * cs - x2 * sn, x1 * sn + x2 * cs], axis=-1).astype(x.dtype)

def _centred_conv(x, w, b):
    taps = w.shape[0]
    p = taps // 2
    t = x.shape[1]
    xp = jnp.pad(x, ((0, 0), (p, p), (0, 0)))
    out = b
    for j in range(taps):
        out = out + xp[:, j:j + t] * w[j]
    return out

def _mlstm_prepare(qk, v, g, conv_w, conv_b, gate_b):
    bsz, t, _ = qk.shape
    qk = jax.nn.silu(_centred_conv(qk, conv_w, conv_b))
    q, k = jnp.split(qk, 2, axis=-1)

    def heads(a, d):
        return a.reshape(bsz, t, ML_HEADS, d).transpose(0, 2, 1, 3).astype(jnp.float32)

    q = heads(q, ML_DQK)
    k = heads(k, ML_DQK) * (ML_DQK ** -0.5)
    v = heads(v, ML_DV)
    g = (g + gate_b).astype(jnp.float32).reshape(bsz, t, 4, ML_HEADS).transpose(2, 0, 3, 1)
    return (q, k, v, g[0], jax.nn.log_sigmoid(g[1]), g[2], jax.nn.log_sigmoid(g[3]))

def _mlstm_state0(bsz):
    return (jnp.zeros((bsz, ML_HEADS, ML_DV, ML_DQK), jnp.float32),
            jnp.zeros((bsz, ML_HEADS, ML_DQK), jnp.float32),
            jnp.zeros((bsz, ML_HEADS), jnp.float32))

def _mlstm_chunk_scan(q, k, v, ig, lf, state):
    bsz, nh, t, _ = q.shape
    nc = t // ML_CHUNK

    def to_chunks(a):
        return jnp.moveaxis(a.reshape((bsz, nh, nc, ML_CHUNK) + a.shape[3:]), 2, 0)

    tri = jnp.tril(jnp.ones((ML_CHUNK, ML_CHUNK), dtype=bool))

    def step(carry, xs):
        c_st, n_st, m_st = carry
        qc, kc, vc, ic, fc = xs
        b = jnp.cumsum(fc, axis=-1)
        log_d = jnp.where(tri, b[..., :, None] - b[..., None, :] + ic[..., None, :], -jnp.inf)
        inter = b + m_st[..., None]
        m_t = jnp.maximum(inter, jnp.max(log_d, axis=-1))
        s = jnp.einsum('bhtd,bhsd->bhts', qc, kc) * jnp.exp(log_d - m_t[..., None])
        w_inter = jnp.exp(inter - m_t)
        num = (jnp.einsum('bhts,bhsv->bhtv', s, vc)
               + w_inter[..., None] * jnp.einsum('bhvd,bhtd->bhtv', c_st, qc))
        den = jnp.sum(s, axis=-1) + w_inter * jnp.einsum('bhd,bhtd->bht', n_st, qc)
        h = num / jnp.maximum(jnp.abs(den), jnp.exp(-m_t))[..., None]
        b_last = b[..., -1]
        log_w = b_last[..., None] - b + ic
        m_new = jnp.maximum(b_last + m_st, jnp.max(log_w, axis=-1))
        wk = jnp.exp(log_w - m_new[..., None])
        decay = jnp.exp(b_last + m_st - m_new)
        c_new = decay[..., None, None] * c_st + jnp.einsum('bhs,bhsv,bhsd->bhvd', wk, vc, kc)
        n_new = decay[..., None] * n_st + jnp.einsum('bhs,bhsd->bhd', wk, kc)
        return (c_new, n_new, m_new), h

    state, hs = lax.scan(step, state, tuple(to_chunks(a) for a in (q, k, v, ig, lf)))
    h = jnp.moveaxis(hs, 0, 2).reshape(bsz, nh, t, -1)
    return h, state

def _mlstm_bidir(lat, ctx_in):
    ql, kl, vl, il_f, fl_f, il_b, fl_b = lat
    qc, kc, vc, ic_f, fc_f, ic_b, fc_b = ctx_in
    bsz = ql.shape[0]

    def rev(a):
        return jnp.flip(a, axis=2)

    hc_f, st_f = _mlstm_chunk_scan(qc, kc, vc, ic_f, fc_f, _mlstm_state0(bsz))
    hl_f, _ = _mlstm_chunk_scan(ql, kl, vl, il_f, fl_f, st_f)
    hc_b, st_b = _mlstm_chunk_scan(rev(qc), rev(kc), rev(vc), rev(ic_b), rev(fc_b), _mlstm_state0(bsz))
    hl_b, _ = _mlstm_chunk_scan(rev(ql), rev(kl), rev(vl), rev(il_b), rev(fl_b), st_b)
    return hl_f + rev(hl_b), hc_f + rev(hc_b)

def _mlstm_out(h, o, g, dtype):
    y = _headnorm(h.transpose(0, 2, 1, 3), g)
    return (y * jax.nn.sigmoid(o.astype(jnp.float32))).astype(dtype)

def _da_heads(q, k, v):
    bsz, t, _ = q.shape
    return (q.reshape(bsz, t, DA_HEADS, 2, DA_DQK),
            k.reshape(bsz, t, DA_HEADS, 2, DA_DQK),
            v.reshape(bsz, t, DA_HEADS, DA_DV))

def _diff_lambda(lp, lam_init):
    lp = lp.astype(jnp.float32)
    return jnp.exp(jnp.sum(lp[0] * lp[1])) - jnp.exp(jnp.sum(lp[2] * lp[3])) + lam_init

def _diff_attend(q, k, v, lam):
    s = jnp.einsum('bqhmd,bkhmd->bhmqk', q, k).astype(jnp.float32) * (DA_DQK ** -0.5)
    p = jax.nn.softmax(s, axis=-1)
    p = p[:, :, 0] - lam * p[:, :, 1]
    return jnp.einsum('bhqk,bkhv->bqhv', p.astype(v.dtype), v)

def _blocked_queries(fn, q):
    bsz, s = q.shape[:2]
    nb = s // Q_BLOCK
    qb = jnp.moveaxis(q.reshape((bsz, nb, Q_BLOCK) + q.shape[2:]), 1, 0)
    out = jnp.moveaxis(lax.map(fn, qb), 0, 1)
    return out.reshape((bsz, s) + out.shape[3:])

def _da_out(o, g, lam_init, dtype):
    return (_headnorm(o, g) * (1.0 - lam_init)).astype(dtype)

def _even_mixer(xl, xc, w_in, conv_w, conv_b, gate_b, ml_g, da_lam, da_g, w_out,
                lam_init, cos, sin, need_ctx):
    dt = xl.dtype
    pl = jnp.split(xl @ w_in, EVEN_SPLITS, axis=-1)
    pc = jnp.split(xc @ w_in, EVEN_SPLITS, axis=-1)
    lat = _mlstm_prepare(pl[0], pl[1], pl[3], conv_w, conv_b, gate_b)
    cin = _mlstm_prepare(pc[0], pc[1], pc[3], conv_w, conv_b, gate_b)
    hl, hc = _mlstm_bidir(lat, cin)
    ml_l = _mlstm_out(hl, pl[2], ml_g, dt)
    lam = _diff_lambda(da_lam, lam_init)
    ql, kl, vl = _da_heads(pl[4], pl[5], pl[6])
    qc, kc, vc = _da_heads(pc[4], pc[5], pc[6])
    ql = _apply_rope(ql, cos, sin)
    kl = _apply_rope(kl, cos, sin)
    kk = jnp.concatenate([kc, kl], axis=1)
    vv = jnp.concatenate([vc, vl], axis=1)
    da_l = _blocked_queries(lambda qb: _diff_attend(qb, kk, vv, lam), ql)
    yl = jnp.concatenate([ml_l, _da_out(da_l, da_g, lam_init, dt)], axis=-1) @ w_out
    yc = None
    if need_ctx:
        ml_c = _mlstm_out(hc, pc[2], ml_g, dt)
        da_c = _da_out(_diff_attend(qc, kc, vc, lam), da_g, lam_init, dt)
        yc = jnp.concatenate([ml_c, da_c], axis=-1) @ w_out
    return yl, yc

def _sink_softmax(s, sink):
    sk = jnp.broadcast_to(sink[None, :, :, None, None], s.shape[:-1] + (1,))
    p = jax.nn.softmax(jnp.concatenate([s, sk], axis=-1), axis=-1)
    return p[..., :-1]

def _ctx_gqa_attend(q, kc, vc, sink):
    bsz, t = q.shape[:2]
    qg = q.reshape(bsz, t, WA_KV_HEADS, WA_GROUP, WA_DH)
    s = jnp.einsum('bqhgd,bkhd->bhgqk', qg, kc).astype(jnp.float32) * (WA_DH ** -0.5)
    p = _sink_softmax(s, sink)
    o = jnp.einsum('bhgqk,bkhd->bqhgd', p.astype(vc.dtype), vc)
    return o.reshape(bsz, t, WA_W)

def _window_attend(q, k, v, kc, vc, sink):
    bsz, s = q.shape[:2]
    nb = s // W_BLOCK
    tc = kc.shape[1]
    qb = q.reshape(bsz, nb, W_BLOCK, WA_KV_HEADS, WA_GROUP, WA_DH)
    pad = ((0, 0), (W_BLOCK, W_BLOCK), (0, 0), (0, 0))
    kp = jnp.pad(k, pad).reshape(bsz, nb + 2, W_BLOCK, WA_KV_HEADS, WA_DH)
    vp = jnp.pad(v, pad).reshape(bsz, nb + 2, W_BLOCK, WA_KV_HEADS, WA_DH)
    kw = jnp.concatenate([kp[:, :-2], kp[:, 1:-1], kp[:, 2:]], axis=2)
    vw = jnp.concatenate([vp[:, :-2], vp[:, 1:-1], vp[:, 2:]], axis=2)
    qpos = jnp.arange(nb)[:, None] * W_BLOCK + jnp.arange(W_BLOCK)[None, :]
    kpos = (jnp.arange(nb)[:, None] - 1) * W_BLOCK + jnp.arange(3 * W_BLOCK)[None, :]
    mask = ((jnp.abs(qpos[:, :, None] - kpos[:, None, :]) <= WINDOW)
            & (kpos[:, None, :] >= 0) & (kpos[:, None, :] < s))
    scale = WA_DH ** -0.5

    def blk(args):
        qi, ki, vi, mi = args
        s_loc = jnp.einsum('bqhgd,bkhd->bhgqk', qi, ki).astype(jnp.float32) * scale
        s_loc = jnp.where(mi, s_loc, -jnp.inf)
        s_ctx = jnp.einsum('bqhgd,bkhd->bhgqk', qi, kc).astype(jnp.float32) * scale
        p = _sink_softmax(jnp.concatenate([s_ctx, s_loc], axis=-1), sink).astype(vi.dtype)
        return (jnp.einsum('bhgqk,bkhd->bqhgd', p[..., :tc], vc)
                + jnp.einsum('bhgqk,bkhd->bqhgd', p[..., tc:], vi))

    out = lax.map(blk, (jnp.moveaxis(qb, 1, 0), jnp.moveaxis(kw, 1, 0), jnp.moveaxis(vw, 1, 0), mask))
    return jnp.moveaxis(out, 0, 1).reshape(bsz, s, WA_W)

def _odd_mixer(xl, xc, w_in, sink, w_out, cos, sin, need_ctx):
    bsz, s, _ = xl.shape
    tc = xc.shape[1]
    ql, kl, vl = jnp.split(xl @ w_in, ODD_SPLITS, axis=-1)
    ql = _apply_rope(ql.reshape(bsz, s, WA_HEADS, WA_DH), cos, sin)
    kl = _apply_rope(kl.reshape(bsz, s, WA_KV_HEADS, WA_DH), cos, sin)
    vl = vl.reshape(bsz, s, WA_KV_HEADS, WA_DH)
    kc, vc = jnp.split(xc @ w_in[:, WA_W:], 2, axis=-1)
    kc = kc.reshape(bsz, tc, WA_KV_HEADS, WA_DH)
    vc = vc.reshape(bsz, tc, WA_KV_HEADS, WA_DH)
    sink = sink.astype(jnp.float32).reshape(WA_KV_HEADS, WA_GROUP)
    yl = _window_attend(ql, kl, vl, kc, vc, sink) @ w_out
    yc = None
    if need_ctx:
        qc = (xc @ w_in[:, :WA_W]).reshape(bsz, tc, WA_HEADS, WA_DH)
        yc = _ctx_gqa_attend(qc, kc, vc, sink) @ w_out
    return yl, yc

def _peer_ffn(x, w_q, keys, u, v):
    shp = x.shape
    xb = x.reshape(-1, PEER_TOK_BLOCK, shp[-1])

    def block(xt):
        n = xt.shape[0]
        q = (xt @ w_q).reshape(n, PEER_HEADS, 2, PEER_DHALF)
        s = jnp.einsum('nhpd,hpkd->nhpk', q, keys).astype(jnp.float32)
        sv, si = lax.top_k(s, PEER_TOPK)
        cand = sv[:, :, 0, :, None] + sv[:, :, 1, None, :]
        cidx = si[:, :, 0, :, None] * PEER_NKEYS + si[:, :, 1, None, :]
        cs, ci = lax.top_k(cand.reshape(n, PEER_HEADS, -1), PEER_TOPK)
        eidx = jnp.take_along_axis(cidx.reshape(n, PEER_HEADS, -1), ci, axis=-1)
        gate = jax.nn.softmax(cs, axis=-1)
        a = jnp.einsum('nd,nhkd->nhk', xt, u[eidx]).astype(jnp.float32)
        w = (gate * jax.nn.gelu(a, approximate=False)).astype(xt.dtype)
        return jnp.einsum('nhk,nhkd->nd', w, v[eidx])

    return lax.map(block, xb).reshape(shp)

def first_inputs(seed: int = 0) -> dict:
    key = jax.random.key(seed)
    ks = iter(jax.random.split(key, 32))

    def nrm(shape, scale):
        return jax.random.normal(next(ks), shape, jnp.float32) * scale

    d = D_MODEL
    zeros_h = jnp.zeros((ML_HEADS,), jnp.float32)
    f_bias = jnp.linspace(3.0, 6.0, ML_HEADS, dtype=jnp.float32)
    gate_base = jnp.concatenate([zeros_h, f_bias, zeros_h, f_bias])
    return {
        'x': nrm((BATCH, SEQ, d), 1.0),
        'c': nrm((BATCH, d), 1.0),
        'ctx': nrm((BATCH, CTX_LEN, d), 1.0),
        'c_ctx': nrm((d,), 1.0),
        'mod_w': nrm((DEPTH, d, N_MOD * d), 0.5 * d ** -0.5),
        'mod_b': nrm((DEPTH, N_MOD * d), 0.02),
        'norm1_g': 1.0 + nrm((DEPTH, d), 0.02),
        'norm2_g': 1.0 + nrm((DEPTH, d), 0.02),
        'ev_w_in': nrm((N_EVEN, d, EVEN_IN), d ** -0.5),
        'ev_ml_conv_w': nrm((N_EVEN, ML_CONV, 2 * ML_HEADS * ML_DQK), ML_CONV ** -0.5),
        'ev_ml_conv_b': nrm((N_EVEN, 2 * ML_HEADS * ML_DQK), 0.02),
        'ev_ml_gate_b': gate_base[None, :] + nrm((N_EVEN, 4 * ML_HEADS), 0.1),
        'ev_ml_norm_g': 1.0 + nrm((N_EVEN, ML_W), 0.02),
        'ev_da_lam': nrm((N_EVEN, 4, DA_DQK), 0.1),
        'ev_da_norm_g': 1.0 + nrm((N_EVEN, DA_W), 0.02),
        'ev_w_out': nrm((N_EVEN, MIX_W, d), MIX_W ** -0.5),
        'od_w_in': nrm((N_ODD, d, ODD_IN), d ** -0.5),
        'od_sink': nrm((N_ODD, WA_HEADS), 1.0),
        'od_w_out': nrm((N_ODD, WA_W, d), WA_W ** -0.5),
        'pr_w_q': nrm((DEPTH, d, PEER_HEADS * PEER_DQ), d ** -0.5),
        'pr_keys': nrm((DEPTH, PEER_HEADS, 2, PEER_NKEYS, PEER_DHALF), PEER_DHALF ** -0.5),
        'pr_u': nrm((DEPTH, PEER_EXPERTS, d), d ** -0.5),
        'pr_v': nrm((DEPTH, PEER_EXPERTS, d), PEER_HEADS ** -0.5),
        'final_g': 1.0 + nrm((d,), 0.02),
    }

def first_block(x, c, ctx, c_ctx, mod_w, mod_b, norm1_g, norm2_g, ev_w_in, ev_ml_conv_w,
              ev_ml_conv_b, ev_ml_gate_b, ev_ml_norm_g, ev_da_lam, ev_da_norm_g, ev_w_out,
              od_w_in, od_sink, od_w_out, pr_w_q, pr_keys, pr_u, pr_v, final_g):
    bsz, s, d = x.shape
    cos_da, sin_da = _axial_rope_tables(s, DA_DQK)
    cos_wa, sin_wa = _axial_rope_tables(s, WA_DH)
    sc = jax.nn.silu(c)
    scc = jax.nn.silu(c_ctx)
    hl, hc = x, ctx
    for i in range(DEPTH):
        need_ctx = i < DEPTH - 1
        j = i // 2
        ml = (sc @ mod_w[i] + mod_b[i]).reshape(bsz, 1, N_MOD, d)
        mc = (scc @ mod_w[i] + mod_b[i]).reshape(N_MOD, d)
        xl = _rmsnorm(hl, norm1_g[i]) * (1.0 + ml[:, :, 1]) + ml[:, :, 0]
        xc = _rmsnorm(hc, norm1_g[i]) * (1.0 + mc[1]) + mc[0]
        if i % 2 == 0:
            lam_init = 0.8 - 0.6 * math.exp(-0.3 * i)
            yl, yc = _even_mixer(xl, xc, ev_w_in[j], ev_ml_conv_w[j], ev_ml_conv_b[j],
                                 ev_ml_gate_b[j], ev_ml_norm_g[j], ev_da_lam[j], ev_da_norm_g[j],
                                 ev_w_out[j], lam_init, cos_da, sin_da, need_ctx)
        else:
            yl, yc = _odd_mixer(xl, xc, od_w_in[j], od_sink[j], od_w_out[j],
                                cos_wa, sin_wa, need_ctx)
        hl = hl + ml[:, :, 2] * yl
        xl = _rmsnorm(hl, norm2_g[i]) * (1.0 + ml[:, :, 4]) + ml[:, :, 3]
        hl = hl + ml[:, :, 5] * _peer_ffn(xl, pr_w_q[i], pr_keys[i], pr_u[i], pr_v[i])
        if need_ctx:
            hc = hc + mc[2] * yc
            xc = _rmsnorm(hc, norm2_g[i]) * (1.0 + mc[4]) + mc[3]
            hc = hc + mc[5] * _peer_ffn(xc, pr_w_q[i], pr_keys[i], pr_u[i], pr_v[i])
    return _rmsnorm(hl, final_g)


N_MIXERS = 2
N_MLA_LAYERS = (DEPTH + N_MIXERS - 1) // N_MIXERS
N_POOL_LAYERS = DEPTH // N_MIXERS
MLA_HEADS = 8
QK_NOPE_DIM = 128
QK_ROPE_DIM = 64
V_HEAD_DIM = 128
Q_LORA_RANK = 384
KV_LORA_RANK = 256
MLA_IN_DIM = Q_LORA_RANK + KV_LORA_RANK + QK_ROPE_DIM
POOL_WINDOWS = (2, 4, 8, 16)
N_POOL_GROUPS = 4
POOL_GROUP_DIM = D_MODEL // N_POOL_GROUPS
PEER_N_KEYS = 128
PEER_N_EXPERTS = PEER_N_KEYS * PEER_N_KEYS
PEER_QUERY_DIM = 256
PEER_HALF = PEER_QUERY_DIM // 2
PEER_BLOCK = 128
LN_EPS = 1e-5
RMS_EPS = 1e-6
DEEPNORM_ALPHA = (2.0 * DEPTH) ** 0.25
DEEPNORM_BETA = (8.0 * DEPTH) ** -0.25


def _layernorm(x, g, b):
    xf = x.astype(jnp.float32)
    mu = jnp.mean(xf, axis=-1, keepdims=True)
    var = jnp.mean(jnp.square(xf - mu), axis=-1, keepdims=True)
    return ((xf - mu) * lax.rsqrt(var + LN_EPS) * g + b).astype(x.dtype)

def _rmsnorm_2(x, g):
    xf = x.astype(jnp.float32)
    return (xf * lax.rsqrt(jnp.mean(jnp.square(xf), axis=-1, keepdims=True) + RMS_EPS) * g).astype(x.dtype)

def _axial_rope_tables_2(n_tokens):
    rows_n = n_tokens // GRID_W
    row = jnp.repeat(jnp.arange(rows_n), GRID_W).astype(jnp.float32)
    col = jnp.tile(jnp.arange(GRID_W), rows_n).astype(jnp.float32)
    n_freq = QK_ROPE_DIM // 4
    freqs = ROPE_THETA ** (-jnp.arange(n_freq, dtype=jnp.float32) / n_freq)
    ang = jnp.concatenate([row[:, None] * freqs, col[:, None] * freqs], axis=-1)
    return jnp.cos(ang), jnp.sin(ang)

def _apply_rope_2(x, cos, sin):
    half = x.shape[-1] // 2
    xf = x.astype(jnp.float32)
    x1, x2 = xf[..., :half], xf[..., half:]
    return jnp.concatenate([x1 * cos - x2 * sin, x1 * sin + x2 * cos], axis=-1).astype(x.dtype)

def _block_attention(q, k, v):
    b, s, h, dk = q.shape
    scale = dk ** -0.5
    qb = q.reshape(b, s // Q_BLOCK, Q_BLOCK, h, dk).transpose(1, 0, 2, 3, 4)

    def one(qblk):
        sc = jnp.einsum('bqhd,bkhd->bhqk', qblk, k, preferred_element_type=jnp.float32) * scale
        p = jax.nn.softmax(sc, axis=-1).astype(v.dtype)
        return jnp.einsum('bhqk,bkhd->bqhd', p, v)

    o = lax.map(one, qb)
    return o.transpose(1, 0, 2, 3, 4).reshape(b, s, h * v.shape[-1])

def _mla_qkv(h, rope, w_in, q_norm_g, kv_norm_g, w_uq, w_ukv, with_queries):
    b, l, _ = h.shape
    z = h @ w_in
    c_q = z[..., :Q_LORA_RANK]
    c_kv = z[..., Q_LORA_RANK:Q_LORA_RANK + KV_LORA_RANK]
    k_rope = z[..., Q_LORA_RANK + KV_LORA_RANK:]
    kv = (_rmsnorm_2(c_kv, kv_norm_g) @ w_ukv).reshape(b, l, MLA_HEADS, QK_NOPE_DIM + V_HEAD_DIM)
    k_nope, v = kv[..., :QK_NOPE_DIM], kv[..., QK_NOPE_DIM:]
    if rope is not None:
        cos, sin = rope
        k_rope = _apply_rope_2(k_rope, cos, sin)
    k = jnp.concatenate([k_nope, jnp.broadcast_to(k_rope[:, :, None, :], (b, l, MLA_HEADS, QK_ROPE_DIM))], axis=-1)
    if not with_queries:
        return None, k, v
    q = (_rmsnorm_2(c_q, q_norm_g) @ w_uq).reshape(b, l, MLA_HEADS, QK_NOPE_DIM + QK_ROPE_DIM)
    q_nope, q_rope = q[..., :QK_NOPE_DIM], q[..., QK_NOPE_DIM:]
    if rope is not None:
        q_rope = _apply_rope_2(q_rope, cos[:, None, :], sin[:, None, :])
    return jnp.concatenate([q_nope, q_rope], axis=-1), k, v

def _centred_mean_minus_self(x, window):
    b, l, ch = x.shape
    xf = x.astype(jnp.float32)
    cs = jnp.concatenate([jnp.zeros((b, 1, ch), jnp.float32), jnp.cumsum(xf, axis=1)], axis=1)
    t = jnp.arange(l)
    lo = jnp.clip(t - window // 2, 0, l)
    hi = jnp.clip(t + window // 2, 0, l)
    tot = jnp.take(cs, hi, axis=1) - jnp.take(cs, lo, axis=1)
    cnt = (hi - lo).astype(jnp.float32)[None, :, None]
    return (tot / cnt - xf).astype(x.dtype)

def _pool_mixer(h, w_in, w_grp, scale, w_out):
    b, l, _ = h.shape
    zg = (h @ w_in).reshape(b, l, N_POOL_GROUPS, POOL_GROUP_DIM)
    pooled = jnp.stack([_centred_mean_minus_self(zg[:, :, g], POOL_WINDOWS[g]) for g in range(N_POOL_GROUPS)], axis=2)
    y = jnp.einsum('blgc,gcd->blgd', pooled, w_grp).reshape(b, l, D_MODEL) * scale
    return y @ w_out

def _peer(h, w_q, k1, k2, u_tab, v_tab):
    b, l, d = h.shape
    q = (h @ w_q).reshape(b, l, PEER_HEADS, 2, PEER_HALF)
    s1 = jnp.einsum('blhc,hnc->blhn', q[..., 0, :], k1, preferred_element_type=jnp.float32)
    s2 = jnp.einsum('blhc,hnc->blhn', q[..., 1, :], k2, preferred_element_type=jnp.float32)
    v1, i1 = lax.top_k(s1, PEER_TOPK)
    v2, i2 = lax.top_k(s2, PEER_TOPK)
    cand_s = (v1[..., :, None] + v2[..., None, :]).reshape(b, l, PEER_HEADS, PEER_TOPK * PEER_TOPK)
    cand_i = (i1[..., :, None] * PEER_N_KEYS + i2[..., None, :]).reshape(b, l, PEER_HEADS, PEER_TOPK * PEER_TOPK)
    top_s, pos = lax.top_k(cand_s, PEER_TOPK)
    idx = jnp.take_along_axis(cand_i, pos, axis=-1)
    g = jax.nn.softmax(top_s, axis=-1).astype(h.dtype)
    n_blk = (b * l) // PEER_BLOCK
    n_sel = PEER_HEADS * PEER_TOPK
    hb = h.reshape(n_blk, PEER_BLOCK, d)
    ib = idx.reshape(n_blk, PEER_BLOCK, n_sel)
    gb = g.reshape(n_blk, PEER_BLOCK, n_sel)

    def one(args):
        hx, ix, gx = args
        u = jnp.take(u_tab, ix, axis=0)
        a = jax.nn.gelu(jnp.einsum('ted,td->te', u, hx), approximate=False)
        vv = jnp.take(v_tab, ix, axis=0)
        return jnp.einsum('te,ted->td', gx * a, vv)

    return lax.map(one, (hb, ib, gb)).reshape(b, l, d)

def _post_norm(x, y, gate, g, b):
    return _layernorm(DEEPNORM_ALPHA * x + gate * y, g, b)

def second_inputs(seed: int = 0) -> dict:
    key = jax.random.key(seed)
    ks = jax.random.split(key, 24)
    nrm = lambda k, shp, s: jax.random.normal(k, shp, jnp.float32) * s
    D = D_MODEL
    return {
        "x": nrm(ks[0], (BATCH, SEQ, D), 1.0),
        "c": nrm(ks[1], (BATCH, D), 1.0),
        "ctx": nrm(ks[2], (BATCH, CTX_LEN, D), 1.0),
        "c_ctx": nrm(ks[3], (D,), 1.0),
        "w_mod": nrm(ks[4], (DEPTH, D, N_MOD * D), 0.5 * D ** -0.5),
        "b_mod": nrm(ks[5], (DEPTH, N_MOD * D), 0.02),
        "ln_g": 1.0 + nrm(ks[6], (DEPTH, 2, D), 0.05),
        "ln_b": nrm(ks[7], (DEPTH, 2, D), 0.02),
        "mla_w_in": nrm(ks[8], (N_MLA_LAYERS, D, MLA_IN_DIM), D ** -0.5),
        "mla_q_norm": 1.0 + nrm(ks[9], (N_MLA_LAYERS, Q_LORA_RANK), 0.05),
        "mla_kv_norm": 1.0 + nrm(ks[10], (N_MLA_LAYERS, KV_LORA_RANK), 0.05),
        "mla_w_uq": nrm(ks[11], (N_MLA_LAYERS, Q_LORA_RANK, MLA_HEADS * (QK_NOPE_DIM + QK_ROPE_DIM)), Q_LORA_RANK ** -0.5),
        "mla_w_ukv": nrm(ks[12], (N_MLA_LAYERS, KV_LORA_RANK, MLA_HEADS * (QK_NOPE_DIM + V_HEAD_DIM)), KV_LORA_RANK ** -0.5),
        "mla_w_o": nrm(ks[13], (N_MLA_LAYERS, MLA_HEADS * V_HEAD_DIM, D), DEEPNORM_BETA * (MLA_HEADS * V_HEAD_DIM) ** -0.5),
        "pool_w_in": nrm(ks[14], (N_POOL_LAYERS, D, D), D ** -0.5),
        "pool_w_grp": nrm(ks[15], (N_POOL_LAYERS, N_POOL_GROUPS, POOL_GROUP_DIM, POOL_GROUP_DIM), POOL_GROUP_DIM ** -0.5),
        "pool_scale": 1.0 + nrm(ks[16], (N_POOL_LAYERS, D), 0.1),
        "pool_w_out": nrm(ks[17], (N_POOL_LAYERS, D, D), DEEPNORM_BETA * D ** -0.5),
        "peer_w_q": nrm(ks[18], (DEPTH, D, PEER_HEADS * PEER_QUERY_DIM), D ** -0.5),
        "peer_k1": nrm(ks[19], (DEPTH, PEER_HEADS, PEER_N_KEYS, PEER_HALF), PEER_HALF ** -0.5),
        "peer_k2": nrm(ks[20], (DEPTH, PEER_HEADS, PEER_N_KEYS, PEER_HALF), PEER_HALF ** -0.5),
        "peer_u": nrm(ks[21], (DEPTH, PEER_N_EXPERTS, D), D ** -0.5),
        "peer_v": nrm(ks[22], (DEPTH, PEER_N_EXPERTS, D), DEEPNORM_BETA),
    }

def second_block(x, c, ctx, c_ctx, w_mod, b_mod, ln_g, ln_b, mla_w_in, mla_q_norm, mla_kv_norm, mla_w_uq, mla_w_ukv, mla_w_o,
              pool_w_in, pool_w_grp, pool_scale, pool_w_out, peer_w_q, peer_k1, peer_k2, peer_u, peer_v):
    b, s, _ = x.shape
    rope = _axial_rope_tables_2(s)
    silu_c = jax.nn.silu(c)
    silu_ctx = jax.nn.silu(c_ctx)
    for i in range(DEPTH):
        mixer = i % N_MIXERS
        j = i // N_MIXERS
        ctx_needed = any(k % N_MIXERS == 0 for k in range(i + 1, DEPTH))
        ml = (silu_c @ w_mod[i] + b_mod[i])[:, None, :]
        mc = silu_ctx @ w_mod[i] + b_mod[i]
        sh1, sc1, g1, sh2, sc2, g2 = jnp.split(ml, N_MOD, axis=-1)
        csh1, csc1, cg1, csh2, csc2, cg2 = jnp.split(mc, N_MOD, axis=-1)
        hx = x * (1.0 + sc1) + sh1
        hc = ctx * (1.0 + csc1) + csh1
        if mixer == 0:
            w = (mla_w_in[j], mla_q_norm[j], mla_kv_norm[j], mla_w_uq[j], mla_w_ukv[j])
            q, k, v = _mla_qkv(hx, rope, *w, True)
            qc, kc, vc = _mla_qkv(hc, None, *w, ctx_needed)
            y = _block_attention(q, jnp.concatenate([k, kc], axis=1), jnp.concatenate([v, vc], axis=1)) @ mla_w_o[j]
            if ctx_needed:
                yc = _block_attention(qc, kc, vc) @ mla_w_o[j]
        else:
            w = (pool_w_in[j], pool_w_grp[j], pool_scale[j], pool_w_out[j])
            y = _pool_mixer(hx, *w)
            if ctx_needed:
                yc = _pool_mixer(hc, *w)
        pw = (peer_w_q[i], peer_k1[i], peer_k2[i], peer_u[i], peer_v[i])
        x = _post_norm(x, y, g1, ln_g[i, 0], ln_b[i, 0])
        x = _post_norm(x, _peer(x * (1.0 + sc2) + sh2, *pw), g2, ln_g[i, 1], ln_b[i, 1])
        if ctx_needed:
            ctx = _post_norm(ctx, yc, cg1, ln_g[i, 0], ln_b[i, 0])
            ctx = _post_norm(ctx, _peer(ctx * (1.0 + csc2) + csh2, *pw), cg2, ln_g[i, 1], ln_b[i, 1])
    return x


def setup_inputs(seed=0):
    out = dict(first_inputs(seed))
    for name, value in second_inputs(seed + 1).items():
        if name != "x":
            out[name + "_2"] = value
    return out


def reference(
    x, c, ctx, c_ctx, mod_w, mod_b, norm1_g, norm2_g, ev_w_in, ev_ml_conv_w, ev_ml_conv_b,
    ev_ml_gate_b, ev_ml_norm_g, ev_da_lam, ev_da_norm_g, ev_w_out, od_w_in, od_sink, od_w_out,
    pr_w_q, pr_keys, pr_u, pr_v, final_g, c_2, ctx_2, c_ctx_2, w_mod_2, b_mod_2, ln_g_2, ln_b_2,
    mla_w_in_2, mla_q_norm_2, mla_kv_norm_2, mla_w_uq_2, mla_w_ukv_2, mla_w_o_2, pool_w_in_2,
    pool_w_grp_2, pool_scale_2, pool_w_out_2, peer_w_q_2, peer_k1_2, peer_k2_2, peer_u_2,
    peer_v_2,
):
    x = first_block(
        x, c, ctx, c_ctx, mod_w, mod_b, norm1_g, norm2_g, ev_w_in, ev_ml_conv_w, ev_ml_conv_b,
        ev_ml_gate_b, ev_ml_norm_g, ev_da_lam, ev_da_norm_g, ev_w_out, od_w_in, od_sink,
        od_w_out, pr_w_q, pr_keys, pr_u, pr_v, final_g,
    )
    return second_block(
        x, c_2, ctx_2, c_ctx_2, w_mod_2, b_mod_2, ln_g_2, ln_b_2, mla_w_in_2, mla_q_norm_2,
        mla_kv_norm_2, mla_w_uq_2, mla_w_ukv_2, mla_w_o_2, pool_w_in_2, pool_w_grp_2,
        pool_scale_2, pool_w_out_2, peer_w_q_2, peer_k1_2, peer_k2_2, peer_u_2, peer_v_2,
    )


_drawn_inputs = setup_inputs


def setup_inputs(seed=0):
    import zlib

    import numpy as np

    out = dict(_drawn_inputs(seed))
    spreads = {}
    factors = {'norm1_g': 5.097,
     'norm2_g': 3.576,
     'ev_ml_conv_b': 7.79,
     'ev_ml_norm_g': 6.911,
     'ev_da_lam': 7.874,
     'ev_da_norm_g': 6.128,
     'od_sink': 8.0,
     'ctx_2': 6.359,
     'c_ctx_2': 3.102,
     'b_mod_2': 3.296,
     'mla_q_norm_2': 8.0,
     'mla_kv_norm_2': 8.0,
     'mla_w_uq_2': 4.293,
     'pool_scale_2': 4.741}
    for name, (base, spread) in spreads.items():
        noise = np.random.default_rng([zlib.crc32(name.encode()), seed]).standard_normal(out[name].shape)
        drawn = base * np.exp(spread * noise) if base else spread * noise
        out[name] = jnp.asarray(drawn.astype(out[name].dtype))
    for name, factor in factors.items():
        out[name] = (out[name] * factor).astype(out[name].dtype)
    return out
```

```python
from contextlib import ExitStack

import numpy as np

import concourse.bass as bass
from concourse import mybir

F32 = mybir.dt.float32
U32 = mybir.dt.uint32
ALU = mybir.AluOpType
ACT = mybir.ActivationFunctionType
AX_X = mybir.AxisListType.X
ds = bass.ds

P = 128
D = 1024
KC = D // P
SEQ = 256
TILES = 4
CTX, LAT = (0, 1), (2, 3)
TOK = TILES * P
NMOD = 6
MODC = NMOD * KC
LAYERS = 4
EPS = 1e-6
LN_EPS = 1e-5
ALPHA = 4.0 ** 0.25
LAM_INIT = 0.2
SCALE64 = 64.0 ** -0.5
SCALE_MLA = 192.0 ** -0.5
NEG = -3.0e38
MASK = -1.0e30

PH, TOPK, NK = 8, 16, 128
EXPERTS = NK * NK
SLOTS = 4
GROUP = 2
GPH = TOPK // GROUP
GPT = PH * GPH
PEER_TILES = [(0, 1, 2, 3), LAT, LAT, LAT]
HEADS_BEFORE = [sum(len(x) for x in PEER_TILES[:l]) * PH for l in range(LAYERS)]

ARENA = 29440
XNAT = 0
SCORES = XNAT + TILES * D
RING = SCORES + (TILES * PH + 1) * 2 * NK
XT2, QT = RING, RING + KC * TOK
XT = 0
XN = 19488
MIX_T = 6160
RAW, QKT, VML, OSIG = 4096, 6160, 8208, 10272
DQT, DKT, DV, MIX = 13344, 15392, 17440, 19488
ATS, EW0, DMASK, MROW = 23584, 25632, 27680, 28192
EW1 = RAW
GW = ATS
L1_QN, L1_KN, L1_QT, L1_KT, L1_V, L1_P, L1_PT = 4096, 6144, 7168, 9216, 10240, 11264, 12288
L2_Z, L2_CQT, L2_CKVT, L2_KRT, L2_QNT, L2_QR, L2_QRT, L2_KNT, L2_V = (
    4096, 6912, 7680, 8704, 9216, 11264, 12288, 13312, 17408)
L2_MIX, L2_P, L2_PT = 21504, 23552, 24576
L3_Z, L3_POOLT, L3_YT = 4096, 6144, 8192
RESID = 10496
SOURCES = (((0,), (0, 1), (0, 1, 2), (0, 1, 2, 3)), ((0, 1), (1,), (0, 1, 2, 3), (0, 1, 3)))
OFF_DIAGONAL = (([(1, 4)], [(2, 4)], [(3, 4)], []), ([(2, 4)], [(0, 1), (2, 4)], [], [(2, 3)]))

WSLOTS, WCOLS = 2, 4096
RSLOTS = 5

CT = dict(ident=(0, 128), tri=(128, 256), win=(384, 256), cos=(640, 64), sin=(704, 64), iota=(768, 16), sel=(784, 512), zero=(1296, 512))
CT_COLS = 1808
PT_ = dict(conv_w=(0, 12), conv_b=(12, 4), gate_b=(16, 4), lam=(20, 256), sink=(276, 16), pool_scale=(292, 8),
           cond=(300, 32), mod_b=(332, LAYERS * MODC))
PT_COLS = 332 + LAYERS * MODC


def block_list():
    out = [((l, "mod", n), KC * 512) for l in range(LAYERS) for n in range(MODC // 4)]
    for l in range(LAYERS):
        if l == 0:
            out += [((l, n), KC * 512) for n in ("qk",)] + [((l, "gates"), KC * 16)]
            out += [((l, n), KC * 512) for n in ("v", "o", "dq", "dk", "dv", "out0", "out1")]
        if l == 1:
            out += [((l, n), KC * 512) for n in ("q0", "q1", "kv", "out0", "out1")]
        if l == 2:
            out += [((l, "zq"), KC * 384), ((l, "zkv"), KC * 320), ((l, "uqn"), 3 * 1024), ((l, "uqr"), 3 * 512),
                    ((l, "ukn"), 2 * 1024), ((l, "uv"), 2 * 1024), ((l, "out0"), KC * 512), ((l, "out1"), KC * 512)]
        if l == 3:
            out += [((l, "in0"), KC * 512), ((l, "in1"), KC * 512), ((l, "band"), 2048), ((l, "grp"), 2048),
                    ((l, "out0"), KC * 512), ((l, "out1"), KC * 512)]
        out += [((l, "wq", n), KC * 512) for n in range(4)] + [((l, "keys"), 2048)]
    return out


BLOCKS = block_list()
BLOCK_AT = {name: n for n, (name, _) in enumerate(BLOCKS)}


def row_list():
    out = []

    def mod(l, s, m, name):
        out.append(((l, name, s), ("mod", l, s, m)))

    def par(l, name, s, r):
        out.append(((l, name, s), ("par", r)))

    for l in (0, 1):
        for s in (1, 0):
            par(l, "g1", s, GAIN[("norm1", l)])
            mod(l, s, 1, "sc1")
            mod(l, s, 0, "sh1")
        if l == 0:
            par(l, "headg", 0, GAIN["headg"])
        for s in ((1, 0) if l == 0 else (0,)):
            mod(l, s, 2, "gate1")
        for s in ((1, 0) if l == 0 else (0,)):
            par(l, "g2", s, GAIN[("norm2", l)])
            mod(l, s, 4, "sc2")
            mod(l, s, 3, "sh2")
        for s in ((1, 0) if l == 0 else (0,)):
            mod(l, s, 5, "gate2")
        if l == 1:
            par(l, "final", 0, GAIN["final"])
    for l in (2, 3):
        for s in ((1, 0) if l == 2 else (0,)):
            mod(l, s, 1, "sc1")
            mod(l, s, 0, "sh1")
        if l == 2:
            par(l, "mlag", 0, GAIN["mlag"])
        mod(l, 0, 2, "gate1")
        par(l, "lng", 0, GAIN[("lng", l, 0)])
        par(l, "lnb", 0, GAIN[("lnb", l, 0)])
        mod(l, 0, 4, "sc2")
        mod(l, 0, 3, "sh2")
        mod(l, 0, 5, "gate2")
        par(l, "lng", 1, GAIN[("lng", l, 1)])
        par(l, "lnb", 1, GAIN[("lnb", l, 1)])
    return out


GAIN = {("norm1", 0): 0, ("norm1", 1): 1, ("norm2", 0): 2, ("norm2", 1): 3, "headg": 4, "final": 5, "mlag": 6}
for _l in (2, 3):
    for _s in (0, 1):
        GAIN[("lng", _l, _s)] = 7 + 4 * (_l - 2) + _s
        GAIN[("lnb", _l, _s)] = 9 + 4 * (_l - 2) + _s
ROWS = row_list()
ROW_AT = {name: n for n, (name, _) in enumerate(ROWS)}


def rev(c0):
    return slice(c0 + 255, c0 - 1 if c0 else None, -1)


def head_of(i):
    c, side = (i % 16) // 2, i % 2
    return (2 * (c // 4) + side) * 4 + c % 4


class Steps:

    def __init__(self, sems, known):
        self.sems, self.known, self.count, self.at = sems, known, dict.fromkeys(sems, 0), {}

    def done(self, engine, *events):
        self.count[engine] += 1
        for e in events:
            assert e not in self.at, e
            self.at[e] = (engine, self.count[engine])
        return 1

    def after(self, *event):
        engine, n = self.known.get(event, ("pe", 1))
        assert not self.known or event in self.known, event
        return self.sems[engine], n


def program(nc, A, known):
    with ExitStack() as ctx:
        def sb(name, shape, dt=F32):
            return ctx.enter_context(nc.sbuf_tensor(name, shape, dt))

        def sem(name):
            return ctx.enter_context(nc.semaphore(name))

        arena = sb("arena", [P, ARENA])
        H = sb("hidden_sb", [P, TILES, D])
        wring = sb("weight_ring", [P, WSLOTS, WCOLS])
        rring = sb("row_ring", [P, RSLOTS, D])
        consts = sb("consts_sb", [P, CT_COLS])
        params = sb("params_sb", [P, PT_COLS])
        silc = sb("silu_cond", [P, KC, 4])
        modcol = sb("mod_columns", [P, 2 * MODC])
        modrow = sb("mod_rows", [2 * MODC, P])
        gcols = sb("gate_columns", [P, 64])
        small = sb("small", [P, 64])
        lamc = sb("lambda", [P, 4])
        newton = sb("newton", [P, 64])
        head_scores = sb("head_scores", [P, 256])
        left = sb("left", [P, 256])
        topv = sb("topv", [P, 2, 16])
        topi = sb("topi", [P, 2, 16], U32)
        topf = sb("topf", [P, 2, 16])
        cv = sb("cv", [P, 16])
        ci = sb("ci", [P, 16], U32)
        ab = sb("ab", [P, 2, 16], U32)
        abf = sb("abf", [P, 2, 16])
        eq = sb("eq", [P, 2, 16, 16])
        selv = sb("selv", [P, 2, 16])
        ef = sb("ef", [P, 16])
        idx = sb("idx", [P, 2, 16], U32)
        neg = sb("neg", [P, 1])
        ex = sb("ex", [P, 16])
        es = sb("es", [P, 1])
        gate = sb("gate", [P, 2, 16])
        dot = sb("dot", [P, SLOTS, GROUP])
        gel = sb("gel", [P, SLOTS, GROUP])
        wgt = sb("wgt", [P, SLOTS, GROUP])
        diag = sb("diag", [P, SLOTS, GROUP, P])
        bank = ctx.enter_context(nc.psum_tensor("banks", [P, 8, 512], F32))
        mods = nc.dram_tensor("mods", [LAYERS, 2 * NMOD, D], F32, kind="Internal").ap()

        sems = {e: sem(f"{e}_steps") for e in ("pe", "dve", "act")}
        consts_landed, params_landed, hidden_landed = sem("consts_landed"), sem("params_landed"), sem("hidden_landed")
        ctx2_landed, stored = sem("ctx2_landed"), sem("stored")
        w_landed = [sem(f"weights_landed{i}") for i in range(WSLOTS)]
        r_landed = [sem(f"row_landed{i}") for i in range(RSLOTS)]
        mods_stored = [sem(f"mods_stored{i}") for i in range(LAYERS)]
        ring_landed = [sem(f"experts_landed{i}") for i in range(SLOTS)]
        slots_free, dots_done, diag_done = sem("slots_free"), sem("dots_done"), sem("diag_done")
        topk_done, head_copied, exp_done = sem("topk_done"), sem("head_copied"), sem("exp_done")

        st = Steps(sems, known)
        after, done = st.after, st.done

        def v(off, n):
            return arena[:, off:off + n]

        def v3(off, a, b):
            return arena[:, off:off + a * b].rearrange("p (a b) -> p a b", a=a)

        def v4(off, a, b, c):
            return arena[:, off:off + a * b * c].rearrange("p (a b c) -> p a b c", a=a, b=b)

        def const(name):
            o, n = CT[name]
            return consts[:, o:o + n]

        def par(name):
            o, n = PT_[name]
            return params[:, o:o + n]

        ident = const("ident")
        ring = arena[:, RING:RING + SLOTS * GROUP * 2 * D].rearrange("p (s x c) -> p s x c", s=SLOTS, x=GROUP)
        scores = v3(SCORES, TILES * PH + 1, 2 * NK)
        xT = v3(XT, KC, TOK)
        xnat = v3(XNAT, TILES, D)
        xn = v3(XN, TILES, D)
        mixT = v3(MIX_T, KC, TOK)
        xT2 = v3(XT2, KC, TOK)
        qT = v3(QT, 2 * PH, TOK)

        def bank3(b, a, n):
            return bank[:, b, 0:a * n].rearrange("p (a n) -> p a n", a=a)

        bank_of = {}

        def block_ap(n, k):
            cols = BLOCKS[n][1]
            return wring[:, n % WSLOTS, 0:cols].rearrange("p (k c) -> p k c", k=k)

        LT = {0: (0, 1, 2, 3), 1: (0, 1, 2, 3), 2: (0, 1, 2, 3), 3: LAT}

        block = ctx.enter_context(nc.Block())

        @block.sync
        def _(sp):
            sp.dma_start(params[:, :], A["params"]).then_inc(params_landed, 16)
            sp.dma_start(consts[:, :], A["consts"]).then_inc(consts_landed, 16)
            for n, (name, cols) in enumerate(BLOCKS):
                if n == 2:
                    sp.dma_start(H[:, :, :], A["hidden"]).then_inc(hidden_landed, 16)
                if n >= WSLOTS:
                    sp.wait_ge(*after("w", n - WSLOTS))
                sp.dma_start(wring[:, n % WSLOTS, 0:cols], A["weights"][n, :, 0:cols]).then_inc(w_landed[n % WSLOTS], 16)
            sp.wait_ge(*after("final_out"))
            sp.dma_start(A["out"], H[:, 2:4, :]).then_inc(stored, 16)
            sp.wait_ge(stored, 16)

        @block.gpsimd
        def _(pool):
            sent = [0]

            def rows_until(stop):
                while sent[0] < stop:
                    n = sent[0]
                    kind, *what = ROWS[n][1]
                    if n >= RSLOTS:
                        pool.wait_ge(*after("row", n - RSLOTS))
                    if kind == "mod":
                        l, s, m = what
                        pool.wait_ge(mods_stored[l], 16)
                        src = mods[l, s * NMOD + m:s * NMOD + m + 1, :]
                    else:
                        src = A["gains"][what[0]:what[0] + 1, :]
                    pool.dma_start(rring[:, n % RSLOTS, :], src.broadcast_to([P, D])).then_inc(r_landed[n % RSLOTS], 16)
                    sent[0] += 1

            for l in range(LAYERS):
                rows_until(1 + max(n for n, (name, _) in enumerate(ROWS) if name[0] == l))
                if l == 1:
                    pool.wait_ge(*after("xn", 1, 1))
                    pool.dma_start(H[:, 0:2, :], A["ctx2"]).then_inc(ctx2_landed, 16)
                pool.wait_ge(*after("scores_mm", l, len(PEER_TILES[l]) - 1, 3))
                for i in range(len(PEER_TILES[l])):
                    q0 = HEADS_BEFORE[l] + i * PH
                    with pool.Fori(0, PH // 2) as it:
                        for e in range(2):
                            pool.wait_ge(topk_done, it * 2 + (q0 + l + e + 1))
                            pool.nop(nofuse=True)
                            for j in range(GPH):
                                pool.wait_ge(slots_free, it * (2 * GPH) + (q0 * GPH + e * GPH + j + 1))
                                pool.nop(nofuse=True)
                                for x in range(GROUP):
                                    k = GROUP * j + x
                                    pool.indirect_dma_start(
                                        out=ring[:, j % SLOTS, x, :], out_offset=None, in_=A[f"uv{l}"],
                                        in_offset=bass.IndirectOffsetOnAxis(ap=idx[:, e, k:k + 1], axis=0),
                                    ).then_inc(ring_landed[j % SLOTS], 16)

        @block.tensor
        def _(pe):
            mm_ = nc.tensor.matmul
            free = {b: None for b in range(8)}
            turn = [0]
            seen = set()

            def new_bank(*key):
                b = turn[0] % 8
                turn[0] += 1
                if free[b] is not None:
                    pe.wait_ge(*after(*free[b]))
                free[b] = ("ev",) + key
                st.at[("bank",) + key] = b
                return b

            def weights(name, k):
                n = BLOCK_AT[name]
                if n not in seen:
                    seen.add(n)
                    pe.wait_ge(w_landed[n % WSLOTS], 16 * (n // WSLOTS + 1))
                return n, block_ap(n, k)

            def transposes(key, t, src, n=8, per=4):
                for half in range((n + per - 1) // per):
                    b = new_bank(*key, t, half)
                    m = min(per, n - half * per)
                    for k in range(m):
                        ins = nc.tensor.transpose(bank[:, b, k * P:(k + 1) * P],
                                                  src[:, (half * per + k) * P:(half * per + k + 1) * P], ident)
                    ins.then_inc(sems["pe"], done("pe", ("mm",) + key + (t, half)))

            def natural(l, name, tiles, src, k, width, cols=None, part=0):
                n, w = weights((l, name), k)
                c0, c1 = cols or (0, width)
                for t in tiles:
                    b = new_bank(l, name, t, part)
                    for kk in range(k):
                        ins = mm_(bank[:, b, 0:c1 - c0], src(kk, t), w[:, kk, c0:c1], start=kk == 0, stop=kk == k - 1)
                    ev = [("mm", l, name, t, part)]
                    if t == tiles[-1] and c1 == width:
                        ev.append(("w", n))
                    ins.then_inc(sems["pe"], done("pe", *ev))

            def feature(l, name, chunks, src, k, ncols, last=True):
                n, w = weights((l, *name) if isinstance(name, tuple) else (l, name), k)
                for c in range(chunks):
                    b = new_bank(l, name, c)
                    for kk in range(k):
                        ins = mm_(bank[:, b, 0:ncols], w[:, kk, c * P:(c + 1) * P], src(kk), start=kk == 0, stop=kk == k - 1)
                    ev = [("mm", l, name, c)]
                    if c == chunks - 1:
                        ev.append(("w", n))
                    ins.then_inc(sems["pe"], done("pe", *ev))

            pe.wait_ge(consts_landed, 16)
            pe.wait_ge(*after("silc"))
            for l in range(LAYERS):
                b = new_bank("mod", l)
                for nb in range(MODC // 4):
                    n, w = weights((l, "mod", nb), KC)
                    for c in range(4):
                        ch = nb * 4 + c
                        for kk in range(KC):
                            ins = mm_(bank[:, b, ch:ch + MODC + 1:MODC], w[:, kk, c * P:(c + 1) * P],
                                      silc[:, kk, 2 * (l // 2):2 * (l // 2) + 2], start=kk == 0, stop=kk == KC - 1)
                    ev = [("w", n)] + ([("mm", "mod", l)] if nb == MODC // 4 - 1 else [])
                    ins.then_inc(sems["pe"], done("pe", *ev))
                b = new_bank("modT", l)
                pe.wait_ge(*after("ev", "mod", l))
                nc.tensor.transpose(bank[0:2 * MODC, b, 0:P], modcol[:, :], ident)\
                    .then_inc(sems["pe"], done("pe", ("mm", "modT", l)))

            for l in range(LAYERS):
                tiles = LT[l]
                for t in tiles:
                    pe.wait_ge(*after("xn", l, t))
                    transposes((l, "xT"), t, xn[:, t, :])
                pe.wait_ge(*after("ev", l, "xT", tiles[-1], 0))
                pe.wait_ge(*after("ev", l, "xT", tiles[-1], 1))
                xs = lambda kk, t: xT[:, kk, t * P:(t + 1) * P]
                if l == 0:
                    feature(0, "qk", 4, lambda kk: xT[:, kk, :], KC, TOK)
                    n, w = weights((0, "gates"), KC)
                    for g in range(4):
                        b = new_bank(0, "gates", g)
                        for kk in range(KC):
                            ins = mm_(bank[0:4, b, :], w[:, kk, 4 * g:4 * g + 4], xT[:, kk, :], start=kk == 0, stop=kk == KC - 1)
                        ev = [("mm", 0, "gates", g)] + ([("w", n)] if g == 3 else [])
                        ins.then_inc(sems["pe"], done("pe", *ev))
                    for name in ("v", "o", "dq", "dk", "dv"):
                        natural(0, name, tiles, xs, KC, 512)
                    dqn = xn
                    for t in tiles:
                        pe.wait_ge(*after("roped", t))
                        transposes((0, "dqkT"), t, dqn[:, t, :])
                    pe.wait_ge(*after("gate_rows"))
                    b = new_bank(0, "gcols")
                    i = 0
                    for q in range(2):
                        for d in range(2):
                            rows_ = arena[0:4, (GW + 3072 if q else GW + 2048) + d * 512:][:, 0:512]
                            for t in range(4):
                                ins = nc.tensor.transpose(bank[:, b, i * 4:i * 4 + 4], rows_[:, t * P:(t + 1) * P], ident[0:4, 0:4])
                                i += 1
                    ins.then_inc(sems["pe"], done("pe", ("mm", 0, "gcols")))
                    qk = v3(QKT, 4, TOK)
                    vml = v4(VML, 4, 4, 129)
                    mrow = arena[0:4, MROW:MROW + 1024].rearrange("p (a b) -> p a b", a=2)
                    selr = consts[0:4, CT["sel"][0]:CT["sel"][0] + 512].rearrange("p (h c) -> p h c", h=4)
                    pe.wait_ge(*after("qkT", 3))
                    pe.wait_ge(*after("vml_ones"))
                    pe.wait_ge(*after("ev", 0, "v", 3, 0))
                    for h in range(4):
                        o = 64 * (h % 2)
                        for s in range(4):
                            b = new_bank(0, "A", h, s)
                            mm_(bank[:, b, :], qk[o:o + 64, 2 + h // 2, s * P:(s + 1) * P], qk[o:o + 64, h // 2, :], start=True, stop=True)\
                                .then_inc(sems["pe"], done("pe", ("mm", 0, "A", h, s)))
                        for d in range(2):
                            b = new_bank(0, "M", h, d)
                            mm_(bank[:, b, :], selr[:, h, :], mrow[:, d, :], start=True, stop=True)\
                                .then_inc(sems["pe"], done("pe", ("mm", 0, "M", h, d)))
                        for d in range(2):
                            wt = v3(EW1 if d else EW0, 4, TOK)
                            pe.wait_ge(*after("WT", h, d))
                            for tp in range(2):
                                b = new_bank(0, "N", h, d, tp)
                                for t in (2 * tp, 2 * tp + 1):
                                    src = SOURCES[d][t]
                                    for s in src:
                                        ins = mm_(bank[:, b, (t % 2) * 129:(t % 2) * 129 + 129], wt[:, s, t * P:(t + 1) * P],
                                                  vml[:, s, h, :], start=s == src[0], stop=s == src[-1])
                                ins.then_inc(sems["pe"], done("pe", ("mm", 0, "N", h, d, tp)))
                    dqT, dkT = v3(DQT, 4, TOK), v3(DKT, 4, TOK)
                    dv = v3(DV, 4, 512)
                    pe.wait_ge(*after("ev", 0, "dqkT", 3, 0))
                    pe.wait_ge(*after("ev", 0, "dqkT", 3, 1))
                    pe.wait_ge(*after("ev", 0, "dv", 3, 0))
                    for t in tiles:
                        nkt = 2 if t < 2 else 4
                        for h in range(4):
                            i = t * 4 + h
                            for m in range(2):
                                b = new_bank(0, "S", t, h, m)
                                mm_(bank[:, b, 0:nkt * P], dqT[64 * m:64 * m + 64, h, t * P:(t + 1) * P],
                                    dkT[64 * m:64 * m + 64, h, 0:nkt * P], start=True, stop=True)\
                                    .then_inc(sems["pe"], done("pe", ("mm", 0, "S", t, h, m)))
                            pe.wait_ge(*after("Pr", 0, i))
                            b = new_bank(0, "PT", i)
                            pr = v(ATS + (i % 2) * 1536, 512)
                            for kk in range(nkt):
                                ins = nc.tensor.transpose(bank[:, b, kk * P:(kk + 1) * P], pr[:, kk * P:(kk + 1) * P], ident)
                            ins.then_inc(sems["pe"], done("pe", ("mm", 0, "PT", i)))
                            b = new_bank(0, "O", i)
                            pe.wait_ge(*after("ev", 0, "PT", i))
                            prT = v3(ATS + (i % 2) * 1536 + 1024, 4, P)
                            for kk in range(nkt):
                                ins = mm_(bank[:, b, 0:P], prT[:, kk, :], dv[:, kk, h * P:(h + 1) * P], start=kk == 0, stop=kk == nkt - 1)
                            ins.then_inc(sems["pe"], done("pe", ("mm", 0, "O", i)))
                    mix_off = MIX
                if l == 1:
                    natural(1, "q0", LAT, xs, KC, 512)
                    natural(1, "q1", LAT, xs, KC, 512)
                    natural(1, "kv", tiles, xs, KC, 512)
                    qn, kn = v3(L1_QN, 2, 1024), v3(L1_KN, 4, 256)
                    for t in LAT:
                        pe.wait_ge(*after("q_roped", t))
                        transposes((1, "qT"), t, qn[:, t - 2, :])
                    for t in tiles:
                        pe.wait_ge(*after("k_roped", t))
                        transposes((1, "kT"), t, kn[:, t, :], n=2)
                    qT1, kT1, v1 = v3(L1_QT, 8, 256), v3(L1_KT, 2, TOK), v3(L1_V, 4, 256)
                    for i in range(32):
                        t, c, sd = i // 16, (i % 16) // 2, i % 2
                        kvh = 2 * (c // 4) + sd
                        b = new_bank(1, "S", i)
                        if i == 0:
                            pe.wait_ge(*after("ev", 1, "qT", 3, 1))
                            pe.wait_ge(*after("ev", 1, "qT", 3, 0))
                            pe.wait_ge(*after("ev", 1, "kT", 3, 0))
                        mm_(bank[:, b, :], qT1[64 * sd:64 * sd + 64, c, t * P:(t + 1) * P], kT1[64 * sd:64 * sd + 64, c // 4, :],
                            start=True, stop=True).then_inc(sems["pe"], done("pe", ("mm", 1, "S", i)))

                        def finish(i):
                            t, c, sd = i // 16, (i % 16) // 2, i % 2
                            kvh = 2 * (c // 4) + sd
                            pe.wait_ge(*after("Pr", 1, i))
                            b = new_bank(1, "PT", i)
                            pr = v(L1_P + (i % 2) * 512, 512)
                            for kk in range(4):
                                ins = nc.tensor.transpose(bank[:, b, kk * P:(kk + 1) * P], pr[:, kk * P:(kk + 1) * P], ident)
                            ins.then_inc(sems["pe"], done("pe", ("mm", 1, "PT", i)))
                            b = new_bank(1, "O", i)
                            pe.wait_ge(*after("ev", 1, "PT", i))
                            prT = v3(L1_PT + (i % 2) * 512, 4, P)
                            for kk in range(4):
                                ins = mm_(bank[:, b, 0:64], prT[:, kk, :], v1[:, kk, kvh * 64:kvh * 64 + 64], start=kk == 0, stop=kk == 3)
                            ins.then_inc(sems["pe"], done("pe", ("mm", 1, "O", i)))

                        if i >= 1:
                            finish(i - 1)
                    finish(31)
                    mix_off = MIX
                if l == 2:
                    natural(2, "zq", LAT, xs, KC, 384)
                    natural(2, "zkv", tiles, xs, KC, 320)
                    z = v3(L2_Z, 4, 704)
                    for t in tiles:
                        if t in LAT:
                            pe.wait_ge(*after("zq_n", t))
                            transposes((2, "cqT"), t, z[:, t, 0:384], n=3)
                        pe.wait_ge(*after("zkv_n", t))
                        transposes((2, "ckvT"), t, z[:, t, 384:640], n=2)
                        pe.wait_ge(*after("kr", t))
                        transposes((2, "krT"), t, v3(L2_QR, 4, P)[:, t, :], n=1)
                    cqT, ckvT = v3(L2_CQT, 3, 256), v3(L2_CKVT, 2, TOK)
                    for t in tiles:
                        if t in LAT:
                            pe.wait_ge(*after("ev", 2, "cqT", t, 0))
                        pe.wait_ge(*after("ev", 2, "ckvT", t, 0))
                        pe.wait_ge(*after("ev", 2, "krT", t, 0))
                    feature(2, "uqn", 8, lambda kk: cqT[:, kk, :], 3, 256)
                    natural(2, "uqr", LAT, lambda kk, t: cqT[:, kk, (t - 2) * P:(t - 1) * P], 3, 512)
                    feature(2, "ukn", 8, lambda kk: ckvT[:, kk, :], 2, TOK)
                    for part in range(2):
                        natural(2, "uv", tiles, lambda kk, t: ckvT[:, kk, t * P:(t + 1) * P], 2, 1024,
                                cols=(part * 512, part * 512 + 512), part=part)
                    qr = v3(L2_QR, 2, 512)
                    for t in LAT:
                        pe.wait_ge(*after("qr_roped", t))
                        transposes((2, "qrT"), t, qr[:, t - 2, :], n=4)
                    qnT, qrT, knT, krT, v2 = (v3(L2_QNT, 8, 256), v3(L2_QRT, 4, 256), v3(L2_KNT, 8, TOK),
                                              v(L2_KRT, TOK), v3(L2_V, 4, 1024))
                    for i in range(16):
                        t, h = i // 8, i % 8
                        b = new_bank(2, "S", i)
                        if i == 0:
                            pe.wait_ge(*after("ev", 2, "qrT", 3, 0))
                            for ev in (("uqn", 6), ("uqn", 7), ("ukn", 6), ("ukn", 7)):
                                pe.wait_ge(*after("ev", 2, *ev))
                            for t_ in tiles:
                                pe.wait_ge(*after("ev", 2, "uv", t_, 1))
                                pe.wait_ge(*after("ev", 2, "uv", t_, 0))
                        o = 64 * (h % 2)
                        mm_(bank[:, b, :], qnT[:, h, t * P:(t + 1) * P], knT[:, h, :], start=True, stop=False)
                        mm_(bank[:, b, :], qrT[o:o + 64, h // 2, t * P:(t + 1) * P], krT[o:o + 64, :], start=False, stop=True)\
                            .then_inc(sems["pe"], done("pe", ("mm", 2, "S", i)))

                        def finish(i):
                            h = i % 8
                            pe.wait_ge(*after("Pr", 2, i))
                            b = new_bank(2, "PT", i)
                            pr = v(L2_P + (i % 2) * 512, 512)
                            for kk in range(4):
                                ins = nc.tensor.transpose(bank[:, b, kk * P:(kk + 1) * P], pr[:, kk * P:(kk + 1) * P], ident)
                            ins.then_inc(sems["pe"], done("pe", ("mm", 2, "PT", i)))
                            b = new_bank(2, "O", i)
                            pe.wait_ge(*after("ev", 2, "PT", i))
                            prT = v3(L2_PT + (i % 2) * 512, 4, P)
                            for kk in range(4):
                                ins = mm_(bank[:, b, 0:P], prT[:, kk, :], v2[:, kk, h * P:(h + 1) * P], start=kk == 0, stop=kk == 3)
                            ins.then_inc(sems["pe"], done("pe", ("mm", 2, "O", i)))

                        if i >= 1:
                            finish(i - 1)
                    finish(15)
                    mix_off = L2_MIX
                out_tiles = PEER_TILES[l]
                if l < 3:
                    m0 = 0 if l == 0 else 2
                    mixv = v3(mix_off, len(out_tiles), D)
                    for t in out_tiles:
                        pe.wait_ge(*after("mix", l, t))
                        transposes((l, "mT"), t, mixv[:, t - m0, :])
                    for t in out_tiles:
                        pe.wait_ge(*after("ev", l, "mT", t, 0))
                        pe.wait_ge(*after("ev", l, "mT", t, 1))
                    ms = lambda kk, t: mixT[:, kk, t * P:(t + 1) * P]
                else:
                    for j in range(2):
                        natural(3, f"in{j}", LAT, xs, KC, 512)
                    z3, pT, yT = v3(L3_Z, 2, 1024), v3(L3_POOLT, 8, 256), v3(L3_YT, 8, 256)
                    n, w = weights((3, "band"), 2)
                    for t in LAT:
                        for j in range(2):
                            pe.wait_ge(*after("ev", 3, f"in{j}", t, 0))
                    for c in range(8):
                        b = new_bank(3, "pool", c)
                        for kk in range(2):
                            ins = mm_(bank[:, b, 0:256], z3[:, kk, c * P:(c + 1) * P], w[:, kk, (c // 2) * 256:(c // 2) * 256 + 256],
                                      start=kk == 0, stop=kk == 1)
                        ev = [("mm", 3, "pool", c)] + ([("w", n)] if c == 7 else [])
                        ins.then_inc(sems["pe"], done("pe", *ev))
                    n, w = weights((3, "grp"), 8)
                    pe.wait_ge(*after("ev", 3, "pool", 6))
                    pe.wait_ge(*after("ev", 3, "pool", 7))
                    for c in range(8):
                        b = new_bank(3, "yT", c)
                        g = c // 2
                        for kk in range(2):
                            ins = mm_(bank[:, b, 0:256], w[:, 2 * g + kk, (c % 2) * P:(c % 2) * P + P], pT[:, 2 * g + kk, :],
                                      start=kk == 0, stop=kk == 1)
                        ev = [("mm", 3, "yT", c)] + ([("w", n)] if c == 7 else [])
                        ins.then_inc(sems["pe"], done("pe", *ev))
                    pe.wait_ge(*after("ev", 3, "yT", 6))
                    pe.wait_ge(*after("ev", 3, "yT", 7))
                    ms = lambda kk, t: yT[:, kk, (t - 2) * P:(t - 1) * P]
                for j in range(2):
                    natural(l, f"out{j}", out_tiles, ms, KC, 512)
                for t in out_tiles:
                    pe.wait_ge(*after("xnat", l, t))
                    transposes((l, "xT2"), t, xnat[:, t - out_tiles[0], :])
                for t in out_tiles:
                    pe.wait_ge(*after("ev", l, "xT2", t, 0))
                    pe.wait_ge(*after("ev", l, "xT2", t, 1))
                ntok = len(out_tiles) * P
                for j in range(4):
                    n, w = weights((l, "wq", j), KC)
                    for c in range(4):
                        b = new_bank(l, "q", 4 * j + c)
                        for kk in range(KC):
                            ins = mm_(bank[:, b, 0:ntok], w[:, kk, c * P:(c + 1) * P], xT2[:, kk, 0:ntok], start=kk == 0, stop=kk == KC - 1)
                        ev = [("mm", l, "q", 4 * j + c)] + ([("w", n)] if c == 3 else [])
                        ins.then_inc(sems["pe"], done("pe", *ev))
                n, w = weights((l, "keys"), 16)
                for i in range(len(out_tiles)):
                    for j in range(4):
                        b = new_bank(l, "sc", i, j)
                        if i == 0:
                            for q in range(4):
                                pe.wait_ge(*after("ev", l, "q", 4 * j + q))
                        for q in range(4):
                            hp = 4 * j + q
                            ins = mm_(bank[:, b, q * P:(q + 1) * P], qT[:, hp, i * P:(i + 1) * P], w[:, hp, :], start=True, stop=True)
                        ev = [("mm", l, "sc", i, j), ("scores_mm", l, i, j)]
                        if j == 3 and i == len(out_tiles) - 1:
                            ev.append(("w", n))
                        ins.then_inc(sems["pe"], done("pe", *ev))
                for i in range(len(out_tiles)):
                    q0 = HEADS_BEFORE[l] + i * PH
                    yb = 2 * (i % 2)
                    for hf in range(2):
                        pe.wait_ge(*after(*free[yb + hf]))
                        free[yb + hf] = ("y_taken", l, i)
                        ins = mm_(bank[:, yb + hf, :], ident, const("zero"), start=True, stop=False, skip_group_check=True)
                    if l == 0 and i == 0:
                        ins.then_inc(slots_free, SLOTS)
                    with pe.Fori(0, PH // 2) as it:
                        for e in range(2):
                            for j in range(GPH):
                                pe.wait_ge(diag_done, it * (2 * GPH) + (q0 * GPH + e * GPH + j + 1))
                                for x in range(GROUP):
                                    for hf in range(2):
                                        ins = mm_(bank[:, yb + hf, :], diag[:, j % SLOTS, x, :],
                                                  ring[:, j % SLOTS, x, D + hf * 512:D + hf * 512 + 512],
                                                  start=False, stop=True, skip_group_check=True)
                                ins.then_inc(slots_free, 1)

        @block.scalar
        def _(act):
            a = nc.scalar
            AF = a.activation

            def b_(*key):
                act.wait_ge(*after("mm", *key))
                return known.get(("bank",) + key, 0)

            def ev(ins, *key):
                ins.then_inc(sems["act"], done("act", ("ev",) + key))

            def copy_T(key, t, dst, half, n=4):
                b = b_(*key, t, half)
                ev(a.copy(dst, bank3(b, n, P)), *key, t, half)

            act.wait_ge(params_landed, 16)
            AF(silc[:, :, :].rearrange("p k c -> p (k c)"), par("cond"), ACT.Silu).then_inc(sems["act"], done("act", ("silc",)))
            for l in range(LAYERS):
                b = b_("modT", l)
                if l:
                    act.wait_ge(mods_stored[l - 1], 16)
                ev(a.copy(modrow[:, :], bank[0:2 * MODC, b, 0:P]), "modT", l)
                act.wait_ge(*after("ev", "modT", l))
                act.dma_start(mods[l, :, :].rearrange("a (b c) -> (a b) c", c=P), modrow[:, :]).then_inc(mods_stored[l], 16)
            act.wait_ge(*after("lam_dots"))
            AF(lamc[:, 0:2], lamc[:, 0:2], ACT.Exp).then_inc(sems["act"], done("act", ("lam_exp",)))
            for l in range(LAYERS):
                tiles = LT[l]
                for t in tiles:
                    copy_T((l, "xT"), t, xT[:, 0:4, t * P:(t + 1) * P], 0)
                if l == 0:
                    raw = v4(RAW, 4, 2, 258)
                    qk = v3(QKT, 4, TOK)
                    for c in range(4):
                        act.wait_ge(*after("conv", c))
                        AF(qk[:, c, :], qk[:, c, :], ACT.Silu).then_inc(sems["act"], done("act", ("qkT", c)))
                    tmp = arena[0:4, GW + 2048:GW + 3072]
                    act.wait_ge(*after("absz"))
                    AF(tmp, tmp, ACT.Exp, scale=-1.0)
                    act.drain()
                    AF(tmp, tmp, ACT.Ln, bias=1.0).then_inc(sems["act"], done("act", ("softplus",)))
                    vml = v4(VML, 4, 4, 129)
                    for t in tiles:
                        b = b_(0, "v", t, 0)
                        ev(a.copy(vml[:, t, :, 0:128], bank3(b, 4, P)), 0, "v", t, 0)
                    for t in tiles:
                        b = b_(0, "o", t, 0)
                        ev(AF(v(OSIG + t * 512, 512), bank[:, b, :], ACT.Sigmoid), 0, "o", t, 0)
                    for t in tiles:
                        b = b_(0, "dv", t, 0)
                        ev(a.copy(v(DV + t * 512, 512), bank[:, b, :]), 0, "dv", t, 0)
                    for t in tiles:
                        copy_T((0, "dqkT"), t, v3(DQT, 4, TOK)[:, :, t * P:(t + 1) * P], 0)
                    act.wait_ge(*after("m_rows"))
                    AF(arena[0:4, GW + 3072:GW + 4096], arena[0:4, GW + 1024:GW + 2048], ACT.Exp, scale=-1.0)\
                        .then_inc(sems["act"], done("act", ("floor_rows",)))
                    ats = v3(ATS, 4, TOK)
                    for h in range(4):
                        for s in range(4):
                            b = b_(0, "A", h, s)
                            if s == 0:
                                if h:
                                    act.wait_ge(*after("WT", h - 1, 1))
                                else:
                                    act.wait_ge(*after("ev", 0, "gcols"))
                            ev(AF(ats[:, s, :], bank[:, b, :], ACT.Copy, scale=SCALE64), 0, "A", h, s)
                        for d in range(2):
                            wt = v3(EW1 if d else EW0, 4, TOK)
                            dm = v3(DMASK, 4, P)
                            b = b_(0, "M", h, d)
                            act.wait_ge(*after("dmask", h, d))
                            if h:
                                act.wait_ge(*after("mm", 0, "N", h - 1, d, 1))
                            for s in range(4):
                                bias = gcols[:, (d * 4 + s) * 4 + h:(d * 4 + s) * 4 + h + 1]
                                ins = AF(wt[:, s, s * P:(s + 1) * P], dm[:, s, :], ACT.Exp, bias=bias)
                                for t0, t1 in OFF_DIAGONAL[d][s]:
                                    ins = AF(wt[:, s, t0 * P:t1 * P], bank[:, b, t0 * P:t1 * P], ACT.Exp, bias=bias)
                            ins.then_inc(sems["act"], done("act", ("ev", 0, "M", h, d), ("E", h, d)))
                    for t in tiles:
                        nk = 256 if t < 2 else 512
                        for h in range(4):
                            i = t * 4 + h
                            act.wait_ge(*after("smax", 0, i))
                            for m in range(2):
                                pr = v(ATS + (i % 2) * 1536 + m * 512, nk)
                                b = b_(0, "S", t, h, m)
                                c = 8 * (i % 2) + m
                                ev(AF(pr, bank[:, b, 0:nk], ACT.Exp, bias=small[:, c:c + 1], scale=SCALE64,
                                      accum_out=small[:, c + 2:c + 3]), 0, "S", t, h, m)
                            b = b_(0, "PT", i)
                            ev(a.copy(v(ATS + (i % 2) * 1536 + 1024, nk), bank[:, b, 0:nk]), 0, "PT", i)
                            b = b_(0, "O", i)
                            ev(a.copy(v3(MIX, 4, D)[:, t, 512 + h * P:512 + (h + 1) * P], bank[:, b, 0:P]), 0, "O", i)
                if l == 1:
                    for t in tiles:
                        b = b_(1, "kv", t, 0)
                        act.wait_ge(*after("k_roped", t))
                        ev(a.copy(v3(L1_V, 4, 256)[:, t, :], bank[:, b, 256:512]), 1, "kv", t, 0)
                    for t in LAT:
                        copy_T((1, "qT"), t, v3(L1_QT, 8, 256)[:, 0:4, (t - 2) * P:(t - 1) * P], 0)
                    for t in tiles:
                        copy_T((1, "kT"), t, v3(L1_KT, 2, TOK)[:, :, t * P:(t + 1) * P], 0, n=2)

                    def finish(i):
                        b = b_(1, "PT", i)
                        ev(a.copy(v(L1_PT + (i % 2) * 512, 512), bank[:, b, :]), 1, "PT", i)

                    for i in range(32):
                        b = b_(1, "S", i)
                        act.wait_ge(*after("smax", 1, i))
                        c = 8 * (i % 2)
                        if i >= 2:
                            act.wait_ge(*after("mm", 1, "PT", i - 2))
                        AF(v(L1_P + (i % 2) * 512, 512), bank[:, b, :], ACT.Exp, bias=small[:, c:c + 1], scale=SCALE64,
                           accum_out=small[:, c + 1:c + 2])
                        hq = head_of(i)
                        ev(AF(small[:, c + 2:c + 3], par("sink")[:, hq:hq + 1], ACT.Exp, bias=small[:, c:c + 1]), 1, "S", i)
                        if i >= 1:
                            finish(i - 1)
                    finish(31)
                if l == 2:
                    for c in range(8):
                        if c % 2 == 0:
                            b = b_(2, "uqn", c)
                            ev(a.copy(v3(L2_QNT, 8, 256)[:, c, :], bank[:, b, 0:256]), 2, "uqn", c)
                    for c in range(8):
                        if c % 2 == 0:
                            b = b_(2, "ukn", c)
                            ev(a.copy(v3(L2_KNT, 8, TOK)[:, c, :], bank[:, b, :]), 2, "ukn", c)
                    for part in range(2):
                        for t in tiles:
                            if t % 2 == 0:
                                b = b_(2, "uv", t, part)
                                ev(a.copy(v3(L2_V, 4, 1024)[:, t, part * 512:part * 512 + 512], bank[:, b, :]), 2, "uv", t, part)

                    def finish(i):
                        b = b_(2, "PT", i)
                        ev(a.copy(v(L2_PT + (i % 2) * 512, 512), bank[:, b, :]), 2, "PT", i)

                    for i in range(16):
                        b = b_(2, "S", i)
                        act.wait_ge(*after("smax", 2, i))
                        c = 8 * (i % 2)
                        if i >= 2:
                            act.wait_ge(*after("mm", 2, "PT", i - 2))
                        ev(AF(v(L2_P + (i % 2) * 512, 512), bank[:, b, :], ACT.Exp, bias=small[:, c:c + 1], scale=SCALE_MLA,
                              accum_out=small[:, c + 1:c + 2]), 2, "S", i)
                        if i >= 1:
                            finish(i - 1)
                    finish(15)
                if l == 3:
                    for t in LAT:
                        b = b_(3, "in0", t, 0)
                        ev(a.copy(v3(L3_Z, 2, 1024)[:, t - 2, 0:512], bank[:, b, :]), 3, "in0", t, 0)
                    for c in range(0, 8, 2):
                        b = b_(3, "pool", c)
                        ev(a.copy(v3(L3_POOLT, 8, 256)[:, c, :], bank[:, b, 0:256]), 3, "pool", c)
                    for c in range(0, 8, 2):
                        b = b_(3, "yT", c)
                        ev(AF(v3(L3_YT, 8, 256)[:, c, :], bank[:, b, 0:256], ACT.Copy, scale=par("pool_scale")[:, c:c + 1]), 3, "yT", c)
                out_tiles = PEER_TILES[l]
                if l < 3:
                    for t in out_tiles:
                        copy_T((l, "mT"), t, mixT[:, 0:4, t * P:(t + 1) * P], 0)
                t0 = out_tiles[0]
                for t in out_tiles:
                    copy_T((l, "xT2"), t, xT2[:, 0:4, (t - t0) * P:(t - t0 + 1) * P], 0)
                ntok = len(out_tiles) * P
                for c in range(0, 2 * PH, 2):
                    b = b_(l, "q", c)
                    ev(a.copy(qT[:, c, 0:ntok], bank[:, b, 0:ntok]), l, "q", c)
                for i in range(len(out_tiles)):
                    for j in range(0, 4, 2):
                        b = b_(l, "sc", i, j)
                        ev(a.copy(scores[:, i * PH + 2 * j:i * PH + 2 * j + 2, :].rearrange("p a b -> p (a b)"), bank[:, b, :]), l, "sc", i, j)

                def exps(wait):
                    act.wait_ge(topk_done, wait)
                    act.nop(nofuse=True)
                    AF(ex[:, :], cv[:, :], ACT.Exp, bias=neg[:, :], accum_out=es[:, :]).then_inc(exp_done, 1)

                k0 = HEADS_BEFORE[l] + l
                act.wait_ge(*after("ev", l, "sc", 0, 0))
                a.copy(head_scores[:, :], scores[:, 0, :]).then_inc(head_copied, 1)
                exps(k0 + 1)
                for i in range(len(out_tiles)):
                    if i == 0:
                        for i_ in range(len(out_tiles)):
                            act.wait_ge(*after("ev", l, "sc", i_, 3))
                            act.wait_ge(*after("ev", l, "sc", i_, 1))
                        act.wait_ge(*after("pad_scores", l))
                    q0 = HEADS_BEFORE[l] + i * PH
                    with act.Fori(0, PH // 2) as it:
                        for e in range(2):
                            act.wait_ge(topk_done, it * 2 + (q0 + l + e + 1))
                            act.nop(nofuse=True)
                            a.copy(head_scores[:, :], scores[:, ds(it * 2 + (i * PH + e + 1), 1), :].rearrange("p a b -> p (a b)"))\
                                .then_inc(head_copied, 1)
                            for j in range(GPH):
                                s = j % SLOTS
                                act.wait_ge(dots_done, it * (2 * GPH) + (q0 * GPH + e * GPH + j + 1))
                                act.nop(nofuse=True)
                                AF(gel[:, s, :], dot[:, s, :], ACT.Gelu)
                                act.drain()
                                for x in range(GROUP):
                                    AF(wgt[:, s, x:x + 1], gel[:, s, x:x + 1], ACT.Copy, scale=gate[:, e, GROUP * j + x:GROUP * j + x + 1])
                                act.drain()
                                for x in range(GROUP):
                                    ins = AF(diag[:, s, x, :], ident, ACT.Copy, scale=wgt[:, s, x:x + 1])
                                ins.then_inc(diag_done, 1)
                                if j == 1:
                                    exps(it * 2 + (q0 + l + e + 2))

        @block.vector
        def _(dve):
            V = nc.vector

            def b_(*key):
                dve.wait_ge(*after("mm", *key))
                return known.get(("bank",) + key, 0)

            def ev(ins, *key, more=()):
                ins.then_inc(sems["dve"], done("dve", ("ev",) + key, *more))

            def sig(ins, *events):
                ins.then_inc(sems["dve"], done("dve", *events))

            def row(l, name, s):
                n = ROW_AT[(l, name, s)]
                dve.wait_ge(r_landed[n % RSLOTS], 16 * (n // RSLOTS + 1))
                return n, rring[:, n % RSLOTS, :]

            def squares(src, sq, ss):
                V.tensor_tensor_reduce(out=sq, in0=src, in1=src, scale=1.0, scalar=0.0, op0=ALU.mult, op1=ALU.add, accum_out=ss)

            def rsqrt(x, scale, eps):
                n = x.shape[-1]
                y, t_ = newton[:, 0:n], newton[:, 32:32 + n]
                dve.drain()
                V.tensor_scalar(x, x, scale, eps, ALU.mult, ALU.add)
                dve.drain()
                V.tensor_scalar(t_.bitcast(U32), x.bitcast(U32), 1, None, ALU.logical_shift_right)
                dve.drain()
                V.tensor_scalar(y.bitcast(U32), t_.bitcast(U32), -1.0, float(0x5F3759DF), ALU.mult, ALU.add)
                dve.drain()
                for _ in range(3):
                    V.scalar_tensor_tensor(out=t_, in0=y, scalar=-0.5, in1=y, op0=ALU.mult, op1=ALU.mult)
                    dve.drain()
                    V.tensor_tensor(t_, t_, x, ALU.mult)
                    dve.drain()
                    V.scalar_tensor_tensor(out=y, in0=t_, scalar=1.5, in1=y, op0=ALU.add, op1=ALU.mult)
                    dve.drain()
                V.tensor_copy(x, y)
                dve.drain()

            def modulated(l, tiles, s, names, dst, event, norm, off=0):
                g_, sc_, sh_ = names
                rows_ = []
                if norm:
                    ng, g = row(l, g_, s)
                    rows_.append(ng)
                nsc, sc = row(l, sc_, s)
                nsh, sh = row(l, sh_, s)
                rows_ += [nsc, nsh]
                if norm:
                    V.scalar_tensor_tensor(out=sc, in0=sc, scalar=1.0, in1=g, op0=ALU.add, op1=ALU.mult)
                else:
                    V.tensor_scalar(sc, sc, 1.0, None, ALU.add)
                dve.drain()
                if norm:
                    for t in tiles:
                        squares(H[:, t, :], dst[:, t - off, :], small[:, 32 + t:33 + t])
                    rsqrt(small[:, 32 + tiles[0]:33 + tiles[-1]], 1.0 / D, EPS)
                for t in tiles:
                    y = dst[:, t - off, :]
                    if norm:
                        V.scalar_tensor_tensor(out=y, in0=H[:, t, :], scalar=small[:, 32 + t:33 + t], in1=sc, op0=ALU.mult, op1=ALU.mult)
                    else:
                        V.tensor_tensor(y, H[:, t, :], sc, ALU.mult)
                    dve.drain()
                    evs = [(event, l, t)]
                    if t == tiles[-1]:
                        evs += [("row", n) for n in rows_]
                    sig(V.tensor_tensor(y, y, sh, ALU.add), *evs)

            def layernorm(l, which):
                ng, g = row(l, "lng", which)
                nb, b2 = row(l, "lnb", which)
                for t in LAT:
                    for c in range(2):
                        V.bn_stats(small[:, 40 + 6 * c:46 + 6 * c], H[:, t, c * 512:(c + 1) * 512])
                    dve.drain()
                    V.bn_aggr(small[:, 32 + 2 * (t - 2):34 + 2 * (t - 2)], small[:, 40:52])
                    dve.drain()
                V.tensor_copy(small[:, 56:58], small[:, 33:37:2])
                rsqrt(small[:, 56:58], 1.0, LN_EPS)
                for t in LAT:
                    x = H[:, t, :]
                    V.tensor_scalar(x, x, small[:, 32 + 2 * (t - 2):33 + 2 * (t - 2)], small[:, 54 + t:55 + t], ALU.subtract, ALU.mult)
                    dve.drain()
                    V.tensor_tensor(x, x, g, ALU.mult)
                    dve.drain()
                    evs = [("ln", l, which, t)] + ([("row", ng), ("row", nb)] if t == 3 else [])
                    sig(V.tensor_tensor(x, x, b2, ALU.add), *evs)
                dve.drain()

            def rope(dst, src, t, groups, tmp):
                cos = const("cos")[:, (t - 2) * 32:(t - 1) * 32].unsqueeze(1).broadcast_to([P, groups, 32])
                sin = const("sin")[:, (t - 2) * 32:(t - 1) * 32].unsqueeze(1).broadcast_to([P, groups, 32])
                ta, tb = tmp
                V.tensor_tensor(dst[:, :, 0, :], src[:, :, 0, :], cos, ALU.mult)
                V.tensor_tensor(ta, src[:, :, 1, :], sin, ALU.mult)
                V.tensor_tensor(dst[:, :, 1, :], src[:, :, 0, :], sin, ALU.mult)
                V.tensor_tensor(tb, src[:, :, 1, :], cos, ALU.mult)
                dve.drain()
                V.tensor_tensor(dst[:, :, 0, :], dst[:, :, 0, :], ta, ALU.subtract)
                return V.tensor_tensor(dst[:, :, 1, :], dst[:, :, 1, :], tb, ALU.add)

            def groups32(ap):
                return ap.rearrange("p (g a b) -> p g a b", a=2, b=32)

            def copy_T(key, t, dst, half, n=4):
                b = b_(*key, t, half)
                ev(V.tensor_copy(dst, bank3(b, n, P)), *key, t, half)

            dve.wait_ge(params_landed, 16)
            for l in range(LAYERS):
                b = b_("mod", l)
                if l:
                    dve.wait_ge(*after("mm", "modT", l - 1))
                mb = par("mod_b")[:, l * MODC:(l + 1) * MODC].unsqueeze(1).broadcast_to([P, 2, MODC])
                ev(V.tensor_tensor(modcol[:, :].rearrange("p (a b) -> p a b", a=2), bank3(b, 2, MODC), mb, ALU.add), "mod", l)
            lam = par("lam").rearrange("p (a b) -> p a b", a=4)
            for q in range(2):
                V.tensor_tensor_reduce(out=left[:, q * 64:(q + 1) * 64], in0=lam[:, 2 * q, :], in1=lam[:, 2 * q + 1, :], scale=1.0,
                                       scalar=0.0, op0=ALU.mult, op1=ALU.add, accum_out=lamc[:, q:q + 1])
            sig(dve.drain(), ("lam_dots",))
            dve.wait_ge(consts_landed, 16)
            dve.wait_ge(hidden_landed, 16)

            for l in range(LAYERS):
                tiles = LT[l]
                norm = l < 2
                if l == 2:
                    dve.wait_ge(ctx2_landed, 16)
                if l != 3:
                    modulated(l, CTX, 1, ("g1", "sc1", "sh1"), xn, "xn", norm)
                modulated(l, LAT, 0, ("g1", "sc1", "sh1"), xn, "xn", norm)
                for t in tiles:
                    copy_T((l, "xT"), t, xT[:, 4:8, t * P:(t + 1) * P], 1)
                if l == 0:
                    raw = v4(RAW, 4, 2, 258)
                    qk = v3(QKT, 4, TOK)
                    V.memset(raw[:, :, :, 0:1], 0.0)
                    V.memset(raw[:, :, :, 257:258], 0.0)
                    sig(V.memset(v4(VML, 4, 4, 129)[:, :, :, 128:129], 1.0), ("vml_ones",))
                    cw = par("conv_w").rearrange("p (c j) -> p c j", c=4)
                    for c in range(4):
                        b = b_(0, "qk", c)
                        ev(V.tensor_copy(raw[:, c, :, 1:257], bank3(b, 2, 256)), 0, "qk", c)
                        dve.drain()
                        y = qk[:, c, :].rearrange("p (a b) -> p a b", a=2)
                        V.tensor_scalar(y, raw[:, c, :, 0:256], cw[:, c, 0:1], par("conv_b")[:, c:c + 1], ALU.mult, ALU.add)
                        dve.drain()
                        V.scalar_tensor_tensor(out=y, in0=raw[:, c, :, 1:257], scalar=cw[:, c, 1:2], in1=y, op0=ALU.mult, op1=ALU.add)
                        dve.drain()
                        sig(V.scalar_tensor_tensor(out=y, in0=raw[:, c, :, 2:258], scalar=cw[:, c, 2:3], in1=y, op0=ALU.mult,
                                                   op1=ALU.add), ("conv", c))
                    gw = arena[0:4, GW:GW + 4096].rearrange("p (q d t) -> p q d t", q=4, d=2)
                    zi, zf, tmp, fl = (gw[:, q, :, :] for q in range(4))
                    mrow = arena[0:4, MROW:MROW + 1024].rearrange("p (a b) -> p a b", a=2)
                    for g in range(4):
                        b = b_(0, "gates", g)
                        dst = (zi, zf)[g % 2]
                        bias = params[0:4, PT_["gate_b"][0] + g:PT_["gate_b"][0] + g + 1]
                        if g < 2:
                            ins = V.tensor_scalar(dst[:, 0, :], bank[0:4, b, :], bias, None, ALU.add)
                        else:
                            V.tensor_scalar(dst[:, 1, 0:256], bank[0:4, b, 255::-1], bias, None, ALU.add)
                            ins = V.tensor_scalar(dst[:, 1, 256:512], bank[0:4, b, 511:255:-1], bias, None, ALU.add)
                        ev(ins, 0, "gates", g)
                    dve.drain()
                    sig(V.scalar_tensor_tensor(out=tmp, in0=zf, scalar=-1.0, in1=zf, op0=ALU.mult, op1=ALU.max), ("absz",))
                    V.tensor_scalar(zf, zf, 0.0, None, ALU.min)
                    dve.wait_ge(*after("softplus"))
                    dve.drain()
                    V.tensor_tensor(zf, zf, tmp, ALU.subtract)
                    V.memset(fl, 1.0)
                    dve.drain()
                    for d in range(2):
                        V.tensor_tensor_scan(tmp[:, d, :], fl[:, d, :], zf[:, d, :], 0.0, ALU.mult, ALU.add)
                    dve.drain()
                    V.tensor_tensor(zi, zi, tmp, ALU.subtract)
                    dve.drain()
                    for d in range(2):
                        V.tensor_tensor_scan(fl[:, d, :], zi[:, d, :], zi[:, d, :], 0.0, ALU.max, ALU.max)
                    dve.drain()
                    V.tensor_tensor(tmp, tmp, fl, ALU.add)
                    dve.drain()
                    V.tensor_copy(zf[:, 0, :], tmp[:, 0, :])
                    V.tensor_scalar(mrow[:, 0, :], fl[:, 0, :], -1.0, None, ALU.mult)
                    for c0 in (0, 256):
                        V.tensor_copy(zf[:, 1, c0:c0 + 256], tmp[:, 1, rev(c0)])
                        V.tensor_scalar(mrow[:, 1, c0:c0 + 256], fl[:, 1, rev(c0)], -1.0, None, ALU.mult)
                    dve.drain()
                    V.tensor_copy(tmp[:, 0, :], zi[:, 0, :])
                    V.tensor_copy(tmp[:, 1, 0:256], zi[:, 1, rev(0)])
                    sig(V.tensor_copy(tmp[:, 1, 256:512], zi[:, 1, rev(256)]), ("m_rows",))
                    rt = (v3(DMASK, 8, 32), v3(DMASK + 256, 8, 32))
                    for q, name in enumerate(("dq", "dk")):
                        for t in tiles:
                            b = b_(0, name, t, 0)
                            dst = xn[:, t, q * 512:(q + 1) * 512]
                            if t < 2:
                                ins = V.tensor_copy(dst, bank[:, b, :])
                            else:
                                ins = rope(groups32(dst), groups32(bank[:, b, :]), t, 8, rt)
                                dve.drain()
                            if q:
                                ev(ins, 0, name, t, 0, more=(("roped", t),))
                            else:
                                ev(ins, 0, name, t, 0)
                    for t in tiles:
                        copy_T((0, "dqkT"), t, v3(DKT, 4, TOK)[:, :, t * P:(t + 1) * P], 1)
                    dve.wait_ge(*after("floor_rows"))
                    sig(dve.drain(), ("gate_rows",))
                    b = b_(0, "gcols")
                    ev(V.tensor_copy(gcols[:, :], bank[:, b, 0:64]), 0, "gcols")
                    dve.drain()
                    ats = v3(ATS, 4, TOK)
                    mix = v3(MIX, 4, D)

                    def masked(h, d):
                        b = b_(0, "M", h, d)
                        if h or d:
                            dve.wait_ge(*after("E", *((h, 0) if d else (h - 1, 1))))
                        tri = const("tri")[:, d * P:(d + 1) * P].unsqueeze(1).broadcast_to([P, 4, P])
                        sig(V.tensor_tensor(v3(DMASK, 4, P), bank3(b, 4, P), tri, ALU.add), ("dmask", h, d))

                    for h in range(4):
                        for d in range(2):
                            wt = v3(EW1 if d else EW0, 4, TOK)
                            masked(h, d)
                            for s in range(4):
                                dve.wait_ge(*after("ev", 0, "A", h, s))
                            dve.wait_ge(*after("E", h, d))
                            for s in range(4):
                                for t0, t1 in [(s, s + 1)] + OFF_DIAGONAL[d][s]:
                                    ins = V.tensor_tensor(wt[:, s, t0 * P:t1 * P], wt[:, s, t0 * P:t1 * P],
                                                          ats[:, s, t0 * P:t1 * P], ALU.mult)
                            sig(ins, ("WT", h, d))
                        for d in range(2):
                            for tp in range(2):
                                b = b_(0, "N", h, d, tp)
                                nd = bank[:, b, 0:258].rearrange("p (a n) -> p a n", a=2)
                                den = small[:, 8 * tp:8 * tp + 2]
                                c = 32 + (d * 4 + 2 * tp) * 4 + h
                                V.tensor_copy(den, nd[:, :, 128])
                                dve.drain()
                                V.scalar_tensor_tensor(out=den, in0=den, scalar=-1.0, in1=den, op0=ALU.mult, op1=ALU.max)
                                dve.drain()
                                V.tensor_tensor(den, den, gcols[:, c:c + 5:4], ALU.max)
                                dve.drain()
                                V.reciprocal(den, den)
                                dve.drain()
                                for q in range(2):
                                    t = 2 * tp + q
                                    dst = mix[:, t, h * P:(h + 1) * P]
                                    if d == 0:
                                        ins = V.tensor_scalar(dst, nd[:, q, 0:128], den[:, q:q + 1], None, ALU.mult)
                                    else:
                                        ins = V.scalar_tensor_tensor(out=dst, in0=nd[:, q, 0:128], scalar=den[:, q:q + 1], in1=dst,
                                                                     op0=ALU.mult, op1=ALU.add)
                                ev(ins, 0, "N", h, d, tp)
                    dve.wait_ge(*after("lam_exp"))
                    V.tensor_tensor(lamc[:, 2:3], lamc[:, 1:2], lamc[:, 0:1], ALU.subtract)
                    dve.drain()
                    V.tensor_scalar(lamc[:, 3:4], lamc[:, 2:3], LAM_INIT, None, ALU.subtract)
                    dve.drain()

                    def da_max(i):
                        t, h = i // 4, i % 4
                        nk = 256 if t < 2 else 512
                        c = 8 * (i % 2)
                        for m in range(2):
                            b = b_(0, "S", t, h, m)
                            V.tensor_reduce(small[:, c + 4 + m:c + 5 + m], bank[:, b, 0:nk], AX_X, ALU.max)
                        dve.drain()
                        sig(V.tensor_scalar(small[:, c:c + 2], small[:, c + 4:c + 6], -SCALE64, None, ALU.mult), ("smax", 0, i))

                    for i in range(16):
                        t, h = i // 4, i % 4
                        nk = 256 if t < 2 else 512
                        c = 8 * (i % 2)
                        da_max(i)
                        dve.wait_ge(*after("ev", 0, "S", t, h, 1))
                        pr0, pr1 = v(ATS + (i % 2) * 1536, nk), v(ATS + (i % 2) * 1536 + 512, nk)
                        V.reciprocal(small[:, c + 2:c + 4], small[:, c + 2:c + 4])
                        dve.drain()
                        V.tensor_scalar(pr0, pr0, small[:, c + 2:c + 3], None, ALU.mult)
                        V.tensor_scalar(pr1, pr1, small[:, c + 3:c + 4], lamc[:, 3:4], ALU.mult, ALU.mult)
                        dve.drain()
                        sig(V.tensor_tensor(pr0, pr0, pr1, ALU.add), ("Pr", 0, i))
                    nh, hg = row(0, "headg", 0)
                    dve.wait_ge(*after("ev", 0, "O", 15))
                    ss = gcols[:, 0:32]
                    for t in tiles:
                        x = mix[:, t, :].rearrange("p (h c) -> p h c", h=8)
                        sq = v3(ATS + (t % 2) * 1024, 8, P)
                        V.tensor_tensor(sq, x, x, ALU.mult)
                        dve.drain()
                        V.tensor_reduce(ss[:, 8 * t:8 * t + 8], sq, AX_X, ALU.add)
                    rsqrt(ss, 1.0 / P, EPS)
                    for t in tiles:
                        x = mix[:, t, :].rearrange("p (h c) -> p h c", h=8)
                        V.tensor_tensor(x, x, ss[:, 8 * t:8 * t + 8].unsqueeze(2).broadcast_to([P, 8, P]), ALU.mult)
                        dve.drain()
                        V.tensor_tensor(mix[:, t, :], mix[:, t, :], hg, ALU.mult)
                        dve.drain()
                        dve.wait_ge(*after("ev", 0, "o", t, 0))
                        V.tensor_tensor(mix[:, t, 0:512], mix[:, t, 0:512], v(OSIG + t * 512, 512), ALU.mult)
                        evs = [("mix", 0, t)] + ([("row", nh)] if t == 3 else [])
                        sig(V.tensor_scalar(mix[:, t, 512:1024], mix[:, t, 512:1024], 1.0 - LAM_INIT, None, ALU.mult), *evs)
                if l == 1:
                    qn, kn = v3(L1_QN, 2, 1024), v3(L1_KN, 4, 256)
                    rt = (v3(L1_P, 8, 32), v3(L1_P + 256, 8, 32))
                    for q in range(2):
                        for t in LAT:
                            b = b_(1, f"q{q}", t, 0)
                            ins = rope(groups32(qn[:, t - 2, q * 512:(q + 1) * 512]), groups32(bank[:, b, :]), t, 8, rt)
                            dve.drain()
                            more = (("q_roped", t),) if q else ()
                            ev(ins, 1, f"q{q}", t, 0, more=more)
                    rt4 = (v3(L1_P, 4, 32), v3(L1_P + 128, 4, 32))
                    for t in tiles:
                        b = b_(1, "kv", t, 0)
                        if t < 2:
                            ins = V.tensor_copy(kn[:, t, :], bank[:, b, 0:256])
                        else:
                            ins = rope(groups32(kn[:, t, :]), groups32(bank[:, b, 0:256]), t, 4, rt4)
                            dve.drain()
                        sig(ins, ("k_roped", t))
                    for t in LAT:
                        copy_T((1, "qT"), t, v3(L1_QT, 8, 256)[:, 4:8, (t - 2) * P:(t - 1) * P], 1)
                    mix = v3(MIX, 2, D)
                    V.tensor_scalar(gcols[:, 0:16], par("sink"), 1.0 / SCALE64, None, ALU.mult)
                    dve.drain()

                    def finish(i):
                        b = b_(1, "O", i)
                        t, hq = i // 16, head_of(i)
                        ev(V.tensor_scalar(mix[:, t, hq * 64:hq * 64 + 64], bank[:, b, 0:64], small[:, 8 * (i % 2) + 3:8 * (i % 2) + 4],
                                           None, ALU.mult), 1, "O", i)

                    for i in range(32):
                        t, c, hq = i // 16, 8 * (i % 2), head_of(i)
                        b = b_(1, "S", i)
                        off = 256 + (P if t == 0 else 0)
                        V.tensor_tensor(bank[:, b, off:off + P], bank[:, b, off:off + P], const("win")[:, t * P:(t + 1) * P], ALU.add)
                        dve.drain()
                        V.tensor_reduce(small[:, c + 4:c + 5], bank[:, b, :], AX_X, ALU.max)
                        dve.drain()
                        sig(V.tensor_scalar(small[:, c:c + 1], small[:, c + 4:c + 5], gcols[:, hq:hq + 1], -SCALE64, ALU.max, ALU.mult),
                            ("smax", 1, i))
                        if i >= 1:
                            finish(i - 1)
                        dve.wait_ge(*after("ev", 1, "S", i))
                        V.tensor_tensor(small[:, c + 3:c + 4], small[:, c + 1:c + 2], small[:, c + 2:c + 3], ALU.add)
                        dve.drain()
                        sig(V.reciprocal(small[:, c + 3:c + 4], small[:, c + 3:c + 4]), ("Pr", 1, i))
                    finish(31)
                    dve.drain()
                    sig(dve.drain(), ("mix", 1, 2), ("mix", 1, 3))
                if l == 2:
                    z = v3(L2_Z, 4, 704)
                    nm, mg = row(2, "mlag", 0)
                    kr = v3(L2_QR, 4, P)
                    for t in LAT:
                        b = b_(2, "zq", t, 0)
                        ev(V.tensor_copy(z[:, t, 0:384], bank[:, b, 0:384]), 2, "zq", t, 0)
                        dve.drain()
                        squares(z[:, t, 0:384], v(L2_PT, 384), small[:, 32:33])
                        rsqrt(small[:, 32:33], 1.0 / 384, EPS)
                        sig(V.scalar_tensor_tensor(out=z[:, t, 0:384], in0=z[:, t, 0:384], scalar=small[:, 32:33], in1=mg[:, 0:384],
                                                   op0=ALU.mult, op1=ALU.mult), ("zq_n", t))
                    rt1 = (v3(L2_P + 512, 1, 32), v3(L2_P + 544, 1, 32))
                    for t in tiles:
                        b = b_(2, "zkv", t, 0)
                        ev(V.tensor_copy(z[:, t, 384:704], bank[:, b, 0:320]), 2, "zkv", t, 0)
                        dve.drain()
                        squares(z[:, t, 384:640], v(L2_PT, 256), small[:, 32:33])
                        rsqrt(small[:, 32:33], 1.0 / 256, EPS)
                        evs = [("zkv_n", t)] + ([("row", nm)] if t == 3 else [])
                        sig(V.scalar_tensor_tensor(out=z[:, t, 384:640], in0=z[:, t, 384:640], scalar=small[:, 32:33],
                                                   in1=mg[:, 384:640], op0=ALU.mult, op1=ALU.mult), *evs)
                        if t < 2:
                            V.tensor_copy(kr[:, t, 0:64], z[:, t, 640:704])
                        else:
                            rope(groups32(kr[:, t, 0:64]), groups32(z[:, t, 640:704]), t, 1, rt1)
                        dve.drain()
                        sig(V.tensor_copy(kr[:, t, 64:128], kr[:, t, 0:64]), ("kr", t))
                    for t in tiles:
                        if t in LAT:
                            copy_T((2, "cqT"), t, v3(L2_CQT, 3, 256)[:, :, (t - 2) * P:(t - 1) * P], 0, n=3)
                        copy_T((2, "ckvT"), t, v3(L2_CKVT, 2, TOK)[:, :, t * P:(t + 1) * P], 0, n=2)
                        copy_T((2, "krT"), t, v3(L2_KRT, 1, TOK)[:, :, t * P:(t + 1) * P], 0, n=1)
                    for c in range(1, 8, 2):
                        b = b_(2, "uqn", c)
                        ev(V.tensor_copy(v3(L2_QNT, 8, 256)[:, c, :], bank[:, b, 0:256]), 2, "uqn", c)
                    qr = v3(L2_QR, 2, 512)
                    rt = (v3(L2_P, 8, 32), v3(L2_P + 256, 8, 32))
                    for t in LAT:
                        b = b_(2, "uqr", t, 0)
                        ins = rope(groups32(qr[:, t - 2, :]), groups32(bank[:, b, :]), t, 8, rt)
                        dve.drain()
                        ev(ins, 2, "uqr", t, 0, more=(("qr_roped", t),))
                    for c in range(1, 8, 2):
                        b = b_(2, "ukn", c)
                        ev(V.tensor_copy(v3(L2_KNT, 8, TOK)[:, c, :], bank[:, b, :]), 2, "ukn", c)
                    for part in range(2):
                        for t in tiles:
                            if t % 2:
                                b = b_(2, "uv", t, part)
                                ev(V.tensor_copy(v3(L2_V, 4, 1024)[:, t, part * 512:part * 512 + 512], bank[:, b, :]), 2, "uv", t, part)
                    for t in LAT:
                        copy_T((2, "qrT"), t, v3(L2_QRT, 4, 256)[:, :, (t - 2) * P:(t - 1) * P], 0)
                    mix = v3(L2_MIX, 2, D)

                    def finish(i):
                        b = b_(2, "O", i)
                        t, h = i // 8, i % 8
                        ev(V.tensor_scalar(mix[:, t, h * P:(h + 1) * P], bank[:, b, 0:P], small[:, 8 * (i % 2) + 3:8 * (i % 2) + 4],
                                           None, ALU.mult), 2, "O", i)

                    for i in range(16):
                        c = 8 * (i % 2)
                        b = b_(2, "S", i)
                        V.tensor_reduce(small[:, c + 4:c + 5], bank[:, b, :], AX_X, ALU.max)
                        dve.drain()
                        sig(V.tensor_scalar(small[:, c:c + 1], small[:, c + 4:c + 5], -SCALE_MLA, None, ALU.mult), ("smax", 2, i))
                        if i >= 1:
                            finish(i - 1)
                        dve.wait_ge(*after("ev", 2, "S", i))
                        sig(V.reciprocal(small[:, c + 3:c + 4], small[:, c + 1:c + 2]), ("Pr", 2, i))
                    finish(15)
                    dve.drain()
                    sig(dve.drain(), ("mix", 2, 2), ("mix", 2, 3))
                if l == 3:
                    for t in LAT:
                        b = b_(3, "in1", t, 0)
                        ev(V.tensor_copy(v3(L3_Z, 2, 1024)[:, t - 2, 512:1024], bank[:, b, :]), 3, "in1", t, 0)
                    for c in range(1, 8, 2):
                        b = b_(3, "pool", c)
                        ev(V.tensor_copy(v3(L3_POOLT, 8, 256)[:, c, :], bank[:, b, 0:256]), 3, "pool", c)
                    for c in range(1, 8, 2):
                        b = b_(3, "yT", c)
                        ev(V.tensor_scalar(v3(L3_YT, 8, 256)[:, c, :], bank[:, b, 0:256], par("pool_scale")[:, c:c + 1], None, ALU.mult),
                           3, "yT", c)
                out_tiles = PEER_TILES[l]
                t0 = out_tiles[0]
                if l < 3:
                    for t in out_tiles:
                        copy_T((l, "mT"), t, mixT[:, 4:8, t * P:(t + 1) * P], 1)
                gates_ = {s: row(l, "gate1", s) for s in ((1, 0) if l == 0 else (0,))}

                def residual(y, t, c0, c1, g, tmp_, events, post):
                    V.tensor_tensor(tmp_, y, g[:, c0:c1], ALU.mult)
                    dve.drain()
                    x = H[:, t, c0:c1]
                    if post:
                        ins = V.scalar_tensor_tensor(out=x, in0=x, scalar=ALPHA, in1=tmp_, op0=ALU.mult, op1=ALU.add)
                    else:
                        ins = V.tensor_tensor(x, x, tmp_, ALU.add)
                    sig(ins, *events)

                tmpr = v(RESID, 1024)
                for j in range(2):
                    for t in out_tiles:
                        b = b_(l, f"out{j}", t, 0)
                        ng, g = gates_[1 if t < 2 else 0]
                        evs = [("ev", l, f"out{j}", t, 0)]
                        if j == 1 and t in (1, 3):
                            evs.append(("row", ng))
                        residual(bank[:, b, :], t, j * 512, j * 512 + 512, g, tmpr[:, (t % 2) * 512:(t % 2) * 512 + 512], evs, l >= 2)
                dve.drain()
                if l >= 2:
                    layernorm(l, 0)
                if l == 0:
                    modulated(l, CTX, 1, ("g2", "sc2", "sh2"), xnat, "xnat", True)
                modulated(l, LAT, 0, ("g2", "sc2", "sh2"), xnat, "xnat", norm, off=t0)
                for t in out_tiles:
                    copy_T((l, "xT2"), t, xT2[:, 4:8, (t - t0) * P:(t - t0 + 1) * P], 1)
                ntok = len(out_tiles) * P
                for c in range(1, 2 * PH, 2):
                    b = b_(l, "q", c)
                    ev(V.tensor_copy(qT[:, c, 0:ntok], bank[:, b, 0:ntok]), l, "q", c)
                sig(V.memset(scores[:, len(out_tiles) * PH, :], 0.0), ("pad_scores", l))
                for i in range(len(out_tiles)):
                    for j in range(1, 4, 2):
                        b = b_(l, "sc", i, j)
                        ev(V.tensor_copy(scores[:, i * PH + 2 * j:i * PH + 2 * j + 2, :].rearrange("p a b -> p (a b)"), bank[:, b, :]),
                           l, "sc", i, j)

                def topk(wait, e):
                    dve.wait_ge(head_copied, wait)
                    dve.nop(nofuse=True)
                    hs = head_scores[:, :].rearrange("p (a b) -> p a b", a=2)
                    lf = left[:, :].rearrange("p (a b) -> p a b", a=2)
                    for q in range(2):
                        V.max(topv[:, q, 0:8], hs[:, q, :])
                    dve.drain()
                    for q in range(2):
                        V.max_index(topi[:, q, 0:8], topv[:, q, 0:8], hs[:, q, :])
                    for q in range(2):
                        V.match_replace(lf[:, q, :], topv[:, q, 0:8], hs[:, q, :], NEG)
                    dve.drain()
                    for q in range(2):
                        V.max(topv[:, q, 8:16], lf[:, q, :])
                    dve.drain()
                    for q in range(2):
                        V.max_index(topi[:, q, 8:16], topv[:, q, 8:16], lf[:, q, :])
                    cand = head_cand
                    V.tensor_tensor(cand.rearrange("p (a b) -> p a b", a=16), topv[:, 0, :].unsqueeze(2).broadcast_to([P, 16, 16]),
                                    topv[:, 1, :].unsqueeze(1).broadcast_to([P, 16, 16]), ALU.add)
                    dve.drain()
                    V.tensor_copy(topf[:, :, :], topi[:, :, :])
                    V.max(cv[:, 0:8], cand)
                    dve.drain()
                    V.max_index(ci[:, 0:8], cv[:, 0:8], cand)
                    V.match_replace(left[:, :], cv[:, 0:8], cand, NEG)
                    dve.drain()
                    V.max(cv[:, 8:16], left[:, :])
                    V.tensor_scalar(neg[:, :], cv[:, 0:1], -1.0, None, ALU.mult)
                    dve.drain()
                    V.max_index(ci[:, 8:16], cv[:, 8:16], left[:, :])
                    dve.drain()
                    V.tensor_scalar(ab[:, 0, :], ci[:, :], 4, None, ALU.logical_shift_right)
                    V.tensor_scalar(ab[:, 1, :], ci[:, :], 15, None, ALU.bitwise_and)
                    dve.drain()
                    V.tensor_copy(abf[:, :, :], ab[:, :, :])
                    dve.drain()
                    V.tensor_tensor(eq[:, :, :, :].rearrange("p a k m -> p (a k) m"),
                                    abf[:, :, :].rearrange("p a k -> p (a k)").unsqueeze(2).broadcast_to([P, 32, 16]),
                                    const("iota").unsqueeze(1).broadcast_to([P, 32, 16]), ALU.is_equal)
                    dve.drain()
                    for q in range(2):
                        V.tensor_tensor(eq[:, q, :, :], eq[:, q, :, :], topf[:, q, :].unsqueeze(1).broadcast_to([P, 16, 16]), ALU.mult)
                    dve.drain()
                    V.tensor_reduce(selv[:, :, :].rearrange("p a k -> p (a k)"), eq[:, :, :, :].rearrange("p a k m -> p (a k) m"),
                                    AX_X, ALU.add)
                    dve.drain()
                    V.scalar_tensor_tensor(out=ef[:, :], in0=selv[:, 0, :], scalar=float(NK), in1=selv[:, 1, :], op0=ALU.mult, op1=ALU.add)
                    dve.drain()
                    V.tensor_copy(idx[:, e, :], ef[:, :]).then_inc(topk_done, 1)

                def gates(wait, wait_free, e):
                    dve.wait_ge(exp_done, wait)
                    dve.nop(nofuse=True)
                    if wait_free is not None:
                        dve.wait_ge(diag_done, wait_free)
                        dve.nop(nofuse=True)
                    V.reciprocal(neg[:, :], es[:, :])
                    dve.drain()
                    V.tensor_scalar(gate[:, e, :], ex[:, :], neg[:, :], None, ALU.mult)

                head_cand = eq[:, 0, :, :].rearrange("p k m -> p (k m)")
                k0 = HEADS_BEFORE[l] + l
                topk(k0 + 1, 0)
                gates(k0 + 1, None, 0)
                gate_rows = {s: row(l, "gate2", s) for s in ((1, 0) if l == 0 else (0,))}
                for i, t in enumerate(out_tiles):
                    q0 = HEADS_BEFORE[l] + i * PH
                    with dve.Fori(0, PH // 2) as it:
                        for e in range(2):
                            for j in range(GPH):
                                s = j % SLOTS
                                dve.wait_ge(ring_landed[s], it * (2 * GPH // SLOTS * GROUP * 16)
                                            + ((q0 * GPH + e * GPH + j) // SLOTS + 1) * GROUP * 16)
                                for x in range(GROUP):
                                    ins = V.tensor_tensor_reduce(out=ring[:, s, x, 0:D], in0=ring[:, s, x, 0:D], in1=xnat[:, i, :],
                                                                 scale=1.0, scalar=0.0, op0=ALU.mult, op1=ALU.add,
                                                                 accum_out=dot[:, s, x:x + 1])
                                ins.then_inc(dots_done, 1)
                                if j == 1:
                                    topk(it * 2 + (q0 + l + e + 2), (e + 1) % 2)
                                if j == 4:
                                    gates(it * 2 + (q0 + l + e + 2), it * (2 * GPH) + (q0 * GPH + e * GPH + 1), (e + 1) % 2)
                    dve.wait_ge(slots_free, SLOTS + (q0 + PH) * GPH)
                    y = bank[:, 2 * (i % 2):2 * (i % 2) + 2, :].rearrange("p a b -> p (a b)")
                    ng, g = gate_rows[1 if t < 2 else 0]
                    evs = [("y_taken", l, i)]
                    if t in (1, 3):
                        evs.append(("row", ng))
                    residual(y, t, 0, D, g, xnat[:, i, :], evs, l >= 2)
                    dve.drain()
                if l == 1:
                    nf, fg = row(1, "final", 0)
                    for t in LAT:
                        squares(H[:, t, :], xnat[:, t - 2, :], small[:, 32 + t:33 + t])
                    rsqrt(small[:, 34:36], 1.0 / D, EPS)
                    for t in LAT:
                        evs = [("final1", t)] + ([("row", nf)] if t == 3 else [])
                        sig(V.scalar_tensor_tensor(out=H[:, t, :], in0=H[:, t, :], scalar=small[:, 32 + t:33 + t], in1=fg, op0=ALU.mult,
                                                   op1=ALU.mult), *evs)
                    dve.drain()
                if l >= 2:
                    layernorm(l, 1)
            sig(dve.drain(), ("final_out",))
        return st.at




def _blocks(inp, f32):
    def tiled(w, k=KC):
        return w.reshape(k, P, -1).transpose(1, 0, 2).reshape(P, -1)

    def cut(w, j, k=KC):
        return tiled(w[:, 512 * j:512 * (j + 1)], k)

    out = np.zeros((len(BLOCKS), P, WCOLS), f32)

    def put(name, a):
        n = BLOCK_AT[name]
        assert a.shape == (P, BLOCKS[n][1]), (name, a.shape)
        out[n, :, :a.shape[1]] = a

    for l in range(LAYERS):
        w = (inp["mod_w"] if l < 2 else inp["w_mod_2"])[l % 2]
        for n in range(MODC // 4):
            put((l, "mod", n), cut(w, n))
        wq = (inp["pr_w_q"] if l < 2 else inp["peer_w_q_2"])[l % 2]
        for n in range(4):
            put((l, "wq", n), cut(wq, n))
        if l < 2:
            keys = inp["pr_keys"][l]
        else:
            keys = np.stack([inp["peer_k1_2"][l - 2], inp["peer_k2_2"][l - 2]], axis=1)
        put((l, "keys"), keys.reshape(2 * PH, NK, P).transpose(2, 0, 1).reshape(P, -1))
    w = inp["ev_w_in"][0]
    put((0, "qk"), tiled(w[:, 0:512]))
    put((0, "v"), tiled(w[:, 512:1024]))
    put((0, "o"), tiled(w[:, 1024:1536]))
    put((0, "gates"), tiled(w[:, 1536:1552]))
    for j, n in enumerate(("dq", "dk", "dv")):
        put((0, n), tiled(w[:, 1552 + 512 * j:2064 + 512 * j]))
    w = inp["od_w_in"][0]
    order = [head_of(i) for i in range(16)]
    wq = w[:, :1024].reshape(D, 16, 64)[:, order].reshape(D, 1024)
    put((1, "q0"), cut(wq, 0))
    put((1, "q1"), cut(wq, 1))
    put((1, "kv"), tiled(w[:, 1024:]))
    w = inp["mla_w_in_2"][0]
    put((2, "zq"), tiled(w[:, :384]))
    put((2, "zkv"), tiled(w[:, 384:]))
    uq = inp["mla_w_uq_2"][0].reshape(384, 8, 192)
    put((2, "uqn"), tiled(uq[:, :, :128].reshape(384, 1024), 3))
    put((2, "uqr"), tiled(uq[:, :, 128:].reshape(384, 512), 3))
    ukv = inp["mla_w_ukv_2"][0].reshape(256, 8, 256)
    put((2, "ukn"), tiled(ukv[:, :, :128].reshape(256, 1024), 2))
    put((2, "uv"), tiled(ukv[:, :, 128:].reshape(256, 1024), 2))
    put((3, "in0"), cut(inp["pool_w_in_2"][0], 0))
    put((3, "in1"), cut(inp["pool_w_in_2"][0], 1))
    band = np.zeros((SEQ, 4, SEQ), f32)
    for g, win in enumerate((2, 4, 8, 16)):
        for t in range(SEQ):
            lo, hi = max(t - win // 2, 0), min(t + win // 2, SEQ)
            band[lo:hi, g, t] = 1.0 / (hi - lo)
            band[t, g, t] -= 1.0
    put((3, "band"), tiled(band.reshape(SEQ, -1), 2))
    put((3, "grp"), inp["pool_w_grp_2"][0].reshape(4, 2, P, 256).transpose(2, 0, 1, 3).reshape(P, -1))
    for l, w in enumerate((inp["ev_w_out"][0], inp["od_w_out"][0], inp["mla_w_o_2"][0], inp["pool_w_out_2"][0])):
        put((l, "out0"), cut(w, 0))
        put((l, "out1"), cut(w, 1))
    return out


def _consts(f32):
    c = np.zeros((P, CT_COLS), f32)
    p, j = np.arange(P)[:, None], np.arange(P)[None, :]

    def at(name):
        o, n = CT[name]
        return c[:, o:o + n]

    at("ident")[:] = np.eye(P)
    at("tri")[:, :P] = np.where(p <= j, 0, MASK)
    at("tri")[:, P:] = np.where(p >= j, 0, MASK)
    at("win")[:, :P] = np.where(j <= p, 0, MASK)
    at("win")[:, P:] = np.where(j >= p, 0, MASK)
    pos = np.arange(SEQ)
    inv = (10000.0 ** (-np.arange(16, dtype=np.float64) / 16))
    ang = np.concatenate([(pos // 64)[:, None] * inv, (pos % 64)[:, None] * inv], axis=1)
    at("cos")[:] = np.cos(ang).reshape(2, P, 32).transpose(1, 0, 2).reshape(P, 64)
    at("sin")[:] = np.sin(ang).reshape(2, P, 32).transpose(1, 0, 2).reshape(P, 64)
    at("iota")[:] = np.arange(16)[None]
    for h in range(4):
        at("sel")[h, h * P:(h + 1) * P] = 1
    return c


def _params(inp, f32):
    c = np.zeros((P, PT_COLS), f32)

    def at(name, rows=P):
        o, n = PT_[name]
        return c[:rows, o:o + n]

    at("conv_w")[:] = inp["ev_ml_conv_w"][0].reshape(3, 4, P).transpose(2, 1, 0).reshape(P, 12)
    at("conv_b")[:] = inp["ev_ml_conv_b"][0].reshape(4, P).T
    at("gate_b", 4)[:] = inp["ev_ml_gate_b"][0].reshape(4, 4).T
    at("lam")[:] = inp["ev_da_lam"][0].reshape(1, 256)
    at("sink")[:] = inp["od_sink"][0].reshape(1, 16)
    at("pool_scale")[:] = inp["pool_scale_2"][0].reshape(8, P).T
    cond = np.stack([inp["c"][0], inp["c_ctx"], inp["c_2"][0], inp["c_ctx_2"]])
    at("cond")[:] = cond.reshape(4, KC, P).transpose(2, 1, 0).reshape(P, 32)
    mb = np.concatenate([inp["mod_b"], inp["b_mod_2"]])
    at("mod_b")[:] = mb.reshape(LAYERS, MODC, P).transpose(2, 0, 1).reshape(P, -1)
    return c


def _gains(inp, f32):
    g = np.zeros((15, D), f32)
    for l in range(2):
        g[GAIN[("norm1", l)]] = inp["norm1_g"][l]
        g[GAIN[("norm2", l)]] = inp["norm2_g"][l]
        for s in range(2):
            g[GAIN[("lng", l + 2, s)]] = inp["ln_g_2"][l, s]
            g[GAIN[("lnb", l + 2, s)]] = inp["ln_b_2"][l, s]
    g[GAIN["headg"]] = np.concatenate([inp["ev_ml_norm_g"][0], inp["ev_da_norm_g"][0]])
    g[GAIN["final"]] = inp["final_g"]
    g[GAIN["mlag"], :384] = inp["mla_q_norm_2"][0]
    g[GAIN["mlag"], 384:640] = inp["mla_kv_norm_2"][0]
    return g


def layout(inputs):
    inp = {k: np.asarray(a) for k, a in inputs.items()}
    f32 = np.float32

    def tok(a):
        return a[0].reshape(2, P, D).transpose(1, 0, 2)

    arrays = {
        "hidden": np.ascontiguousarray(np.concatenate([tok(inp["ctx"]), tok(inp["x"])], axis=1)),
        "ctx2": np.ascontiguousarray(tok(inp["ctx_2"])),
        "weights": _blocks(inp, f32),
        "consts": _consts(f32),
        "params": _params(inp, f32),
        "gains": _gains(inp, f32),
    }
    for l in range(LAYERS):
        u = inp["pr_u" if l < 2 else "peer_u_2"][l % 2]
        v = inp["pr_v" if l < 2 else "peer_v_2"][l % 2]
        arrays[f"uv{l}"] = np.concatenate([u, v], axis=1)
    return arrays


def build(make, arrays):
    known = {}
    for _ in range(2):
        nc = make()
        A = {n: nc.dram_tensor(n, a.shape, mybir.dt.from_np(a.dtype), kind="ExternalInput").ap() for n, a in arrays.items()}
        A["out"] = nc.dram_tensor("out", (P, 2, D), F32, kind="ExternalOutput").ap()
        known = program(nc, A, known)
    return nc


def kernel(**inputs):
    import concourse.bacc as bacc
    from concourse.bass_utils import run_bass_kernel_spmd

    arrays = layout(inputs)
    nc = build(lambda: bacc.Bacc("TRN2", target_bir_lowering=False, num_devices=1), arrays)
    r = run_bass_kernel_spmd(nc, [arrays], core_ids=[0])
    out = r.results[0]["out"]
    return np.ascontiguousarray(out.transpose(1, 0, 2).reshape(1, SEQ, D))
```

```python
from contextlib import ExitStack

import numpy as np

import concourse.bass as bass
from concourse import mybir

F32 = mybir.dt.float32
U32 = mybir.dt.uint32
ALU = mybir.AluOpType
ACT = mybir.ActivationFunctionType
AX_X = mybir.AxisListType.X
ds = bass.ds

P = 128
D = 1024
KC = D // P
SEQ = 256
TILES = 4
CTX, LAT = (0, 1), (2, 3)
TOK = TILES * P
NMOD = 6
MODC = NMOD * KC
MODB = MODC // 4
LAYERS = 4
EPS = 1e-6
LN_EPS = 1e-5
ALPHA = 4.0 ** 0.25
LAM_INIT = 0.2
SCALE64 = 64.0 ** -0.5
SCALE_MLA = 192.0 ** -0.5
NEG = -3.0e38
MASK = -1.0e30

PH, TOPK, NK = 8, 16, 128
EXPERTS = NK * NK
SLOTS = 4
GROUP = 2
GPH = TOPK // GROUP
GPT = PH * GPH
PEER_TILES = [(0, 1, 2, 3), LAT, LAT, LAT]
HEADS_BEFORE = [sum(len(x) for x in PEER_TILES[:l]) * PH for l in range(LAYERS)]

ARENA = 29440
XNAT = 0
SCORES = XNAT + TILES * D
RING = SCORES + (TILES * PH + 1) * 2 * NK
XT2, QT = RING, RING + KC * TOK
XT2_LATE = XNAT + 2 * D
QT_LATE = SCORES + (2 * PH + 1) * 2 * NK
KEYS_LATE = QT_LATE + 8 * 2 * P
XT = 0
XN = 19488
MIX_T = 6160
RAW, QKT, VML, OSIG = 4096, 6160, 8208, 10272
DQT, DKT, DV, MIX = 13344, 15392, 17440, 19488
ATS, EW0, DMASK, MROW = 23584, 25632, 27680, 28192
EW1 = RAW
GW = ATS
L1_QN, L1_KN, L1_QT, L1_KT, L1_V, L1_P, L1_PT = 4096, 6144, 7168, 9216, 10240, 12544, 13568
L2_Z, L2_CQT, L2_CKVT, L2_KRT, L2_QNT, L2_QR, L2_QRT, L2_KNT, L2_V = (
    4096, 6912, 7680, 8704, 9216, 11264, 12288, 13312, 17408)
L2_MIX, L2_P, L2_PT = 21504, 23552, 24576
L3_Z, L3_POOLT, L3_YT = 4096, 6144, 8192
RESID = 10496
SOURCES = (((0,), (0, 1), (0, 1, 2), (0, 1, 2, 3)), ((0, 1), (1,), (0, 1, 2, 3), (0, 1, 3)))
OFF_DIAGONAL = (([(1, 4)], [(2, 4)], [(3, 4)], []), ([(2, 4)], [(0, 1), (2, 4)], [], [(2, 3)]))

WSLOTS, WCOLS = 2, 4096
RSLOTS = 5

CT = dict(ident=(0, 128), tri=(128, 256), win=(384, 256), cos=(640, 64), sin=(704, 64), iota=(768, 16), sel=(784, 512), zero=(1296, 512), add4=(1808, 2))
CT_COLS = 1810
PT_ = dict(conv_w=(0, 12), conv_b=(12, 4), gate_b=(16, 16), lam=(32, 256), sink=(288, 16), pool_scale=(304, 8),
           cond=(312, 64), mod_b=(376, LAYERS * MODC))
PT_COLS = 376 + LAYERS * MODC


def block_list():
    def block(l, *names, k=KC, width=512):
        return [((l, n), k * width) for n in names]

    def mods(l, first, last):
        return [((l, "mod", n), KC * 512) for n in range(first, last)]

    def queries(l):
        return [((l, "wq", n), KC * 512) for n in range(4)]

    out = mods(0, 0, 4) + block(0, "qk") + block(0, "gates", width=16) + block(0, "v", "o", "dq", "dk", "dv")
    out += mods(0, 4, MODB) + mods(1, 0, MODB) + block(0, "out0", "out1") + queries(0) + block(0, "keys", k=1, width=2048)
    out += block(1, "q0", "q1", "kv") + mods(2, 0, MODB) + block(1, "out0", "out1") + queries(1)
    out += block(2, "zq", width=384) + block(2, "zkv", width=320) + block(2, "uqn", k=3, width=1024) + block(2, "uqr", k=3)
    out += block(2, "ukn", "uv", k=2, width=1024) + mods(3, 0, MODB) + block(2, "out0", "out1") + queries(2)
    out += block(3, "in0", "in1") + block(3, "band", "grp", k=1, width=2048) + block(3, "out0", "out1") + queries(3)
    return out


BLOCKS = block_list()
BLOCK_AT = {name: n for n, (name, _) in enumerate(BLOCKS)}


def row_list():
    out = []

    def mod(l, s, m, name):
        out.append(((l, name, s), ("mod", l, s, m)))

    def par(l, name, s, r):
        out.append(((l, name, s), ("par", r)))

    for l in (0, 1):
        for s in (1, 0):
            par(l, "g1", s, GAIN[("norm1", l)])
            mod(l, s, 1, "sc1")
            mod(l, s, 0, "sh1")
        if l == 0:
            par(l, "headg", 0, GAIN["headg"])
        for s in ((1, 0) if l == 0 else (0,)):
            mod(l, s, 2, "gate1")
        for s in ((1, 0) if l == 0 else (0,)):
            par(l, "g2", s, GAIN[("norm2", l)])
            mod(l, s, 4, "sc2")
            mod(l, s, 3, "sh2")
        for s in ((1, 0) if l == 0 else (0,)):
            mod(l, s, 5, "gate2")
        if l == 1:
            par(l, "final", 0, GAIN["final"])
    for l in (2, 3):
        for s in ((1, 0) if l == 2 else (0,)):
            mod(l, s, 1, "sc1")
            mod(l, s, 0, "sh1")
        if l == 2:
            par(l, "mlag", 0, GAIN["mlag"])
        mod(l, 0, 2, "gate1")
        par(l, "lng", 0, GAIN[("lng", l, 0)])
        par(l, "lnb", 0, GAIN[("lnb", l, 0)])
        mod(l, 0, 4, "sc2")
        mod(l, 0, 3, "sh2")
        mod(l, 0, 5, "gate2")
        par(l, "lng", 1, GAIN[("lng", l, 1)])
        par(l, "lnb", 1, GAIN[("lnb", l, 1)])
    return out


GAIN = {("norm1", 0): 0, ("norm1", 1): 1, ("norm2", 0): 2, ("norm2", 1): 3, "headg": 4, "final": 5, "mlag": 6}
for _l in (2, 3):
    for _s in (0, 1):
        GAIN[("lng", _l, _s)] = 7 + 4 * (_l - 2) + _s
        GAIN[("lnb", _l, _s)] = 9 + 4 * (_l - 2) + _s
ROWS = row_list()
ROW_AT = {name: n for n, (name, _) in enumerate(ROWS)}


def rev(c0):
    return slice(c0 + 255, c0 - 1 if c0 else None, -1)


def head_of(i):
    c, side = (i % 16) // 2, i % 2
    return (2 * (c // 4) + side) * 4 + c % 4


MODS_FIRST = [(0, n) for n in range(4)]
MODS_BESIDE = {0: [(0, n) for n in range(4, MODB)] + [(1, n) for n in range(MODB)],
               1: [(2, n) for n in range(MODB)], 2: [(3, n) for n in range(MODB)]}
MOD_ORDER = MODS_FIRST + MODS_BESIDE[0] + MODS_BESIDE[1] + MODS_BESIDE[2]
MOD_SHARE = {0: [3] * 8 + [3] * 13, 1: [1, 2] * 16, 2: [3] * 16}


def mod_pieces(blocks):
    out = []
    for n, b in enumerate(blocks):
        out += [("low", b)] + ([("sum", blocks[n - 1])] if n else []) + [("high", b)]
    return out + [("sum", blocks[-1])]


def mod_ready(l, step):
    share = MOD_SHARE[l]
    before, now = sum(share[:step]), sum(share[:step + 1])
    return [p for p in mod_pieces(MODS_BESIDE[l])[before:now] if p[0] != "low"]


class Steps:

    def __init__(self, sems, known):
        self.sems, self.known, self.count, self.at = sems, known, dict.fromkeys(sems, 0), {}

    def done(self, engine, *events):
        self.count[engine] += 1
        for e in events:
            assert e not in self.at, e
            self.at[e] = (engine, self.count[engine])
        return 1

    def after(self, *event):
        engine, n = self.known.get(event, ("pe", 1))
        assert not self.known or event in self.known, event
        return self.sems[engine], n


def program(nc, A, known):
    with ExitStack() as ctx:
        def sb(name, shape, dt=F32):
            return ctx.enter_context(nc.sbuf_tensor(name, shape, dt))

        def sem(name):
            return ctx.enter_context(nc.semaphore(name))

        arena = sb("arena", [P, ARENA])
        H = sb("hidden_sb", [P, TILES, D])
        wring = sb("weight_ring", [P, WSLOTS, WCOLS])
        rring = sb("row_ring", [P, RSLOTS, D])
        consts = sb("consts_sb", [P, CT_COLS])
        params = sb("params_sb", [P, PT_COLS])
        silc = sb("silu_cond", [P, 2 * KC * 4])
        modst = sb("mod_staged", [2, 2, 512])
        gnat = sb("gates_by_token", [P, TILES, 16])
        gcols = sb("gate_columns", [P, 64])
        small = sb("small", [P, 64])
        lamc = sb("lambda", [P, 4])
        newton = sb("newton", [P, 64])
        head_scores = sb("head_scores", [P, 256])
        left = sb("left", [P, 256])
        topv = sb("topv", [P, 2, 16])
        topi = sb("topi", [P, 2, 16], U32)
        topf = sb("topf", [P, 2, 16])
        cv = sb("cv", [P, 16])
        ci = sb("ci", [P, 16], U32)
        ab = sb("ab", [P, 2, 16], U32)
        abf = sb("abf", [P, 2, 16])
        eq = sb("eq", [P, 2, 16, 16])
        selv = sb("selv", [P, 2, 16])
        ef = sb("ef", [P, 16])
        idx = sb("idx", [P, 2, 16], U32)
        neg = sb("neg", [P, 1])
        ex = sb("ex", [P, 16])
        es = sb("es", [P, 1])
        gate = sb("gate", [P, 2, 16])
        dot = sb("dot", [P, SLOTS, GROUP])
        gel = sb("gel", [P, SLOTS, GROUP])
        wgt = sb("wgt", [P, SLOTS, GROUP])
        diag = sb("diag", [P, SLOTS, GROUP, P])
        modparts = diag[:, 0:2, :, :].rearrange("p s x c -> p (s x c)")
        bank = ctx.enter_context(nc.psum_tensor("banks", [P, 8, 512], F32))
        mods = nc.dram_tensor("mods", [LAYERS, 2 * NMOD, D], F32, kind="Internal").ap()

        sems = {e: sem(f"{e}_steps") for e in ("pe", "dve", "act")}
        consts_landed, params_landed, hidden_landed = sem("consts_landed"), sem("params_landed"), sem("hidden_landed")
        ctx2_landed, stored = sem("ctx2_landed"), sem("stored")
        w_landed = [sem(f"weights_landed{i}") for i in range(WSLOTS)]
        r_landed = [sem(f"row_landed{i}") for i in range(RSLOTS)]
        mods_stored = [sem(f"mods_stored{i}") for i in range(2)]
        keys_landed = sem("keys_landed")
        ring_landed = [sem(f"experts_landed{i}") for i in range(SLOTS)]
        slots_free, dots_done, diag_done = sem("slots_free"), sem("dots_done"), sem("diag_done")
        topk_done, head_copied, exp_done = sem("topk_done"), sem("head_copied"), sem("exp_done")

        st = Steps(sems, known)
        after, done = st.after, st.done

        def v(off, n):
            return arena[:, off:off + n]

        def v3(off, a, b):
            return arena[:, off:off + a * b].rearrange("p (a b) -> p a b", a=a)

        def v4(off, a, b, c):
            return arena[:, off:off + a * b * c].rearrange("p (a b c) -> p a b c", a=a, b=b)

        def const(name):
            o, n = CT[name]
            return consts[:, o:o + n]

        def par(name):
            o, n = PT_[name]
            return params[:, o:o + n]

        ident = const("ident")
        ring = arena[:, RING:RING + SLOTS * GROUP * 2 * D].rearrange("p (s x c) -> p s x c", s=SLOTS, x=GROUP)
        scores = v3(SCORES, TILES * PH + 1, 2 * NK)
        xT = v3(XT, KC, TOK)
        xnat = v3(XNAT, TILES, D)
        xn = v3(XN, TILES, D)
        mixT = v3(MIX_T, KC, TOK)
        xT2_of = [v3(XT2, KC, TOK)] + [v3(XT2_LATE, KC, 2 * P)] * 3
        qT_of = [v3(QT, 2 * PH, TOK)] + [v3(QT_LATE, 8, 2 * P)] * 3

        def bank3(b, a, n):
            return bank[:, b, 0:a * n].rearrange("p (a n) -> p a n", a=a)

        bank_of = {}

        def block_ap(n, k):
            cols = BLOCKS[n][1]
            return wring[:, n % WSLOTS, 0:cols].rearrange("p (k c) -> p k c", k=k)

        LT = {0: (0, 1, 2, 3), 1: (0, 1, 2, 3), 2: (0, 1, 2, 3), 3: LAT}

        block = ctx.enter_context(nc.Block())

        @block.sync
        def _(sp):
            sp.dma_start(params[:, :], A["params"]).then_inc(params_landed, 16)
            sp.dma_start(consts[:, :], A["consts"]).then_inc(consts_landed, 16)
            for n, (name, cols) in enumerate(BLOCKS):
                if n == 2:
                    sp.dma_start(H[:, :, :], A["hidden"]).then_inc(hidden_landed, 16)
                if n >= WSLOTS:
                    sp.wait_ge(*after("w", n - WSLOTS))
                if name[0] and name[1:] == ("wq", 0):
                    sp.wait_ge(*after("ring_room", name[0]))
                    sp.dma_start(v(KEYS_LATE, 2 * PH * NK), A["late_keys"][name[0] - 1]).then_inc(keys_landed, 16)
                sp.dma_start(wring[:, n % WSLOTS, 0:cols], A["weights"][n, :, 0:cols]).then_inc(w_landed[n % WSLOTS], 16)
            sp.wait_ge(*after("final_out"))
            sp.dma_start(A["out"], H[:, 2:4, :]).then_inc(stored, 16)
            sp.wait_ge(stored, 16)

        @block.gpsimd
        def _(pool):
            sent = [0]

            def rows_until(stop):
                while sent[0] < stop:
                    n = sent[0]
                    kind, *what = ROWS[n][1]
                    if n >= RSLOTS:
                        pool.wait_ge(*after("row", n - RSLOTS))
                    if kind == "mod":
                        l, s, m = what
                        for q in range(2):
                            pool.wait_ge(mods_stored[q], 16 * (l * NMOD + m + 1))
                        src = mods[l, s * NMOD + m:s * NMOD + m + 1, :]
                    else:
                        src = A["gains"][what[0]:what[0] + 1, :]
                    pool.dma_start(rring[:, n % RSLOTS, :], src.broadcast_to([P, D])).then_inc(r_landed[n % RSLOTS], 16)
                    sent[0] += 1

            for l in range(LAYERS):
                rows_until(1 + max(n for n, (name, _) in enumerate(ROWS) if name[0] == l))
                if l == 1:
                    pool.wait_ge(*after("xn", 1, 1))
                    pool.dma_start(H[:, 0:2, :], A["ctx2"]).then_inc(ctx2_landed, 16)
                if l == 0:
                    pool.wait_ge(*after("mm", l, "sc", TILES - 1, 3))
                else:
                    pool.wait_ge(*after("ring_room", l))
                for i in range(len(PEER_TILES[l])):
                    q0 = HEADS_BEFORE[l] + i * PH
                    with pool.Fori(0, PH // 2) as it:
                        for e in range(2):
                            pool.wait_ge(topk_done, it * 2 + (q0 + l + e + 1))
                            pool.nop(nofuse=True)
                            for j in range(GPH):
                                pool.wait_ge(slots_free, it * (2 * GPH) + (q0 * GPH + e * GPH + j + 1))
                                pool.nop(nofuse=True)
                                for x in range(GROUP):
                                    k = GROUP * j + x
                                    pool.indirect_dma_start(
                                        out=ring[:, j % SLOTS, x, :], out_offset=None, in_=A[f"uv{l}"],
                                        in_offset=bass.IndirectOffsetOnAxis(ap=idx[:, e, k:k + 1], axis=0),
                                    ).then_inc(ring_landed[j % SLOTS], 16)

        @block.tensor
        def _(pe):
            mm_ = nc.tensor.matmul
            free = {b: None for b in range(8)}
            turn = [0]
            seen = set()

            def new_bank(*key):
                b = turn[0] % 7
                turn[0] += 1
                if free[b] is not None:
                    pe.wait_ge(*after(*free[b]))
                free[b] = ("ev",) + key
                st.at[("bank",) + key] = b
                return b

            def weights(name, k):
                n = BLOCK_AT[name]
                if n not in seen:
                    seen.add(n)
                    pe.wait_ge(w_landed[n % WSLOTS], 16 * (n // WSLOTS + 1))
                return n, block_ap(n, k)

            def transposes(key, t, src, n=8, per=4):
                for half in range((n + per - 1) // per):
                    b = new_bank(*key, t, half)
                    m = min(per, n - half * per)
                    for k in range(m):
                        ins = nc.tensor.transpose(bank[:, b, k * P:(k + 1) * P],
                                                  src[:, (half * per + k) * P:(half * per + k + 1) * P], ident)
                    ins.then_inc(sems["pe"], done("pe", ("mm",) + key + (t, half)))

            def natural(l, name, tiles, src, k, width, cols=None, part=0):
                n, w = weights((l, name), k)
                c0, c1 = cols or (0, width)
                for t in tiles:
                    b = new_bank(l, name, t, part)
                    for kk in range(k):
                        ins = mm_(bank[:, b, 0:c1 - c0], src(kk, t), w[:, kk, c0:c1], start=kk == 0, stop=kk == k - 1)
                    ev = [("mm", l, name, t, part)]
                    if t == tiles[-1] and c1 == width:
                        ev.append(("w", n))
                    ins.then_inc(sems["pe"], done("pe", *ev))

            def feature(l, name, chunks, src, k, ncols, last=True):
                n, w = weights((l, *name) if isinstance(name, tuple) else (l, name), k)
                for c in range(chunks):
                    b = new_bank(l, name, c)
                    for kk in range(k):
                        ins = mm_(bank[:, b, 0:ncols], w[:, kk, c * P:(c + 1) * P], src(kk), start=kk == 0, stop=kk == k - 1)
                    ev = [("mm", l, name, c)]
                    if c == chunks - 1:
                        ev.append(("w", n))
                    ins.then_inc(sems["pe"], done("pe", *ev))

            def modulations(blocks):
                for kind, (l, nb) in mod_pieces(blocks):
                    if kind == "sum":
                        pe.wait_ge(*after("parts", l, nb))
                        b = new_bank("mod", l, nb)
                        mm_(bank[0:2, b, :], const("add4"), modparts[:, :], start=True, stop=True)\
                            .then_inc(sems["pe"], done("pe", ("mm", "mod", l, nb)))
                        yield
                        continue
                    n, w = weights((l, "mod", nb), KC)
                    mb = MOD_ORDER.index((l, nb))
                    if kind == "low" and mb:
                        pe.wait_ge(*after("parts", *MOD_ORDER[mb - 1]))
                    for j in range(4):
                        kk = j + (4 if kind == "high" else 0)
                        cond = silc[:, 4 * kk + 2 * (l // 2):][:, 0:32]
                        mm_(bank[32 * j:32 * j + 32, 7, :], cond, w[:, kk, :], start=kind == "low", stop=False, skip_group_check=True)
                    if kind == "high":
                        for j in range(4):
                            ch = PT_["mod_b"][0] + l * MODC + 4 * nb + j
                            ins = mm_(bank[32 * j:32 * j + 32, 7, j * P:(j + 1) * P], params[:, ch:ch + 1].broadcast_to([P, 32]), ident,
                                      start=False, stop=True, skip_group_check=True)
                        ins.then_inc(sems["pe"], done("pe", ("mm", "parts", l, nb), ("w", n)))
                    yield

            def take(stream, n):
                for _ in range(n):
                    next(stream, None)

            pe.wait_ge(consts_landed, 16)
            pe.wait_ge(*after("silc"))
            take(modulations(MODS_FIRST), len(mod_pieces(MODS_FIRST)))

            for l in range(LAYERS):
                tiles = LT[l]
                for t in tiles:
                    pe.wait_ge(*after("xn", l, t))
                    transposes((l, "xT"), t, xn[:, t, :])
                pe.wait_ge(*after("ev", l, "xT", tiles[-1], 0))
                pe.wait_ge(*after("ev", l, "xT", tiles[-1], 1))
                xs = lambda kk, t: xT[:, kk, t * P:(t + 1) * P]
                if l == 0:
                    feature(0, "qk", 4, lambda kk: xT[:, kk, :], KC, TOK)
                    n, w = weights((0, "gates"), KC)
                    b = new_bank(0, "gnat")
                    for t in tiles:
                        for kk in range(KC):
                            ins = mm_(bank[:, b, t * 16:t * 16 + 16], xT[:, kk, t * P:(t + 1) * P], w[:, kk, :], start=kk == 0, stop=kk == KC - 1)
                    ins.then_inc(sems["pe"], done("pe", ("mm", 0, "gnat"), ("w", n)))
                    natural(0, "v", tiles, xs, KC, 512)
                    pe.wait_ge(*after("ev", 0, "gnat"))
                    for g in range(4):
                        b = new_bank(0, "gates", g)
                        for t in tiles:
                            ins = nc.tensor.transpose(bank[0:4, b, t * P:(t + 1) * P], gnat[:, t, 4 * g:4 * g + 4], ident)
                        ins.then_inc(sems["pe"], done("pe", ("mm", 0, "gates", g)))
                    for name in ("o", "dq", "dk", "dv"):
                        natural(0, name, tiles, xs, KC, 512)
                    dqn = xn
                    for t in tiles:
                        pe.wait_ge(*after("roped", t))
                        transposes((0, "dqkT"), t, dqn[:, t, :])
                    pe.wait_ge(*after("gate_rows"))
                    b = new_bank(0, "gcols")
                    i = 0
                    for q in range(2):
                        for d in range(2):
                            rows_ = arena[0:4, (GW + 3072 if q else GW + 2048) + d * 512:][:, 0:512]
                            for t in range(4):
                                ins = nc.tensor.transpose(bank[:, b, i * 4:i * 4 + 4], rows_[:, t * P:(t + 1) * P], ident[0:4, 0:4])
                                i += 1
                    ins.then_inc(sems["pe"], done("pe", ("mm", 0, "gcols")))
                    qk = v3(QKT, 4, TOK)
                    vml = v4(VML, 4, 4, 129)
                    mrow = arena[0:4, MROW:MROW + 1024].rearrange("p (a b) -> p a b", a=2)
                    selr = consts[0:4, CT["sel"][0]:CT["sel"][0] + 512].rearrange("p (h c) -> p h c", h=4)
                    pe.wait_ge(*after("qkT", 3))
                    pe.wait_ge(*after("vml_ones"))
                    pe.wait_ge(*after("ev", 0, "v", 3, 0))
                    beside = modulations(MODS_BESIDE[0])
                    for h in range(4):
                        o = 64 * (h % 2)
                        for s in range(4):
                            b = new_bank(0, "A", h, s)
                            mm_(bank[:, b, :], qk[o:o + 64, 2 + h // 2, s * P:(s + 1) * P], qk[o:o + 64, h // 2, :], start=True, stop=True)\
                                .then_inc(sems["pe"], done("pe", ("mm", 0, "A", h, s)))
                        for d in range(2):
                            b = new_bank(0, "M", h, d)
                            mm_(bank[:, b, :], selr[:, h, :], mrow[:, d, :], start=True, stop=True)\
                                .then_inc(sems["pe"], done("pe", ("mm", 0, "M", h, d)))
                        for d in range(2):
                            wt = v3(EW1 if d else EW0, 4, TOK)
                            take(beside, MOD_SHARE[0][2 * h + d])
                            pe.wait_ge(*after("WT", h, d))
                            for tp in range(2):
                                b = new_bank(0, "N", h, d, tp)
                                for t in (2 * tp, 2 * tp + 1):
                                    src = SOURCES[d][t]
                                    for s in src:
                                        ins = mm_(bank[:, b, (t % 2) * 129:(t % 2) * 129 + 129], wt[:, s, t * P:(t + 1) * P],
                                                  vml[:, s, h, :], start=s == src[0], stop=s == src[-1])
                                ins.then_inc(sems["pe"], done("pe", ("mm", 0, "N", h, d, tp)))
                    dqT, dkT = v3(DQT, 4, TOK), v3(DKT, 4, TOK)
                    dv = v3(DV, 4, 512)
                    pe.wait_ge(*after("ev", 0, "dqkT", 3, 0))
                    pe.wait_ge(*after("ev", 0, "dqkT", 3, 1))
                    pe.wait_ge(*after("ev", 0, "dv", 3, 0))
                    for step in range(16 + 4):
                        if step < 16:
                            i = step
                            t, h = i // 4, i % 4
                            nkt = 2 if t < 2 else 4
                            for m in range(2):
                                b = new_bank(0, "S", t, h, m)
                                mm_(bank[:, b, 0:nkt * P], dqT[64 * m:64 * m + 64, h, t * P:(t + 1) * P],
                                    dkT[64 * m:64 * m + 64, h, 0:nkt * P], start=True, stop=True)\
                                    .then_inc(sems["pe"], done("pe", ("mm", 0, "S", t, h, m)))
                        if step < 13:
                            take(beside, MOD_SHARE[0][8 + step])
                        if 0 <= step - 3 < 16:
                            i = step - 3
                            nkt = 2 if i < 8 else 4
                            pe.wait_ge(*after("Pr", 0, i))
                            b = new_bank(0, "PT", i)
                            pr = v(ATS + (i % 3) * 1024, 512)
                            for kk in range(nkt):
                                ins = nc.tensor.transpose(bank[:, b, kk * P:(kk + 1) * P], pr[:, kk * P:(kk + 1) * P], ident)
                            ins.then_inc(sems["pe"], done("pe", ("mm", 0, "PT", i)))
                        if 0 <= step - 4 < 16:
                            i = step - 4
                            h = i % 4
                            nkt = 2 if i < 8 else 4
                            b = new_bank(0, "O", i)
                            pe.wait_ge(*after("ev", 0, "PT", i))
                            prT = v3(ATS + 3072 + (i % 2) * 512, 4, P)
                            for kk in range(nkt):
                                ins = mm_(bank[:, b, 0:P], prT[:, kk, :], dv[:, kk, h * P:(h + 1) * P], start=kk == 0, stop=kk == nkt - 1)
                            ins.then_inc(sems["pe"], done("pe", ("mm", 0, "O", i)))
                    assert next(beside, None) is None
                    mix_off = MIX
                if l == 1:
                    natural(1, "q0", LAT, xs, KC, 512)
                    natural(1, "q1", LAT, xs, KC, 512)
                    natural(1, "kv", tiles, xs, KC, 512)
                    qn, kn = v3(L1_QN, 2, 1024), v3(L1_KN, 4, 256)
                    for t in LAT:
                        pe.wait_ge(*after("q_roped", t))
                        transposes((1, "qT"), t, qn[:, t - 2, :])
                    for t in tiles:
                        pe.wait_ge(*after("k_roped", t))
                        transposes((1, "kT"), t, kn[:, t, :], n=2)
                    qT1, kT1, v1 = v3(L1_QT, 8, 256), v3(L1_KT, 2, TOK), v3(L1_V, 4, 256)
                    pe.wait_ge(*after("ev", 1, "qT", 3, 1))
                    pe.wait_ge(*after("ev", 1, "qT", 3, 0))
                    pe.wait_ge(*after("ev", 1, "kT", 3, 0))
                    beside = modulations(MODS_BESIDE[1])
                    for step in range(32 + 3):
                        if step < 32:
                            i = step
                            t, c, sd = i // 16, (i % 16) // 2, i % 2
                            b = new_bank(1, "S", i)
                            mm_(bank[:, b, :], qT1[64 * sd:64 * sd + 64, c, t * P:(t + 1) * P], kT1[64 * sd:64 * sd + 64, c // 4, :],
                                start=True, stop=True).then_inc(sems["pe"], done("pe", ("mm", 1, "S", i)))
                            take(beside, MOD_SHARE[1][step])
                        if 0 <= step - 2 < 32:
                            i = step - 2
                            pe.wait_ge(*after("ev", 1, "S", i))
                            b = new_bank(1, "PT", i)
                            pr = v(L1_P + (i % 2) * 512, 512)
                            for kk in range(4):
                                ins = nc.tensor.transpose(bank[:, b, kk * P:(kk + 1) * P], pr[:, kk * P:(kk + 1) * P], ident)
                            ins.then_inc(sems["pe"], done("pe", ("mm", 1, "PT", i)))
                        if 0 <= step - 3 < 32:
                            i = step - 3
                            c, sd = (i % 16) // 2, i % 2
                            kvh = 2 * (c // 4) + sd
                            b = new_bank(1, "O", i)
                            pe.wait_ge(*after("ev", 1, "PT", i))
                            prT = v3(L1_PT + (i % 2) * 512, 4, P)
                            for kk in range(4):
                                ins = mm_(bank[:, b, 0:64], prT[:, kk, :], v1[:, kk, kvh * 64:kvh * 64 + 64], start=kk == 0, stop=kk == 3)
                            ins.then_inc(sems["pe"], done("pe", ("mm", 1, "O", i)))
                    assert next(beside, None) is None
                    mix_off = MIX
                if l == 2:
                    natural(2, "zq", LAT, xs, KC, 384)
                    natural(2, "zkv", tiles, xs, KC, 320)
                    z = v3(L2_Z, 4, 704)
                    for t in tiles:
                        if t in LAT:
                            pe.wait_ge(*after("zq_n", t))
                            transposes((2, "cqT"), t, z[:, t, 0:384], n=3)
                        pe.wait_ge(*after("zkv_n", t))
                        transposes((2, "ckvT"), t, z[:, t, 384:640], n=2)
                        pe.wait_ge(*after("kr", t))
                        transposes((2, "krT"), t, v3(L2_QR, 4, P)[:, t, :], n=1)
                    cqT, ckvT = v3(L2_CQT, 3, 256), v3(L2_CKVT, 2, TOK)
                    for t in tiles:
                        if t in LAT:
                            pe.wait_ge(*after("ev", 2, "cqT", t, 0))
                        pe.wait_ge(*after("ev", 2, "ckvT", t, 0))
                        pe.wait_ge(*after("ev", 2, "krT", t, 0))
                    feature(2, "uqn", 8, lambda kk: cqT[:, kk, :], 3, 256)
                    natural(2, "uqr", LAT, lambda kk, t: cqT[:, kk, (t - 2) * P:(t - 1) * P], 3, 512)
                    feature(2, "ukn", 8, lambda kk: ckvT[:, kk, :], 2, TOK)
                    for part in range(2):
                        natural(2, "uv", tiles, lambda kk, t: ckvT[:, kk, t * P:(t + 1) * P], 2, 1024,
                                cols=(part * 512, part * 512 + 512), part=part)
                    qr = v3(L2_QR, 2, 512)
                    for t in LAT:
                        pe.wait_ge(*after("qr_roped", t))
                        transposes((2, "qrT"), t, qr[:, t - 2, :], n=4)
                    qnT, qrT, knT, krT, v2 = (v3(L2_QNT, 8, 256), v3(L2_QRT, 4, 256), v3(L2_KNT, 8, TOK),
                                              v(L2_KRT, TOK), v3(L2_V, 4, 1024))
                    pe.wait_ge(*after("ev", 2, "qrT", 3, 0))
                    for ev in (("uqn", 6), ("uqn", 7), ("ukn", 6), ("ukn", 7)):
                        pe.wait_ge(*after("ev", 2, *ev))
                    for t_ in tiles:
                        pe.wait_ge(*after("ev", 2, "uv", t_, 1))
                        pe.wait_ge(*after("ev", 2, "uv", t_, 0))
                    beside = modulations(MODS_BESIDE[2])
                    for step in range(16 + 3):
                        if step < 16:
                            i = step
                            t, h = i // 8, i % 8
                            b = new_bank(2, "S", i)
                            o = 64 * (h % 2)
                            mm_(bank[:, b, :], qnT[:, h, t * P:(t + 1) * P], knT[:, h, :], start=True, stop=False)
                            mm_(bank[:, b, :], qrT[o:o + 64, h // 2, t * P:(t + 1) * P], krT[o:o + 64, :], start=False, stop=True)\
                                .then_inc(sems["pe"], done("pe", ("mm", 2, "S", i)))
                            take(beside, MOD_SHARE[2][step])
                        if 0 <= step - 2 < 16:
                            i = step - 2
                            pe.wait_ge(*after("ev", 2, "S", i))
                            b = new_bank(2, "PT", i)
                            pr = v(L2_P + (i % 2) * 512, 512)
                            for kk in range(4):
                                ins = nc.tensor.transpose(bank[:, b, kk * P:(kk + 1) * P], pr[:, kk * P:(kk + 1) * P], ident)
                            ins.then_inc(sems["pe"], done("pe", ("mm", 2, "PT", i)))
                        if 0 <= step - 3 < 16:
                            i = step - 3
                            h = i % 8
                            b = new_bank(2, "O", i)
                            pe.wait_ge(*after("ev", 2, "PT", i))
                            prT = v3(L2_PT + (i % 2) * 512, 4, P)
                            for kk in range(4):
                                ins = mm_(bank[:, b, 0:P], prT[:, kk, :], v2[:, kk, h * P:(h + 1) * P], start=kk == 0, stop=kk == 3)
                            ins.then_inc(sems["pe"], done("pe", ("mm", 2, "O", i)))
                    assert next(beside, None) is None
                    mix_off = L2_MIX
                out_tiles = PEER_TILES[l]
                xT2, qT = xT2_of[l], qT_of[l]
                if l < 3:
                    m0 = 0 if l == 0 else 2
                    mixv = v3(mix_off, len(out_tiles), D)
                    for t in out_tiles:
                        pe.wait_ge(*after("mix", l, t))
                        transposes((l, "mT"), t, mixv[:, t - m0, :])
                    for t in out_tiles:
                        pe.wait_ge(*after("ev", l, "mT", t, 0))
                        pe.wait_ge(*after("ev", l, "mT", t, 1))
                    ms = lambda kk, t: mixT[:, kk, t * P:(t + 1) * P]
                else:
                    for j in range(2):
                        natural(3, f"in{j}", LAT, xs, KC, 512)
                    z3, pT, yT = v3(L3_Z, 2, 1024), v3(L3_POOLT, 8, 256), v3(L3_YT, 8, 256)
                    n, w = weights((3, "band"), 2)
                    for t in LAT:
                        for j in range(2):
                            pe.wait_ge(*after("ev", 3, f"in{j}", t, 0))
                    for c in range(8):
                        b = new_bank(3, "pool", c)
                        for kk in range(2):
                            ins = mm_(bank[:, b, 0:256], z3[:, kk, c * P:(c + 1) * P], w[:, kk, (c // 2) * 256:(c // 2) * 256 + 256],
                                      start=kk == 0, stop=kk == 1)
                        ev = [("mm", 3, "pool", c)] + ([("w", n)] if c == 7 else [])
                        ins.then_inc(sems["pe"], done("pe", *ev))
                    n, w = weights((3, "grp"), 8)
                    pe.wait_ge(*after("ev", 3, "pool", 6))
                    pe.wait_ge(*after("ev", 3, "pool", 7))
                    for c in range(8):
                        b = new_bank(3, "yT", c)
                        g = c // 2
                        for kk in range(2):
                            ins = mm_(bank[:, b, 0:256], w[:, 2 * g + kk, (c % 2) * P:(c % 2) * P + P], pT[:, 2 * g + kk, :],
                                      start=kk == 0, stop=kk == 1)
                        ev = [("mm", 3, "yT", c)] + ([("w", n)] if c == 7 else [])
                        ins.then_inc(sems["pe"], done("pe", *ev))
                    pe.wait_ge(*after("ev", 3, "yT", 6))
                    pe.wait_ge(*after("ev", 3, "yT", 7))
                    ms = lambda kk, t: yT[:, kk, (t - 2) * P:(t - 1) * P]
                for j in range(2):
                    natural(l, f"out{j}", out_tiles, ms, KC, 512)
                for t in out_tiles:
                    pe.wait_ge(*after("xnat", l, t))
                    transposes((l, "xT2"), t, xnat[:, t - out_tiles[0], :])
                for t in out_tiles:
                    pe.wait_ge(*after("ev", l, "xT2", t, 0))
                    pe.wait_ge(*after("ev", l, "xT2", t, 1))
                ntok = len(out_tiles) * P
                def key_scores(i, j, w):
                    b = new_bank(l, "sc", i, j)
                    for q in range(4):
                        hp = 4 * j + q
                        ins = mm_(bank[:, b, q * P:(q + 1) * P], qT[:, hp % qT.shape[1], i * P:(i + 1) * P], w[:, hp, :],
                                  start=True, stop=True)
                    return ins, [("mm", l, "sc", i, j)]

                for j in range(4):
                    n, w = weights((l, "wq", j), KC)
                    for c in range(4):
                        b = new_bank(l, "q", 4 * j + c)
                        for kk in range(KC):
                            ins = mm_(bank[:, b, 0:ntok], w[:, kk, c * P:(c + 1) * P], xT2[:, kk, 0:ntok], start=kk == 0, stop=kk == KC - 1)
                        ev = [("mm", l, "q", 4 * j + c)] + ([("w", n)] if c == 3 else [])
                        ins.then_inc(sems["pe"], done("pe", *ev))
                    if l:
                        if j == 0:
                            pe.wait_ge(keys_landed, 16 * l)
                        for i in range(2):
                            for q in range(4):
                                pe.wait_ge(*after("ev", l, "q", 4 * j + q))
                            ins, ev = key_scores(i, j, v3(KEYS_LATE, 2 * PH, NK))
                            ins.then_inc(sems["pe"], done("pe", *ev))
                if l == 0:
                    for j in range(4):
                        for q in range(4):
                            pe.wait_ge(*after("ev", l, "q", 4 * j + q))
                    n, w = weights((0, "keys"), 16)
                    for i in range(TILES):
                        for j in range(4):
                            ins, ev = key_scores(i, j, w)
                            if j == 3 and i == TILES - 1:
                                ev.append(("w", n))
                            ins.then_inc(sems["pe"], done("pe", *ev))
                for i in range(len(out_tiles)):
                    q0 = HEADS_BEFORE[l] + i * PH
                    yb = 2 * (i % 2)
                    for hf in range(2):
                        pe.wait_ge(*after(*free[yb + hf]))
                        free[yb + hf] = ("y_taken", l, i)
                        ins = mm_(bank[:, yb + hf, :], ident, const("zero"), start=True, stop=False, skip_group_check=True)
                    if l == 0 and i == 0:
                        ins.then_inc(slots_free, SLOTS)
                    with pe.Fori(0, PH // 2) as it:
                        for e in range(2):
                            for j in range(GPH):
                                pe.wait_ge(diag_done, it * (2 * GPH) + (q0 * GPH + e * GPH + j + 1))
                                for x in range(GROUP):
                                    for hf in range(2):
                                        ins = mm_(bank[:, yb + hf, :], diag[:, j % SLOTS, x, :],
                                                  ring[:, j % SLOTS, x, D + hf * 512:D + hf * 512 + 512],
                                                  start=False, stop=True, skip_group_check=True)
                                ins.then_inc(slots_free, 1)

        @block.scalar
        def _(act):
            a = nc.scalar
            AF = a.activation

            def b_(*key):
                act.wait_ge(*after("mm", *key))
                return known.get(("bank",) + key, 0)

            def ev(ins, *key):
                ins.then_inc(sems["act"], done("act", ("ev",) + key))

            def copy_T(key, t, dst, half, n=4):
                b = b_(*key, t, half)
                ev(a.copy(dst, bank3(b, n, P)), *key, t, half)

            act.wait_ge(params_landed, 16)
            AF(silc[:, :], par("cond"), ACT.Silu).then_inc(sems["act"], done("act", ("silc",)))

            def take_mod(kind, lb):
                l, nb = lb
                mb = MOD_ORDER.index((l, nb))
                if kind == "high":
                    act.wait_ge(*after("mm", "parts", l, nb))
                    a.copy(modparts[:, :], bank[:, 7, :]).then_inc(sems["act"], done("act", ("parts", l, nb)))
                if kind == "sum":
                    b = b_("mod", l, nb)
                    if mb >= 2:
                        act.wait_ge(mods_stored[mb % 2], 16 * (mb // 2))
                    ev(a.copy(modst[:, mb % 2, :], bank[0:2, b, :]), "mod", l, nb)
                    act.wait_ge(*after("ev", "mod", l, nb))
                    dst = mods[l, :, :].rearrange("(s m) d -> s (m d)", s=2)[:, nb * 512:(nb + 1) * 512]
                    act.dma_start(dst, modst[:, mb % 2, :]).then_inc(mods_stored[mb % 2], 16)

            for kind, m in mod_pieces(MODS_FIRST):
                take_mod(kind, m)
            act.wait_ge(*after("lam_dots"))
            AF(lamc[:, 0:2], lamc[:, 0:2], ACT.Exp).then_inc(sems["act"], done("act", ("lam_exp",)))
            for l in range(LAYERS):
                tiles = LT[l]
                for t in tiles:
                    copy_T((l, "xT"), t, xT[:, 0:4, t * P:(t + 1) * P], 0)
                if l == 0:
                    raw = v4(RAW, 4, 2, 258)
                    qk = v3(QKT, 4, TOK)
                    for c in range(4):
                        act.wait_ge(*after("conv", c))
                        AF(qk[:, c, :], qk[:, c, :], ACT.Silu).then_inc(sems["act"], done("act", ("qkT", c)))
                    vml = v4(VML, 4, 4, 129)
                    for t in tiles:
                        b = b_(0, "v", t, 0)
                        ev(a.copy(vml[:, t, :, 0:128], bank3(b, 4, P)), 0, "v", t, 0)
                    tmp = arena[0:4, GW + 2048:GW + 3072]
                    act.wait_ge(*after("absz"))
                    AF(tmp, tmp, ACT.Exp, scale=-1.0)
                    act.drain()
                    AF(tmp, tmp, ACT.Ln, bias=1.0).then_inc(sems["act"], done("act", ("softplus",)))
                    for t in tiles:
                        b = b_(0, "o", t, 0)
                        ev(AF(v(OSIG + t * 512, 512), bank[:, b, :], ACT.Sigmoid), 0, "o", t, 0)
                    for t in tiles:
                        b = b_(0, "dv", t, 0)
                        ev(a.copy(v(DV + t * 512, 512), bank[:, b, :]), 0, "dv", t, 0)
                    for t in tiles:
                        copy_T((0, "dqkT"), t, v3(DQT, 4, TOK)[:, :, t * P:(t + 1) * P], 0)
                    act.wait_ge(*after("m_rows"))
                    AF(arena[0:4, GW + 3072:GW + 4096], arena[0:4, GW + 1024:GW + 2048], ACT.Exp, scale=-1.0)\
                        .then_inc(sems["act"], done("act", ("floor_rows",)))
                    ats = v3(ATS, 4, TOK)
                    for h in range(4):
                        for s in range(4):
                            b = b_(0, "A", h, s)
                            if s == 0:
                                if h:
                                    act.wait_ge(*after("WT", h - 1, 1))
                                else:
                                    act.wait_ge(*after("ev", 0, "gcols"))
                            ev(AF(ats[:, s, :], bank[:, b, :], ACT.Copy, scale=SCALE64), 0, "A", h, s)
                        for d in range(2):
                            wt = v3(EW1 if d else EW0, 4, TOK)
                            dm = v3(DMASK, 4, P)
                            b = b_(0, "M", h, d)
                            act.wait_ge(*after("dmask", h, d))
                            if h:
                                act.wait_ge(*after("mm", 0, "N", h - 1, d, 1))
                            for s in range(4):
                                bias = gcols[:, (d * 4 + s) * 4 + h:(d * 4 + s) * 4 + h + 1]
                                ins = AF(wt[:, s, s * P:(s + 1) * P], dm[:, s, :], ACT.Exp, bias=bias)
                                for t0, t1 in OFF_DIAGONAL[d][s]:
                                    ins = AF(wt[:, s, t0 * P:t1 * P], bank[:, b, t0 * P:t1 * P], ACT.Exp, bias=bias)
                            ins.then_inc(sems["act"], done("act", ("ev", 0, "M", h, d), ("E", h, d)))
                            for piece in mod_ready(0, 2 * h + d):
                                take_mod(*piece)
                    for step in range(16 + 4):
                        if 0 <= step - 1 < 16:
                            i = step - 1
                            t, h = i // 4, i % 4
                            nk = 256 if t < 2 else 512
                            act.wait_ge(*after("smax", 0, i))
                            for m in range(2):
                                b = b_(0, "S", t, h, m)
                                c = 8 * (i % 4) + m
                                ev(AF(v(ATS + (i % 3) * 1024 + m * 512, nk), bank[:, b, 0:nk], ACT.Exp, bias=small[:, c:c + 1],
                                      scale=SCALE64, accum_out=small[:, c + 2:c + 3]), 0, "S", t, h, m)
                        if step < 13:
                            for piece in mod_ready(0, 8 + step):
                                take_mod(*piece)
                        if 0 <= step - 3 < 16:
                            i = step - 3
                            nk = 256 if i < 8 else 512
                            b = b_(0, "PT", i)
                            ev(a.copy(v(ATS + 3072 + (i % 2) * 512, nk), bank[:, b, 0:nk]), 0, "PT", i)
                        if 0 <= step - 4 < 16:
                            i = step - 4
                            t, h = i // 4, i % 4
                            b = b_(0, "O", i)
                            ev(a.copy(v3(MIX, 4, D)[:, t, 512 + h * P:512 + (h + 1) * P], bank[:, b, 0:P]), 0, "O", i)
                if l == 1:
                    for t in tiles:
                        b = b_(1, "kv", t, 0)
                        act.wait_ge(*after("k_roped", t))
                        ev(a.copy(v3(L1_V, 4, 256)[:, t, :], bank[:, b, 256:512]), 1, "kv", t, 0)
                    for t in LAT:
                        copy_T((1, "qT"), t, v3(L1_QT, 8, 256)[:, 0:4, (t - 2) * P:(t - 1) * P], 0)
                    for t in tiles:
                        copy_T((1, "kT"), t, v3(L1_KT, 2, TOK)[:, :, t * P:(t + 1) * P], 0, n=2)

                    for step in range(32 + 3):
                        if 0 <= step - 1 < 32:
                            i = step - 1
                            b = b_(1, "S", i)
                            act.wait_ge(*after("smax", 1, i))
                            c = 8 * (i % 4)
                            if i >= 2:
                                act.wait_ge(*after("mm", 1, "PT", i - 2))
                            AF(v(L1_P + (i % 2) * 512, 512), bank[:, b, :], ACT.Exp, bias=small[:, c:c + 1], scale=SCALE64,
                               accum_out=small[:, c + 1:c + 2])
                            hq = head_of(i)
                            ev(AF(small[:, c + 2:c + 3], par("sink")[:, hq:hq + 1], ACT.Exp, bias=small[:, c:c + 1]), 1, "S", i)
                        if step < 32:
                            for piece in mod_ready(1, step):
                                take_mod(*piece)
                        if 0 <= step - 2 < 32:
                            i = step - 2
                            b = b_(1, "PT", i)
                            ev(a.copy(v(L1_PT + (i % 2) * 512, 512), bank[:, b, :]), 1, "PT", i)
                if l == 2:
                    for c in range(8):
                        if c % 2 == 0:
                            b = b_(2, "uqn", c)
                            ev(a.copy(v3(L2_QNT, 8, 256)[:, c, :], bank[:, b, 0:256]), 2, "uqn", c)
                    for c in range(8):
                        if c % 2 == 0:
                            b = b_(2, "ukn", c)
                            ev(a.copy(v3(L2_KNT, 8, TOK)[:, c, :], bank[:, b, :]), 2, "ukn", c)
                    for part in range(2):
                        for t in tiles:
                            if t % 2 == 0:
                                b = b_(2, "uv", t, part)
                                ev(a.copy(v3(L2_V, 4, 1024)[:, t, part * 512:part * 512 + 512], bank[:, b, :]), 2, "uv", t, part)

                    for step in range(16 + 3):
                        if 0 <= step - 1 < 16:
                            i = step - 1
                            b = b_(2, "S", i)
                            act.wait_ge(*after("smax", 2, i))
                            c = 8 * (i % 4)
                            if i >= 2:
                                act.wait_ge(*after("mm", 2, "PT", i - 2))
                            ev(AF(v(L2_P + (i % 2) * 512, 512), bank[:, b, :], ACT.Exp, bias=small[:, c:c + 1], scale=SCALE_MLA,
                                  accum_out=small[:, c + 1:c + 2]), 2, "S", i)
                        if step < 16:
                            for piece in mod_ready(2, step):
                                take_mod(*piece)
                        if 0 <= step - 2 < 16:
                            i = step - 2
                            b = b_(2, "PT", i)
                            ev(a.copy(v(L2_PT + (i % 2) * 512, 512), bank[:, b, :]), 2, "PT", i)
                if l == 3:
                    for t in LAT:
                        b = b_(3, "in0", t, 0)
                        ev(a.copy(v3(L3_Z, 2, 1024)[:, t - 2, 0:512], bank[:, b, :]), 3, "in0", t, 0)
                    for c in range(0, 8, 2):
                        b = b_(3, "pool", c)
                        ev(a.copy(v3(L3_POOLT, 8, 256)[:, c, :], bank[:, b, 0:256]), 3, "pool", c)
                    for c in range(0, 8, 2):
                        b = b_(3, "yT", c)
                        ev(AF(v3(L3_YT, 8, 256)[:, c, :], bank[:, b, 0:256], ACT.Copy, scale=par("pool_scale")[:, c:c + 1]), 3, "yT", c)
                out_tiles = PEER_TILES[l]
                xT2, qT = xT2_of[l], qT_of[l]
                if l < 3:
                    for t in out_tiles:
                        copy_T((l, "mT"), t, mixT[:, 0:4, t * P:(t + 1) * P], 0)
                t0 = out_tiles[0]
                for t in out_tiles:
                    copy_T((l, "xT2"), t, xT2[:, 0:4, (t - t0) * P:(t - t0 + 1) * P], 0)
                ntok = len(out_tiles) * P
                def take_queries(j):
                    for c in (4 * j, 4 * j + 2):
                        b = b_(l, "q", c)
                        ev(a.copy(qT[:, c % qT.shape[1], 0:ntok], bank[:, b, 0:ntok]), l, "q", c)

                def take_scores(i, j):
                    b = b_(l, "sc", i, j)
                    ev(a.copy(scores[:, i * PH + 2 * j:i * PH + 2 * j + 2, :].rearrange("p a b -> p (a b)"), bank[:, b, :]), l, "sc", i, j)

                def exps(wait):
                    act.wait_ge(topk_done, wait)
                    act.nop(nofuse=True)
                    AF(ex[:, :], cv[:, :], ACT.Exp, bias=neg[:, :], accum_out=es[:, :]).then_inc(exp_done, 1)

                def first_head():
                    act.wait_ge(*after("ev", l, "sc", 0, 0))
                    a.copy(head_scores[:, :], scores[:, 0, :]).then_inc(head_copied, 1)

                k0 = HEADS_BEFORE[l] + l
                if l == 0:
                    for j in range(4):
                        take_queries(j)
                    for i in range(TILES):
                        for j in (0, 2):
                            take_scores(i, j)
                            if (i, j) == (0, 0):
                                first_head()
                else:
                    for j in range(4):
                        take_queries(j)
                        take_scores(0, j)
                        if j == 0:
                            first_head()
                exps(k0 + 1)

                for i in range(len(out_tiles)):
                    if i == 0:
                        act.wait_ge(*after("ev", l, "sc", len(out_tiles) - 1, 3))
                        act.wait_ge(*after("pad_scores", l))
                    q0 = HEADS_BEFORE[l] + i * PH
                    with act.Fori(0, PH // 2) as it:
                        for e in range(2):
                            act.wait_ge(topk_done, it * 2 + (q0 + l + e + 1))
                            act.nop(nofuse=True)
                            a.copy(head_scores[:, :], scores[:, ds(it * 2 + (i * PH + e + 1), 1), :].rearrange("p a b -> p (a b)"))\
                                .then_inc(head_copied, 1)
                            for j in range(GPH):
                                s = j % SLOTS
                                act.wait_ge(dots_done, it * (2 * GPH) + (q0 * GPH + e * GPH + j + 1))
                                act.nop(nofuse=True)
                                AF(gel[:, s, :], dot[:, s, :], ACT.Gelu)
                                act.drain()
                                for x in range(GROUP):
                                    AF(wgt[:, s, x:x + 1], gel[:, s, x:x + 1], ACT.Copy, scale=gate[:, e, GROUP * j + x:GROUP * j + x + 1])
                                act.drain()
                                for x in range(GROUP):
                                    ins = AF(diag[:, s, x, :], ident, ACT.Copy, scale=wgt[:, s, x:x + 1])
                                ins.then_inc(diag_done, 1)
                                if j == 1:
                                    exps(it * 2 + (q0 + l + e + 2))

        @block.vector
        def _(dve):
            V = nc.vector

            def b_(*key):
                dve.wait_ge(*after("mm", *key))
                return known.get(("bank",) + key, 0)

            def ev(ins, *key, more=()):
                ins.then_inc(sems["dve"], done("dve", ("ev",) + key, *more))

            def sig(ins, *events):
                ins.then_inc(sems["dve"], done("dve", *events))

            def row(l, name, s):
                n = ROW_AT[(l, name, s)]
                dve.wait_ge(r_landed[n % RSLOTS], 16 * (n // RSLOTS + 1))
                return n, rring[:, n % RSLOTS, :]

            def squares(src, sq, ss):
                V.tensor_tensor_reduce(out=sq, in0=src, in1=src, scale=1.0, scalar=0.0, op0=ALU.mult, op1=ALU.add, accum_out=ss)

            def rsqrt(x, scale, eps):
                n = x.shape[-1]
                y, t_ = newton[:, 0:n], newton[:, 32:32 + n]
                dve.drain()
                V.tensor_scalar(x, x, scale, eps, ALU.mult, ALU.add)
                dve.drain()
                V.tensor_scalar(t_.bitcast(U32), x.bitcast(U32), 1, None, ALU.logical_shift_right)
                dve.drain()
                V.tensor_scalar(y.bitcast(U32), t_.bitcast(U32), -1.0, float(0x5F3759DF), ALU.mult, ALU.add)
                dve.drain()
                for _ in range(3):
                    V.scalar_tensor_tensor(out=t_, in0=y, scalar=-0.5, in1=y, op0=ALU.mult, op1=ALU.mult)
                    dve.drain()
                    V.tensor_tensor(t_, t_, x, ALU.mult)
                    dve.drain()
                    V.scalar_tensor_tensor(out=y, in0=t_, scalar=1.5, in1=y, op0=ALU.add, op1=ALU.mult)
                    dve.drain()
                V.tensor_copy(x, y)
                dve.drain()

            def modulated(l, tiles, s, names, dst, event, norm, off=0):
                g_, sc_, sh_ = names
                rows_ = []
                if norm:
                    ng, g = row(l, g_, s)
                    rows_.append(ng)
                nsc, sc = row(l, sc_, s)
                nsh, sh = row(l, sh_, s)
                rows_ += [nsc, nsh]
                if norm:
                    V.scalar_tensor_tensor(out=sc, in0=sc, scalar=1.0, in1=g, op0=ALU.add, op1=ALU.mult)
                else:
                    V.tensor_scalar(sc, sc, 1.0, None, ALU.add)
                dve.drain()
                if norm:
                    for t in tiles:
                        squares(H[:, t, :], dst[:, t - off, :], small[:, 32 + t:33 + t])
                    rsqrt(small[:, 32 + tiles[0]:33 + tiles[-1]], 1.0 / D, EPS)
                for t in tiles:
                    y = dst[:, t - off, :]
                    if norm:
                        V.scalar_tensor_tensor(out=y, in0=H[:, t, :], scalar=small[:, 32 + t:33 + t], in1=sc, op0=ALU.mult, op1=ALU.mult)
                    else:
                        V.tensor_tensor(y, H[:, t, :], sc, ALU.mult)
                    dve.drain()
                    evs = [(event, l, t)]
                    if t == tiles[-1]:
                        evs += [("row", n) for n in rows_]
                    sig(V.tensor_tensor(y, y, sh, ALU.add), *evs)

            def layernorm(l, which):
                ng, g = row(l, "lng", which)
                nb, b2 = row(l, "lnb", which)
                for t in LAT:
                    for c in range(2):
                        V.bn_stats(small[:, 40 + 6 * c:46 + 6 * c], H[:, t, c * 512:(c + 1) * 512])
                    dve.drain()
                    V.bn_aggr(small[:, 32 + 2 * (t - 2):34 + 2 * (t - 2)], small[:, 40:52])
                    dve.drain()
                V.tensor_copy(small[:, 56:58], small[:, 33:37:2])
                rsqrt(small[:, 56:58], 1.0, LN_EPS)
                for t in LAT:
                    x = H[:, t, :]
                    V.tensor_scalar(x, x, small[:, 32 + 2 * (t - 2):33 + 2 * (t - 2)], small[:, 54 + t:55 + t], ALU.subtract, ALU.mult)
                    dve.drain()
                    V.tensor_tensor(x, x, g, ALU.mult)
                    dve.drain()
                    evs = [("ln", l, which, t)] + ([("row", ng), ("row", nb)] if t == 3 else [])
                    sig(V.tensor_tensor(x, x, b2, ALU.add), *evs)
                dve.drain()

            def rope(dst, src, t, groups, tmp):
                cos = const("cos")[:, (t - 2) * 32:(t - 1) * 32].unsqueeze(1).broadcast_to([P, groups, 32])
                sin = const("sin")[:, (t - 2) * 32:(t - 1) * 32].unsqueeze(1).broadcast_to([P, groups, 32])
                ta, tb = tmp
                V.tensor_tensor(dst[:, :, 0, :], src[:, :, 0, :], cos, ALU.mult)
                V.tensor_tensor(ta, src[:, :, 1, :], sin, ALU.mult)
                V.tensor_tensor(dst[:, :, 1, :], src[:, :, 0, :], sin, ALU.mult)
                V.tensor_tensor(tb, src[:, :, 1, :], cos, ALU.mult)
                dve.drain()
                V.tensor_tensor(dst[:, :, 0, :], dst[:, :, 0, :], ta, ALU.subtract)
                return V.tensor_tensor(dst[:, :, 1, :], dst[:, :, 1, :], tb, ALU.add)

            def groups32(ap):
                return ap.rearrange("p (g a b) -> p g a b", a=2, b=32)

            def copy_T(key, t, dst, half, n=4):
                b = b_(*key, t, half)
                ev(V.tensor_copy(dst, bank3(b, n, P)), *key, t, half)

            dve.wait_ge(params_landed, 16)
            lam = par("lam").rearrange("p (a b) -> p a b", a=4)
            for q in range(2):
                V.tensor_tensor_reduce(out=left[:, q * 64:(q + 1) * 64], in0=lam[:, 2 * q, :], in1=lam[:, 2 * q + 1, :], scale=1.0,
                                       scalar=0.0, op0=ALU.mult, op1=ALU.add, accum_out=lamc[:, q:q + 1])
            sig(dve.drain(), ("lam_dots",))
            dve.wait_ge(consts_landed, 16)
            dve.wait_ge(hidden_landed, 16)

            for l in range(LAYERS):
                tiles = LT[l]
                norm = l < 2
                if l == 2:
                    dve.wait_ge(ctx2_landed, 16)
                if l != 3:
                    modulated(l, CTX, 1, ("g1", "sc1", "sh1"), xn, "xn", norm)
                modulated(l, LAT, 0, ("g1", "sc1", "sh1"), xn, "xn", norm)
                for t in tiles:
                    copy_T((l, "xT"), t, xT[:, 4:8, t * P:(t + 1) * P], 1)
                if l == 0:
                    raw = v4(RAW, 4, 2, 258)
                    qk = v3(QKT, 4, TOK)
                    V.memset(raw[:, :, :, 0:1], 0.0)
                    V.memset(raw[:, :, :, 257:258], 0.0)
                    sig(V.memset(v4(VML, 4, 4, 129)[:, :, :, 128:129], 1.0), ("vml_ones",))
                    cw = par("conv_w").rearrange("p (c j) -> p c j", c=4)
                    for c in range(4):
                        b = b_(0, "qk", c)
                        ev(V.tensor_copy(raw[:, c, :, 1:257], bank3(b, 2, 256)), 0, "qk", c)
                        dve.drain()
                        y = qk[:, c, :].rearrange("p (a b) -> p a b", a=2)
                        V.tensor_scalar(y, raw[:, c, :, 0:256], cw[:, c, 0:1], par("conv_b")[:, c:c + 1], ALU.mult, ALU.add)
                        dve.drain()
                        V.scalar_tensor_tensor(out=y, in0=raw[:, c, :, 1:257], scalar=cw[:, c, 1:2], in1=y, op0=ALU.mult, op1=ALU.add)
                        dve.drain()
                        sig(V.scalar_tensor_tensor(out=y, in0=raw[:, c, :, 2:258], scalar=cw[:, c, 2:3], in1=y, op0=ALU.mult,
                                                   op1=ALU.add), ("conv", c))
                    b = b_(0, "gnat")
                    ev(V.tensor_tensor(gnat[:, :, :], bank3(b, 4, 16), par("gate_b").unsqueeze(1).broadcast_to([P, 4, 16]), ALU.add), 0, "gnat")
                    gw = arena[0:4, GW:GW + 4096].rearrange("p (q d t) -> p q d t", q=4, d=2)
                    zi, zf, tmp, fl = (gw[:, q, :, :] for q in range(4))
                    mrow = arena[0:4, MROW:MROW + 1024].rearrange("p (a b) -> p a b", a=2)
                    for g in range(4):
                        b = b_(0, "gates", g)
                        dst = (zi, zf)[g % 2]
                        if g < 2:
                            ins = V.tensor_copy(dst[:, 0, :], bank[0:4, b, :])
                        else:
                            V.tensor_copy(dst[:, 1, 0:256], bank[0:4, b, rev(0)])
                            ins = V.tensor_copy(dst[:, 1, 256:512], bank[0:4, b, rev(256)])
                        ev(ins, 0, "gates", g)
                    dve.drain()
                    sig(V.scalar_tensor_tensor(out=tmp, in0=zf, scalar=-1.0, in1=zf, op0=ALU.mult, op1=ALU.max), ("absz",))
                    V.tensor_scalar(zf, zf, 0.0, None, ALU.min)
                    dve.wait_ge(*after("softplus"))
                    dve.drain()
                    V.tensor_tensor(zf, zf, tmp, ALU.subtract)
                    V.memset(fl, 1.0)
                    dve.drain()
                    for d in range(2):
                        V.tensor_tensor_scan(tmp[:, d, :], fl[:, d, :], zf[:, d, :], 0.0, ALU.mult, ALU.add)
                    dve.drain()
                    V.tensor_tensor(zi, zi, tmp, ALU.subtract)
                    dve.drain()
                    for d in range(2):
                        V.tensor_tensor_scan(fl[:, d, :], zi[:, d, :], zi[:, d, :], 0.0, ALU.max, ALU.max)
                    dve.drain()
                    V.tensor_tensor(tmp, tmp, fl, ALU.add)
                    dve.drain()
                    V.tensor_copy(zf[:, 0, :], tmp[:, 0, :])
                    V.tensor_scalar(mrow[:, 0, :], fl[:, 0, :], -1.0, None, ALU.mult)
                    for c0 in (0, 256):
                        V.tensor_copy(zf[:, 1, c0:c0 + 256], tmp[:, 1, rev(c0)])
                        V.tensor_scalar(mrow[:, 1, c0:c0 + 256], fl[:, 1, rev(c0)], -1.0, None, ALU.mult)
                    dve.drain()
                    V.tensor_copy(tmp[:, 0, :], zi[:, 0, :])
                    V.tensor_copy(tmp[:, 1, 0:256], zi[:, 1, rev(0)])
                    sig(V.tensor_copy(tmp[:, 1, 256:512], zi[:, 1, rev(256)]), ("m_rows",))
                    rt = (v3(DMASK, 8, 32), v3(DMASK + 256, 8, 32))
                    for q, name in enumerate(("dq", "dk")):
                        for t in tiles:
                            b = b_(0, name, t, 0)
                            dst = xn[:, t, q * 512:(q + 1) * 512]
                            if t < 2:
                                ins = V.tensor_copy(dst, bank[:, b, :])
                            else:
                                ins = rope(groups32(dst), groups32(bank[:, b, :]), t, 8, rt)
                                dve.drain()
                            if q:
                                ev(ins, 0, name, t, 0, more=(("roped", t),))
                            else:
                                ev(ins, 0, name, t, 0)
                    for t in tiles:
                        copy_T((0, "dqkT"), t, v3(DKT, 4, TOK)[:, :, t * P:(t + 1) * P], 1)
                    dve.wait_ge(*after("floor_rows"))
                    sig(dve.drain(), ("gate_rows",))
                    b = b_(0, "gcols")
                    ev(V.tensor_copy(gcols[:, :], bank[:, b, 0:64]), 0, "gcols")
                    dve.drain()
                    ats = v3(ATS, 4, TOK)
                    mix = v3(MIX, 4, D)

                    def masked(h, d):
                        b = b_(0, "M", h, d)
                        if h or d:
                            dve.wait_ge(*after("E", *((h, 0) if d else (h - 1, 1))))
                        tri = const("tri")[:, d * P:(d + 1) * P].unsqueeze(1).broadcast_to([P, 4, P])
                        sig(V.tensor_tensor(v3(DMASK, 4, P), bank3(b, 4, P), tri, ALU.add), ("dmask", h, d))

                    for h in range(4):
                        for d in range(2):
                            wt = v3(EW1 if d else EW0, 4, TOK)
                            masked(h, d)
                            for s in range(4):
                                dve.wait_ge(*after("ev", 0, "A", h, s))
                            dve.wait_ge(*after("E", h, d))
                            for s in range(4):
                                for t0, t1 in [(s, s + 1)] + OFF_DIAGONAL[d][s]:
                                    ins = V.tensor_tensor(wt[:, s, t0 * P:t1 * P], wt[:, s, t0 * P:t1 * P],
                                                          ats[:, s, t0 * P:t1 * P], ALU.mult)
                            sig(ins, ("WT", h, d))
                        for d in range(2):
                            for tp in range(2):
                                b = b_(0, "N", h, d, tp)
                                nd = bank[:, b, 0:258].rearrange("p (a n) -> p a n", a=2)
                                den = small[:, 8 * tp:8 * tp + 2]
                                c = 32 + (d * 4 + 2 * tp) * 4 + h
                                V.tensor_copy(den, nd[:, :, 128])
                                dve.drain()
                                V.scalar_tensor_tensor(out=den, in0=den, scalar=-1.0, in1=den, op0=ALU.mult, op1=ALU.max)
                                dve.drain()
                                V.tensor_tensor(den, den, gcols[:, c:c + 5:4], ALU.max)
                                dve.drain()
                                V.reciprocal(den, den)
                                dve.drain()
                                for q in range(2):
                                    t = 2 * tp + q
                                    dst = mix[:, t, h * P:(h + 1) * P]
                                    if d == 0:
                                        ins = V.tensor_scalar(dst, nd[:, q, 0:128], den[:, q:q + 1], None, ALU.mult)
                                    else:
                                        ins = V.scalar_tensor_tensor(out=dst, in0=nd[:, q, 0:128], scalar=den[:, q:q + 1], in1=dst,
                                                                     op0=ALU.mult, op1=ALU.add)
                                ev(ins, 0, "N", h, d, tp)
                    dve.wait_ge(*after("lam_exp"))
                    V.tensor_tensor(lamc[:, 2:3], lamc[:, 1:2], lamc[:, 0:1], ALU.subtract)
                    dve.drain()
                    V.tensor_scalar(lamc[:, 3:4], lamc[:, 2:3], LAM_INIT, None, ALU.subtract)
                    dve.drain()

                    for step in range(16 + 2):
                        if step < 16:
                            i = step
                            t, h = i // 4, i % 4
                            nk = 256 if t < 2 else 512
                            c = 8 * (i % 4)
                            for m in range(2):
                                b = b_(0, "S", t, h, m)
                                V.tensor_reduce(small[:, c + 4 + m:c + 5 + m], bank[:, b, 0:nk], AX_X, ALU.max)
                            dve.drain()
                            sig(V.tensor_scalar(small[:, c:c + 2], small[:, c + 4:c + 6], -SCALE64, None, ALU.mult), ("smax", 0, i))
                        if 0 <= step - 2 < 16:
                            i = step - 2
                            t, h = i // 4, i % 4
                            nk = 256 if t < 2 else 512
                            c = 8 * (i % 4)
                            dve.wait_ge(*after("ev", 0, "S", t, h, 1))
                            pr0, pr1 = v(ATS + (i % 3) * 1024, nk), v(ATS + (i % 3) * 1024 + 512, nk)
                            V.reciprocal(small[:, c + 2:c + 4], small[:, c + 2:c + 4])
                            dve.drain()
                            V.tensor_scalar(pr1, pr1, small[:, c + 3:c + 4], lamc[:, 3:4], ALU.mult, ALU.mult)
                            dve.drain()
                            sig(V.scalar_tensor_tensor(out=pr0, in0=pr0, scalar=small[:, c + 2:c + 3], in1=pr1, op0=ALU.mult,
                                                       op1=ALU.add), ("Pr", 0, i))
                    nh, hg = row(0, "headg", 0)
                    dve.wait_ge(*after("ev", 0, "O", 15))
                    ss = gcols[:, 0:32]
                    for t in tiles:
                        x = mix[:, t, :].rearrange("p (h c) -> p h c", h=8)
                        sq = v3(ATS + (t % 2) * 1024, 8, P)
                        V.tensor_tensor(sq, x, x, ALU.mult)
                        dve.drain()
                        V.tensor_reduce(ss[:, 8 * t:8 * t + 8], sq, AX_X, ALU.add)
                    rsqrt(ss, 1.0 / P, EPS)
                    for t in tiles:
                        x = mix[:, t, :].rearrange("p (h c) -> p h c", h=8)
                        V.tensor_tensor(x, x, ss[:, 8 * t:8 * t + 8].unsqueeze(2).broadcast_to([P, 8, P]), ALU.mult)
                        dve.drain()
                        V.tensor_tensor(mix[:, t, :], mix[:, t, :], hg, ALU.mult)
                        dve.drain()
                        dve.wait_ge(*after("ev", 0, "o", t, 0))
                        V.tensor_tensor(mix[:, t, 0:512], mix[:, t, 0:512], v(OSIG + t * 512, 512), ALU.mult)
                        evs = [("mix", 0, t)] + ([("row", nh)] if t == 3 else [])
                        sig(V.tensor_scalar(mix[:, t, 512:1024], mix[:, t, 512:1024], 1.0 - LAM_INIT, None, ALU.mult), *evs)
                if l == 1:
                    qn, kn = v3(L1_QN, 2, 1024), v3(L1_KN, 4, 256)
                    rt = (v3(L1_P, 8, 32), v3(L1_P + 256, 8, 32))
                    for q in range(2):
                        for t in LAT:
                            b = b_(1, f"q{q}", t, 0)
                            ins = rope(groups32(qn[:, t - 2, q * 512:(q + 1) * 512]), groups32(bank[:, b, :]), t, 8, rt)
                            dve.drain()
                            more = (("q_roped", t),) if q else ()
                            ev(ins, 1, f"q{q}", t, 0, more=more)
                    rt4 = (v3(L1_P, 4, 32), v3(L1_P + 128, 4, 32))
                    for t in tiles:
                        b = b_(1, "kv", t, 0)
                        if t < 2:
                            ins = V.tensor_copy(kn[:, t, :], bank[:, b, 0:256])
                        else:
                            ins = rope(groups32(kn[:, t, :]), groups32(bank[:, b, 0:256]), t, 4, rt4)
                            dve.drain()
                        sig(ins, ("k_roped", t))
                    for t in LAT:
                        copy_T((1, "qT"), t, v3(L1_QT, 8, 256)[:, 4:8, (t - 2) * P:(t - 1) * P], 1)
                    mix = v3(MIX, 2, D)
                    V.tensor_scalar(gcols[:, 0:16], par("sink"), 1.0 / SCALE64, None, ALU.mult)
                    dve.drain()

                    for step in range(32 + 3):
                        if step < 32:
                            i = step
                            t, c, hq = i // 16, 8 * (i % 4), head_of(i)
                            b = b_(1, "S", i)
                            off = 256 + (P if t == 0 else 0)
                            V.tensor_tensor(bank[:, b, off:off + P], bank[:, b, off:off + P], const("win")[:, t * P:(t + 1) * P], ALU.add)
                            dve.drain()
                            V.tensor_reduce(small[:, c + 4:c + 5], bank[:, b, :], AX_X, ALU.max)
                            dve.drain()
                            sig(V.tensor_scalar(small[:, c:c + 1], small[:, c + 4:c + 5], gcols[:, hq:hq + 1], -SCALE64, ALU.max, ALU.mult),
                                ("smax", 1, i))
                        if 0 <= step - 3 < 32:
                            i = step - 3
                            t, c, hq = i // 16, 8 * (i % 4), head_of(i)
                            b = b_(1, "O", i)
                            V.tensor_tensor(small[:, c + 3:c + 4], small[:, c + 1:c + 2], small[:, c + 2:c + 3], ALU.add)
                            dve.drain()
                            V.reciprocal(small[:, c + 3:c + 4], small[:, c + 3:c + 4])
                            dve.drain()
                            ev(V.tensor_scalar(mix[:, t, hq * 64:hq * 64 + 64], bank[:, b, 0:64], small[:, c + 3:c + 4],
                                               None, ALU.mult), 1, "O", i)
                    dve.drain()
                    sig(dve.drain(), ("mix", 1, 2), ("mix", 1, 3))
                if l == 2:
                    z = v3(L2_Z, 4, 704)
                    nm, mg = row(2, "mlag", 0)
                    kr = v3(L2_QR, 4, P)
                    for t in LAT:
                        b = b_(2, "zq", t, 0)
                        ev(V.tensor_copy(z[:, t, 0:384], bank[:, b, 0:384]), 2, "zq", t, 0)
                        dve.drain()
                        squares(z[:, t, 0:384], v(L2_PT, 384), small[:, 32:33])
                        rsqrt(small[:, 32:33], 1.0 / 384, EPS)
                        sig(V.scalar_tensor_tensor(out=z[:, t, 0:384], in0=z[:, t, 0:384], scalar=small[:, 32:33], in1=mg[:, 0:384],
                                                   op0=ALU.mult, op1=ALU.mult), ("zq_n", t))
                    rt1 = (v3(L2_P + 512, 1, 32), v3(L2_P + 544, 1, 32))
                    for t in tiles:
                        b = b_(2, "zkv", t, 0)
                        ev(V.tensor_copy(z[:, t, 384:704], bank[:, b, 0:320]), 2, "zkv", t, 0)
                        dve.drain()
                        squares(z[:, t, 384:640], v(L2_PT, 256), small[:, 32:33])
                        rsqrt(small[:, 32:33], 1.0 / 256, EPS)
                        evs = [("zkv_n", t)] + ([("row", nm)] if t == 3 else [])
                        sig(V.scalar_tensor_tensor(out=z[:, t, 384:640], in0=z[:, t, 384:640], scalar=small[:, 32:33],
                                                   in1=mg[:, 384:640], op0=ALU.mult, op1=ALU.mult), *evs)
                        if t < 2:
                            V.tensor_copy(kr[:, t, 0:64], z[:, t, 640:704])
                        else:
                            rope(groups32(kr[:, t, 0:64]), groups32(z[:, t, 640:704]), t, 1, rt1)
                        dve.drain()
                        sig(V.tensor_copy(kr[:, t, 64:128], kr[:, t, 0:64]), ("kr", t))
                    for t in tiles:
                        if t in LAT:
                            copy_T((2, "cqT"), t, v3(L2_CQT, 3, 256)[:, :, (t - 2) * P:(t - 1) * P], 0, n=3)
                        copy_T((2, "ckvT"), t, v3(L2_CKVT, 2, TOK)[:, :, t * P:(t + 1) * P], 0, n=2)
                        copy_T((2, "krT"), t, v3(L2_KRT, 1, TOK)[:, :, t * P:(t + 1) * P], 0, n=1)
                    for c in range(1, 8, 2):
                        b = b_(2, "uqn", c)
                        ev(V.tensor_copy(v3(L2_QNT, 8, 256)[:, c, :], bank[:, b, 0:256]), 2, "uqn", c)
                    qr = v3(L2_QR, 2, 512)
                    rt = (v3(L2_P, 8, 32), v3(L2_P + 256, 8, 32))
                    for t in LAT:
                        b = b_(2, "uqr", t, 0)
                        ins = rope(groups32(qr[:, t - 2, :]), groups32(bank[:, b, :]), t, 8, rt)
                        dve.drain()
                        ev(ins, 2, "uqr", t, 0, more=(("qr_roped", t),))
                    for c in range(1, 8, 2):
                        b = b_(2, "ukn", c)
                        ev(V.tensor_copy(v3(L2_KNT, 8, TOK)[:, c, :], bank[:, b, :]), 2, "ukn", c)
                    for part in range(2):
                        for t in tiles:
                            if t % 2:
                                b = b_(2, "uv", t, part)
                                ev(V.tensor_copy(v3(L2_V, 4, 1024)[:, t, part * 512:part * 512 + 512], bank[:, b, :]), 2, "uv", t, part)
                    for t in LAT:
                        copy_T((2, "qrT"), t, v3(L2_QRT, 4, 256)[:, :, (t - 2) * P:(t - 1) * P], 0)
                    mix = v3(L2_MIX, 2, D)

                    for step in range(16 + 3):
                        if step < 16:
                            i = step
                            c = 8 * (i % 4)
                            b = b_(2, "S", i)
                            V.tensor_reduce(small[:, c + 4:c + 5], bank[:, b, :], AX_X, ALU.max)
                            dve.drain()
                            sig(V.tensor_scalar(small[:, c:c + 1], small[:, c + 4:c + 5], -SCALE_MLA, None, ALU.mult), ("smax", 2, i))
                        if 0 <= step - 3 < 16:
                            i = step - 3
                            t, h, c = i // 8, i % 8, 8 * (i % 4)
                            b = b_(2, "O", i)
                            V.reciprocal(small[:, c + 3:c + 4], small[:, c + 1:c + 2])
                            dve.drain()
                            ev(V.tensor_scalar(mix[:, t, h * P:(h + 1) * P], bank[:, b, 0:P], small[:, c + 3:c + 4],
                                               None, ALU.mult), 2, "O", i)
                    dve.drain()
                    sig(dve.drain(), ("mix", 2, 2), ("mix", 2, 3))
                if l == 3:
                    for t in LAT:
                        b = b_(3, "in1", t, 0)
                        ev(V.tensor_copy(v3(L3_Z, 2, 1024)[:, t - 2, 512:1024], bank[:, b, :]), 3, "in1", t, 0)
                    for c in range(1, 8, 2):
                        b = b_(3, "pool", c)
                        ev(V.tensor_copy(v3(L3_POOLT, 8, 256)[:, c, :], bank[:, b, 0:256]), 3, "pool", c)
                    for c in range(1, 8, 2):
                        b = b_(3, "yT", c)
                        ev(V.tensor_scalar(v3(L3_YT, 8, 256)[:, c, :], bank[:, b, 0:256], par("pool_scale")[:, c:c + 1], None, ALU.mult),
                           3, "yT", c)
                out_tiles = PEER_TILES[l]
                xT2, qT = xT2_of[l], qT_of[l]
                t0 = out_tiles[0]
                if l < 3:
                    for t in out_tiles:
                        copy_T((l, "mT"), t, mixT[:, 4:8, t * P:(t + 1) * P], 1)
                gates_ = {s: row(l, "gate1", s) for s in ((1, 0) if l == 0 else (0,))}

                def residual(y, t, c0, c1, g, tmp_, events, post):
                    V.tensor_tensor(tmp_, y, g[:, c0:c1], ALU.mult)
                    dve.drain()
                    x = H[:, t, c0:c1]
                    if post:
                        ins = V.scalar_tensor_tensor(out=x, in0=x, scalar=ALPHA, in1=tmp_, op0=ALU.mult, op1=ALU.add)
                    else:
                        ins = V.tensor_tensor(x, x, tmp_, ALU.add)
                    sig(ins, *events)

                tmpr = v(RESID, 1024)
                for j in range(2):
                    for t in out_tiles:
                        b = b_(l, f"out{j}", t, 0)
                        ng, g = gates_[1 if t < 2 else 0]
                        evs = [("ev", l, f"out{j}", t, 0)]
                        if j == 1 and t in (1, 3):
                            evs.append(("row", ng))
                        residual(bank[:, b, :], t, j * 512, j * 512 + 512, g, tmpr[:, (t % 2) * 512:(t % 2) * 512 + 512], evs, l >= 2)
                sig(dve.drain(), ("ring_room", l))
                if l >= 2:
                    layernorm(l, 0)
                if l == 0:
                    modulated(l, CTX, 1, ("g2", "sc2", "sh2"), xnat, "xnat", True)
                modulated(l, LAT, 0, ("g2", "sc2", "sh2"), xnat, "xnat", norm, off=t0)
                for t in out_tiles:
                    copy_T((l, "xT2"), t, xT2[:, 4:8, (t - t0) * P:(t - t0 + 1) * P], 1)
                ntok = len(out_tiles) * P
                def take_queries(j):
                    for c in (4 * j + 1, 4 * j + 3):
                        b = b_(l, "q", c)
                        ev(V.tensor_copy(qT[:, c % qT.shape[1], 0:ntok], bank[:, b, 0:ntok]), l, "q", c)

                def take_scores(i, j):
                    b = b_(l, "sc", i, j)
                    ev(V.tensor_copy(scores[:, i * PH + 2 * j:i * PH + 2 * j + 2, :].rearrange("p a b -> p (a b)"), bank[:, b, :]),
                       l, "sc", i, j)

                sig(V.memset(scores[:, len(out_tiles) * PH, :], 0.0), ("pad_scores", l))
                if l == 0:
                    for j in range(4):
                        take_queries(j)
                    for i in range(TILES):
                        for j in (1, 3):
                            take_scores(i, j)

                def topk(wait, e):
                    dve.wait_ge(head_copied, wait)
                    dve.nop(nofuse=True)
                    hs = head_scores[:, :].rearrange("p (a b) -> p a b", a=2)
                    lf = left[:, :].rearrange("p (a b) -> p a b", a=2)
                    for q in range(2):
                        V.max(topv[:, q, 0:8], hs[:, q, :])
                    dve.drain()
                    for q in range(2):
                        V.max_index(topi[:, q, 0:8], topv[:, q, 0:8], hs[:, q, :])
                    for q in range(2):
                        V.match_replace(lf[:, q, :], topv[:, q, 0:8], hs[:, q, :], NEG)
                    dve.drain()
                    for q in range(2):
                        V.max(topv[:, q, 8:16], lf[:, q, :])
                    dve.drain()
                    for q in range(2):
                        V.max_index(topi[:, q, 8:16], topv[:, q, 8:16], lf[:, q, :])
                    cand = head_cand
                    V.tensor_tensor(cand.rearrange("p (a b) -> p a b", a=16), topv[:, 0, :].unsqueeze(2).broadcast_to([P, 16, 16]),
                                    topv[:, 1, :].unsqueeze(1).broadcast_to([P, 16, 16]), ALU.add)
                    dve.drain()
                    V.tensor_copy(topf[:, :, :], topi[:, :, :])
                    V.max(cv[:, 0:8], cand)
                    dve.drain()
                    V.max_index(ci[:, 0:8], cv[:, 0:8], cand)
                    V.match_replace(left[:, :], cv[:, 0:8], cand, NEG)
                    dve.drain()
                    V.max(cv[:, 8:16], left[:, :])
                    V.tensor_scalar(neg[:, :], cv[:, 0:1], -1.0, None, ALU.mult)
                    dve.drain()
                    V.max_index(ci[:, 8:16], cv[:, 8:16], left[:, :])
                    dve.drain()
                    V.tensor_scalar(ab[:, 0, :], ci[:, :], 4, None, ALU.logical_shift_right)
                    V.tensor_scalar(ab[:, 1, :], ci[:, :], 15, None, ALU.bitwise_and)
                    dve.drain()
                    V.tensor_copy(abf[:, :, :], ab[:, :, :])
                    dve.drain()
                    V.tensor_tensor(eq[:, :, :, :].rearrange("p a k m -> p (a k) m"),
                                    abf[:, :, :].rearrange("p a k -> p (a k)").unsqueeze(2).broadcast_to([P, 32, 16]),
                                    const("iota").unsqueeze(1).broadcast_to([P, 32, 16]), ALU.is_equal)
                    dve.drain()
                    for q in range(2):
                        V.tensor_tensor(eq[:, q, :, :], eq[:, q, :, :], topf[:, q, :].unsqueeze(1).broadcast_to([P, 16, 16]), ALU.mult)
                    dve.drain()
                    V.tensor_reduce(selv[:, :, :].rearrange("p a k -> p (a k)"), eq[:, :, :, :].rearrange("p a k m -> p (a k) m"),
                                    AX_X, ALU.add)
                    dve.drain()
                    V.scalar_tensor_tensor(out=ef[:, :], in0=selv[:, 0, :], scalar=float(NK), in1=selv[:, 1, :], op0=ALU.mult, op1=ALU.add)
                    dve.drain()
                    V.tensor_copy(idx[:, e, :], ef[:, :]).then_inc(topk_done, 1)

                def gates(wait, wait_free, e):
                    dve.wait_ge(exp_done, wait)
                    dve.nop(nofuse=True)
                    if wait_free is not None:
                        dve.wait_ge(diag_done, wait_free)
                        dve.nop(nofuse=True)
                    V.reciprocal(neg[:, :], es[:, :])
                    dve.drain()
                    V.tensor_scalar(gate[:, e, :], ex[:, :], neg[:, :], None, ALU.mult)

                head_cand = eq[:, 0, :, :].rearrange("p k m -> p (k m)")
                k0 = HEADS_BEFORE[l] + l
                if l:
                    for j in range(4):
                        take_queries(j)
                        take_scores(1, j)
                        if j == 1:
                            topk(k0 + 1, 0)
                else:
                    topk(k0 + 1, 0)
                gates(k0 + 1, None, 0)
                gate_rows = {s: row(l, "gate2", s) for s in ((1, 0) if l == 0 else (0,))}
                for i, t in enumerate(out_tiles):
                    q0 = HEADS_BEFORE[l] + i * PH
                    with dve.Fori(0, PH // 2) as it:
                        for e in range(2):
                            for j in range(GPH):
                                s = j % SLOTS
                                dve.wait_ge(ring_landed[s], it * (2 * GPH // SLOTS * GROUP * 16)
                                            + ((q0 * GPH + e * GPH + j) // SLOTS + 1) * GROUP * 16)
                                for x in range(GROUP):
                                    ins = V.tensor_tensor_reduce(out=ring[:, s, x, 0:D], in0=ring[:, s, x, 0:D], in1=xnat[:, i, :],
                                                                 scale=1.0, scalar=0.0, op0=ALU.mult, op1=ALU.add,
                                                                 accum_out=dot[:, s, x:x + 1])
                                ins.then_inc(dots_done, 1)
                                if j == 1:
                                    topk(it * 2 + (q0 + l + e + 2), (e + 1) % 2)
                                if j == 4:
                                    gates(it * 2 + (q0 + l + e + 2), it * (2 * GPH) + (q0 * GPH + e * GPH + 1), (e + 1) % 2)
                    dve.wait_ge(slots_free, SLOTS + (q0 + PH) * GPH)
                    y = bank[:, 2 * (i % 2):2 * (i % 2) + 2, :].rearrange("p a b -> p (a b)")
                    ng, g = gate_rows[1 if t < 2 else 0]
                    evs = [("y_taken", l, i)]
                    if t in (1, 3):
                        evs.append(("row", ng))
                    residual(y, t, 0, D, g, xnat[:, i, :], evs, l >= 2)
                    dve.drain()
                if l == 1:
                    nf, fg = row(1, "final", 0)
                    for t in LAT:
                        squares(H[:, t, :], xnat[:, t - 2, :], small[:, 32 + t:33 + t])
                    rsqrt(small[:, 34:36], 1.0 / D, EPS)
                    for t in LAT:
                        evs = [("final1", t)] + ([("row", nf)] if t == 3 else [])
                        sig(V.scalar_tensor_tensor(out=H[:, t, :], in0=H[:, t, :], scalar=small[:, 32 + t:33 + t], in1=fg, op0=ALU.mult,
                                                   op1=ALU.mult), *evs)
                    dve.drain()
                if l >= 2:
                    layernorm(l, 1)
            sig(dve.drain(), ("final_out",))
        return st.at




def _blocks(inp, f32):
    def tiled(w, k=KC):
        return w.reshape(k, P, -1).transpose(1, 0, 2).reshape(P, -1)

    def cut(w, j, k=KC):
        return tiled(w[:, 512 * j:512 * (j + 1)], k)

    out = np.zeros((len(BLOCKS), P, WCOLS), f32)

    late_keys = np.zeros((LAYERS - 1, P, 2 * PH * NK), f32)

    def put(name, a):
        n = BLOCK_AT[name]
        assert a.shape == (P, BLOCKS[n][1]), (name, a.shape)
        out[n, :, :a.shape[1]] = a

    for l in range(LAYERS):
        w = (inp["mod_w"] if l < 2 else inp["w_mod_2"])[l % 2]
        for n in range(MODC // 4):
            put((l, "mod", n), cut(w, n))
        wq = (inp["pr_w_q"] if l < 2 else inp["peer_w_q_2"])[l % 2]
        for n in range(4):
            put((l, "wq", n), cut(wq, n))
        if l < 2:
            keys = inp["pr_keys"][l]
        else:
            keys = np.stack([inp["peer_k1_2"][l - 2], inp["peer_k2_2"][l - 2]], axis=1)
        keys = keys.reshape(2 * PH, NK, P).transpose(2, 0, 1).reshape(P, -1)
        if l:
            late_keys[l - 1] = keys
        else:
            put((0, "keys"), keys)
    w = inp["ev_w_in"][0]
    put((0, "qk"), tiled(w[:, 0:512]))
    put((0, "v"), tiled(w[:, 512:1024]))
    put((0, "o"), tiled(w[:, 1024:1536]))
    put((0, "gates"), tiled(w[:, 1536:1552]))
    for j, n in enumerate(("dq", "dk", "dv")):
        put((0, n), tiled(w[:, 1552 + 512 * j:2064 + 512 * j]))
    w = inp["od_w_in"][0]
    order = [head_of(i) for i in range(16)]
    wq = w[:, :1024].reshape(D, 16, 64)[:, order].reshape(D, 1024)
    put((1, "q0"), cut(wq, 0))
    put((1, "q1"), cut(wq, 1))
    put((1, "kv"), tiled(w[:, 1024:]))
    w = inp["mla_w_in_2"][0]
    put((2, "zq"), tiled(w[:, :384]))
    put((2, "zkv"), tiled(w[:, 384:]))
    uq = inp["mla_w_uq_2"][0].reshape(384, 8, 192)
    put((2, "uqn"), tiled(uq[:, :, :128].reshape(384, 1024), 3))
    put((2, "uqr"), tiled(uq[:, :, 128:].reshape(384, 512), 3))
    ukv = inp["mla_w_ukv_2"][0].reshape(256, 8, 256)
    put((2, "ukn"), tiled(ukv[:, :, :128].reshape(256, 1024), 2))
    put((2, "uv"), tiled(ukv[:, :, 128:].reshape(256, 1024), 2))
    put((3, "in0"), cut(inp["pool_w_in_2"][0], 0))
    put((3, "in1"), cut(inp["pool_w_in_2"][0], 1))
    band = np.zeros((SEQ, 4, SEQ), f32)
    for g, win in enumerate((2, 4, 8, 16)):
        for t in range(SEQ):
            lo, hi = max(t - win // 2, 0), min(t + win // 2, SEQ)
            band[lo:hi, g, t] = 1.0 / (hi - lo)
            band[t, g, t] -= 1.0
    put((3, "band"), tiled(band.reshape(SEQ, -1), 2))
    put((3, "grp"), inp["pool_w_grp_2"][0].reshape(4, 2, P, 256).transpose(2, 0, 1, 3).reshape(P, -1))
    for l, w in enumerate((inp["ev_w_out"][0], inp["od_w_out"][0], inp["mla_w_o_2"][0], inp["pool_w_out_2"][0])):
        put((l, "out0"), cut(w, 0))
        put((l, "out1"), cut(w, 1))
    return out, late_keys


def _consts(f32):
    c = np.zeros((P, CT_COLS), f32)
    p, j = np.arange(P)[:, None], np.arange(P)[None, :]

    def at(name):
        o, n = CT[name]
        return c[:, o:o + n]

    at("ident")[:] = np.eye(P)
    at("tri")[:, :P] = np.where(p <= j, 0, MASK)
    at("tri")[:, P:] = np.where(p >= j, 0, MASK)
    at("win")[:, :P] = np.where(j <= p, 0, MASK)
    at("win")[:, P:] = np.where(j >= p, 0, MASK)
    pos = np.arange(SEQ)
    inv = (10000.0 ** (-np.arange(16, dtype=np.float64) / 16))
    ang = np.concatenate([(pos // 64)[:, None] * inv, (pos % 64)[:, None] * inv], axis=1)
    at("cos")[:] = np.cos(ang).reshape(2, P, 32).transpose(1, 0, 2).reshape(P, 64)
    at("sin")[:] = np.sin(ang).reshape(2, P, 32).transpose(1, 0, 2).reshape(P, 64)
    at("iota")[:] = np.arange(16)[None]
    for h in range(4):
        at("sel")[h, h * P:(h + 1) * P] = 1
    at("add4")[:] = (p % 32) == np.arange(2)
    return c


def _params(inp, f32):
    c = np.zeros((P, PT_COLS), f32)

    def at(name, rows=P):
        o, n = PT_[name]
        return c[:rows, o:o + n]

    at("conv_w")[:] = inp["ev_ml_conv_w"][0].reshape(3, 4, P).transpose(2, 1, 0).reshape(P, 12)
    at("conv_b")[:] = inp["ev_ml_conv_b"][0].reshape(4, P).T
    at("gate_b")[:] = inp["ev_ml_gate_b"][0].reshape(1, 16)
    at("lam")[:] = inp["ev_da_lam"][0].reshape(1, 256)
    at("sink")[:] = inp["od_sink"][0].reshape(1, 16)
    at("pool_scale")[:] = inp["pool_scale_2"][0].reshape(8, P).T
    cond = np.stack([inp["c"][0], inp["c_ctx"], inp["c_2"][0], inp["c_ctx_2"]])
    at("cond")[:, 0:32] = cond.reshape(4, KC, P).transpose(2, 1, 0).reshape(P, 32)
    mb = np.concatenate([inp["mod_b"], inp["b_mod_2"]])
    at("mod_b")[:] = mb.reshape(LAYERS, MODC, P).transpose(2, 0, 1).reshape(P, -1)
    return c


def _gains(inp, f32):
    g = np.zeros((15, D), f32)
    for l in range(2):
        g[GAIN[("norm1", l)]] = inp["norm1_g"][l]
        g[GAIN[("norm2", l)]] = inp["norm2_g"][l]
        for s in range(2):
            g[GAIN[("lng", l + 2, s)]] = inp["ln_g_2"][l, s]
            g[GAIN[("lnb", l + 2, s)]] = inp["ln_b_2"][l, s]
    g[GAIN["headg"]] = np.concatenate([inp["ev_ml_norm_g"][0], inp["ev_da_norm_g"][0]])
    g[GAIN["final"]] = inp["final_g"]
    g[GAIN["mlag"], :384] = inp["mla_q_norm_2"][0]
    g[GAIN["mlag"], 384:640] = inp["mla_kv_norm_2"][0]
    return g


def layout(inputs):
    inp = {k: np.asarray(a) for k, a in inputs.items()}
    f32 = np.float32

    def tok(a):
        return a[0].reshape(2, P, D).transpose(1, 0, 2)

    arrays = {
        "hidden": np.ascontiguousarray(np.concatenate([tok(inp["ctx"]), tok(inp["x"])], axis=1)),
        "ctx2": np.ascontiguousarray(tok(inp["ctx_2"])),
        "consts": _consts(f32),
        "params": _params(inp, f32),
        "gains": _gains(inp, f32),
    }
    arrays["weights"], arrays["late_keys"] = _blocks(inp, f32)
    for l in range(LAYERS):
        u = inp["pr_u" if l < 2 else "peer_u_2"][l % 2]
        v = inp["pr_v" if l < 2 else "peer_v_2"][l % 2]
        arrays[f"uv{l}"] = np.concatenate([u, v], axis=1)
    return arrays


def build(make, arrays):
    known = {}
    for _ in range(2):
        nc = make()
        A = {n: nc.dram_tensor(n, a.shape, mybir.dt.from_np(a.dtype), kind="ExternalInput").ap() for n, a in arrays.items()}
        A["out"] = nc.dram_tensor("out", (P, 2, D), F32, kind="ExternalOutput").ap()
        known = program(nc, A, known)
    return nc


def kernel(**inputs):
    import concourse.bacc as bacc
    from concourse.bass_utils import run_bass_kernel_spmd

    arrays = layout(inputs)
    nc = build(lambda: bacc.Bacc("TRN2", target_bir_lowering=False, num_devices=1), arrays)
    r = run_bass_kernel_spmd(nc, [arrays], core_ids=[0])
    out = r.results[0]["out"]
    return np.ascontiguousarray(out.transpose(1, 0, 2).reshape(1, SEQ, D))
```

```python
from contextlib import ExitStack

import numpy as np

import concourse.bass as bass
from concourse import mybir

F32 = mybir.dt.float32
U32 = mybir.dt.uint32
ALU = mybir.AluOpType
ACT = mybir.ActivationFunctionType
AX_X = mybir.AxisListType.X
ds = bass.ds

P = 128
D = 1024
KC = D // P
SEQ = 256
TILES = 4
CTX, LAT = (0, 1), (2, 3)
TOK = TILES * P
NMOD = 6
MODC = NMOD * KC
MODB = MODC // 4
LAYERS = 4
EPS = 1e-6
LN_EPS = 1e-5
ALPHA = 4.0 ** 0.25
LAM_INIT = 0.2
SCALE64 = 64.0 ** -0.5
SCALE_MLA = 192.0 ** -0.5
NEG = -3.0e38
MASK = -1.0e30

PH, TOPK, NK = 8, 16, 128
EXPERTS = NK * NK
SLOTS = 4
GROUP = 2
GPH = TOPK // GROUP
MIX_TILES = [(0, 1, 2, 3), LAT, LAT, LAT]
ROUNDS = [(0, CTX), (0, LAT), (1, LAT), (2, LAT), (3, LAT)]
ROUNDS_OF = [[r for r, (l, _) in enumerate(ROUNDS) if l == layer] for layer in range(LAYERS)]
ROUND_HEADS = 2 * PH

ARENA = 29440
XNAT = 0
SCORES = XNAT + 4 * D
XT2 = XNAT + 2 * D
QT = SCORES + (ROUND_HEADS + 1) * 2 * NK
KEYS = QT + 8 * 2 * P
RING = KEYS + 2 * PH * NK
XNAT_NEXT = QT + 4 * 2 * P
XT = 0
XN = 19488
MIX_T = 6160
RAW, QKT, VML, OSIG = 4096, 6160, 8208, 10272
DQT, DKT, DV, MIX = 13344, 15392, 17440, 19488
ATS, EW0, DMASK, MROW = 23584, 25632, 27680, 28192
EW1 = RAW
GW = ATS
L1_QN, L1_KN, L1_QT, L1_KT, L1_V, L1_P, L1_PT = 4096, 6144, 7168, 9216, 10240, 12544, 13568
L2_Z, L2_CQT, L2_CKVT, L2_KRT, L2_QNT, L2_QR, L2_QRT, L2_KNT, L2_V = (
    4096, 6912, 7680, 8704, 9216, 11264, 12288, 13312, 17408)
L2_MIX, L2_P, L2_PT = 21504, 23552, 24576
L3_Z, L3_POOLT, L3_YT = 4096, 6144, 8192
RESID = 10496
SOURCES = (((0,), (0, 1), (0, 1, 2), (0, 1, 2, 3)), ((0, 1), (1,), (0, 1, 2, 3), (0, 1, 3)))
OFF_DIAGONAL = (([(1, 4)], [(2, 4)], [(3, 4)], []), ([(2, 4)], [(0, 1), (2, 4)], [], [(2, 3)]))

WSLOTS, WCOLS = 2, 4096
RSLOTS = 5

CT = dict(ident=(0, 128), tri=(128, 256), win=(384, 256), cos=(640, 64), sin=(704, 64), iota=(768, 16), sel=(784, 512), zero=(1296, 512), add4=(1808, 2))
CT_COLS = 1810
PT_ = dict(conv_w=(0, 12), conv_b=(12, 4), gate_b=(16, 16), lam=(32, 256), sink=(288, 16), pool_scale=(304, 8),
           cond=(312, 64), mod_b=(376, LAYERS * MODC))
PT_COLS = 376 + LAYERS * MODC


def block_list():
    def block(l, *names, k=KC, width=512):
        return [((l, n), k * width) for n in names]

    def mods(l, first, last):
        return [((l, "mod", n), KC * 512) for n in range(first, last)]

    def queries(r):
        return [((ROUNDS[r][0], "wq", n, r), KC * 512) for n in range(4)]

    out = mods(0, 0, 4) + block(0, "qk") + block(0, "gates", width=16) + block(0, "v")
    out += mods(0, 4, 5) + block(0, "o") + mods(0, 5, 6) + block(0, "dq") + mods(0, 6, 7) + block(0, "dk") + mods(0, 7, 8)
    out += block(0, "dv") + mods(0, 8, MODB) + mods(1, 0, MODB) + block(0, "out0", "out1") + queries(0) + queries(1)
    out += block(1, "q0") + mods(2, 0, 1) + block(1, "q1") + mods(2, 1, 2) + block(1, "kv") + mods(2, 2, MODB) + block(1, "out0", "out1") + queries(2)
    out += block(2, "zq", width=384) + mods(3, 0, 1) + block(2, "zkv", width=320) + mods(3, 1, 2)
    out += block(2, "uqn", k=3, width=1024) + mods(3, 2, 3) + block(2, "uqr", k=3)
    out += block(2, "ukn", "uv", k=2, width=1024) + mods(3, 3, MODB) + block(2, "out0", "out1") + queries(3)
    out += block(3, "in0", "in1") + block(3, "band", "grp", k=1, width=2048) + block(3, "out0", "out1") + queries(4)
    return out


BLOCKS = block_list()
BLOCK_AT = {name: n for n, (name, _) in enumerate(BLOCKS)}
HALFWAY = [(0, "v"), (0, "o"), (0, "dq"), (0, "dk"), (0, "dv"), (1, "q0"), (1, "q1"), (1, "kv"), (2, "zq"), (2, "zkv")]


def slots():
    freed = list(range(len(BLOCKS)))
    for name in HALFWAY:
        n = BLOCK_AT[name]
        freed[n], freed[n + 1] = n + 1, n
    out, uses = [], [0] * WSLOTS
    for n in range(len(BLOCKS)):
        before = freed[n - WSLOTS] if n >= WSLOTS else None
        s = n if before is None else out[before][0]
        uses[s] += 1
        out.append((s, uses[s], before))
    return out


SLOT = slots()


def row_list():
    out = []

    def mod(l, s, m, name):
        out.append(((l, name, s), ("mod", l, s, m)))

    def par(l, name, s, r):
        out.append(((l, name, s), ("par", r)))

    for l in (0, 1):
        for s in (1, 0):
            par(l, "g1", s, GAIN[("norm1", l)])
            mod(l, s, 1, "sc1")
            mod(l, s, 0, "sh1")
        if l == 0:
            par(l, "headg", 0, GAIN["headg"])
        for s in ((1, 0) if l == 0 else (0,)):
            mod(l, s, 2, "gate1")
        for s in ((1, 0) if l == 0 else (0,)):
            par(l, "g2", s, GAIN[("norm2", l)])
            mod(l, s, 4, "sc2")
            mod(l, s, 3, "sh2")
            mod(l, s, 5, "gate2")
        if l == 1:
            par(l, "final", 0, GAIN["final"])
    for l in (2, 3):
        for s in ((1, 0) if l == 2 else (0,)):
            mod(l, s, 1, "sc1")
            mod(l, s, 0, "sh1")
        if l == 2:
            par(l, "mlag", 0, GAIN["mlag"])
        mod(l, 0, 2, "gate1")
        par(l, "lng", 0, GAIN[("lng", l, 0)])
        par(l, "lnb", 0, GAIN[("lnb", l, 0)])
        mod(l, 0, 4, "sc2")
        mod(l, 0, 3, "sh2")
        mod(l, 0, 5, "gate2")
        par(l, "lng", 1, GAIN[("lng", l, 1)])
        par(l, "lnb", 1, GAIN[("lnb", l, 1)])
    return out


GAIN = {("norm1", 0): 0, ("norm1", 1): 1, ("norm2", 0): 2, ("norm2", 1): 3, "headg": 4, "final": 5, "mlag": 6}
for _l in (2, 3):
    for _s in (0, 1):
        GAIN[("lng", _l, _s)] = 7 + 4 * (_l - 2) + _s
        GAIN[("lnb", _l, _s)] = 9 + 4 * (_l - 2) + _s
ROWS = row_list()
ROW_AT = {name: n for n, (name, _) in enumerate(ROWS)}


def rev(c0):
    return slice(c0 + 255, c0 - 1 if c0 else None, -1)


def head_of(i):
    c, side = (i % 16) // 2, i % 2
    return (2 * (c // 4) + side) * 4 + c % 4


MODS_FIRST = [(0, n) for n in range(4)]
MODS_BESIDE = {0: [(0, n) for n in range(4, MODB)] + [(1, n) for n in range(MODB)],
               1: [(2, n) for n in range(MODB)], 2: [(3, n) for n in range(MODB)]}
MOD_ORDER = MODS_FIRST + MODS_BESIDE[0] + MODS_BESIDE[1] + MODS_BESIDE[2]
MOD_SHARE = {0: [2, 3, 3, 3, 3] + [3] * 8 + [2] * 11, 1: [2, 3, 3] + [1] * 28, 2: [2, 3, 3] + [2] * 12 + [1] * 4}


def mod_pieces(blocks):
    out = []
    for n, b in enumerate(blocks):
        out += [("low", b)] + ([("sum", blocks[n - 1])] if n else []) + [("high", b)]
    return out + [("sum", blocks[-1])]


def mod_ready(l, step):
    share = MOD_SHARE[l]
    before, now = sum(share[:step]), sum(share[:step + 1])
    return [p for p in mod_pieces(MODS_BESIDE[l])[before:now] if p[0] != "low"]


CHUNK_LAG = 2
SCORES_AFTER = {6: 2, 10: 3}
SCORES_LAG = 2


class Steps:

    def __init__(self, sems, known):
        self.sems, self.known, self.count, self.at = sems, known, dict.fromkeys(sems, 0), {}

    def done(self, engine, *events):
        self.count[engine] += 1
        for e in events:
            assert e not in self.at, e
            self.at[e] = (engine, self.count[engine])
        return 1

    def after(self, *event):
        engine, n = self.known.get(event, ("pe", 1))
        assert not self.known or event in self.known, event
        return self.sems[engine], n


def program(nc, A, known):
    with ExitStack() as ctx:
        def sb(name, shape, dt=F32):
            return ctx.enter_context(nc.sbuf_tensor(name, shape, dt))

        def sem(name):
            return ctx.enter_context(nc.semaphore(name))

        arena = sb("arena", [P, ARENA])
        H = sb("hidden_sb", [P, TILES, D])
        wring = sb("weight_ring", [P, WSLOTS, WCOLS])
        rring = sb("row_ring", [P, RSLOTS, D])
        consts = sb("consts_sb", [P, CT_COLS])
        params = sb("params_sb", [P, PT_COLS])
        silc = sb("silu_cond", [P, 2 * KC * 4])
        modst = sb("mod_staged", [2, 2, 512])
        gnat = sb("gates_by_token", [P, TILES, 16])
        gcols = sb("gate_columns", [P, 64])
        small = sb("small", [P, 64])
        lamc = sb("lambda", [P, 4])
        newton = sb("newton", [P, 64])
        head_scores = sb("head_scores", [P, 256])
        left = sb("left", [P, 256])
        topv = sb("topv", [P, 2, 16])
        topi = sb("topi", [P, 2, 16], U32)
        topf = sb("topf", [P, 2, 16])
        cv = sb("cv", [P, 16])
        ci = sb("ci", [P, 16], U32)
        ab = sb("ab", [P, 2, 16], U32)
        abf = sb("abf", [P, 2, 16])
        eq = sb("eq", [P, 2, 16, 16])
        selv = sb("selv", [P, 2, 16])
        ef = sb("ef", [P, 16])
        idx = sb("idx", [P, 2, 16], U32)
        neg = sb("neg", [P, 1])
        ex = sb("ex", [P, 16])
        es = sb("es", [P, 1])
        gate = sb("gate", [P, 2, 16])
        dot = sb("dot", [P, SLOTS, GROUP])
        gel = sb("gel", [P, SLOTS, GROUP])
        wgt = sb("wgt", [P, SLOTS, GROUP])
        diag = sb("diag", [P, SLOTS, GROUP, P])
        modparts = diag[:, 0:2, :, :].rearrange("p s x c -> p (s x c)")
        bank = ctx.enter_context(nc.psum_tensor("banks", [P, 8, 512], F32))
        mods = nc.dram_tensor("mods", [LAYERS, 2 * NMOD, D], F32, kind="Internal").ap()

        sems = {e: sem(f"{e}_steps") for e in ("pe", "dve", "act")}
        consts_landed, params_landed, hidden_landed = sem("consts_landed"), sem("params_landed"), sem("hidden_landed")
        ctx2_landed, stored = sem("ctx2_landed"), sem("stored")
        w_landed = [sem(f"weights_landed{i}") for i in range(WSLOTS)]
        r_landed = [sem(f"row_landed{i}") for i in range(RSLOTS)]
        mods_stored = [sem(f"mods_stored{i}") for i in range(2)]
        keys_landed = sem("keys_landed")
        ring_landed = [sem(f"experts_landed{i}") for i in range(SLOTS)]
        slots_free, dots_done, diag_done = sem("slots_free"), sem("dots_done"), sem("diag_done")
        topk_done, head_copied, exp_done = sem("topk_done"), sem("head_copied"), sem("exp_done")

        st = Steps(sems, known)
        after, done = st.after, st.done

        def v(off, n):
            return arena[:, off:off + n]

        def v3(off, a, b):
            return arena[:, off:off + a * b].rearrange("p (a b) -> p a b", a=a)

        def v4(off, a, b, c):
            return arena[:, off:off + a * b * c].rearrange("p (a b c) -> p a b c", a=a, b=b)

        def const(name):
            o, n = CT[name]
            return consts[:, o:o + n]

        def par(name):
            o, n = PT_[name]
            return params[:, o:o + n]

        ident = const("ident")
        ring = arena[:, RING:RING + SLOTS * GROUP * 2 * D].rearrange("p (s x c) -> p s x c", s=SLOTS, x=GROUP)
        scores = v3(SCORES, ROUND_HEADS + 1, 2 * NK)
        xT = v3(XT, KC, TOK)
        xnat = v3(XNAT, 2, D)
        xn = v3(XN, TILES, D)
        mixT = v3(MIX_T, KC, TOK)
        xT2 = v3(XT2, KC, 2 * P)
        qT = v3(QT, 8, 2 * P)
        keys_sb = v3(KEYS, 2 * PH, NK)

        def bank3(b, a, n):
            return bank[:, b, 0:a * n].rearrange("p (a n) -> p a n", a=a)

        bank_of = {}

        def block_ap(n, k):
            cols = BLOCKS[n][1]
            return wring[:, SLOT[n][0], 0:cols].rearrange("p (k c) -> p k c", k=k)

        LT = {0: (0, 1, 2, 3), 1: (0, 1, 2, 3), 2: (0, 1, 2, 3), 3: LAT}

        def xnat_of(r, t):
            if (r, t) == (1, 3):
                return v(XNAT_NEXT, D)
            return xnat[:, t % 2, :]

        block = ctx.enter_context(nc.Block())

        @block.sync
        def _(sp):
            sp.dma_start(params[:, :], A["params"]).then_inc(params_landed, 16)
            sp.dma_start(consts[:, :], A["consts"]).then_inc(consts_landed, 16)
            for n, (name, cols) in enumerate(BLOCKS):
                if n == 2:
                    sp.dma_start(H[:, :, :], A["hidden"]).then_inc(hidden_landed, 16)
                slot, _, before = SLOT[n]
                if before is not None:
                    sp.wait_ge(*after("w", before))
                if name[1:3] == ("wq", 0) and name[3] == ROUNDS_OF[name[0]][0]:
                    sp.wait_ge(*after("ring_room", name[0]))
                    sp.dma_start(v(KEYS, 2 * PH * NK), A["keys"][name[0]]).then_inc(keys_landed, 16)
                sp.dma_start(wring[:, slot, 0:cols], A["weights"][n, :, 0:cols]).then_inc(w_landed[slot], 16)
            sp.wait_ge(*after("final_out"))
            sp.dma_start(A["out"], H[:, 2:4, :]).then_inc(stored, 16)
            sp.wait_ge(stored, 16)

        @block.gpsimd
        def _(pool):
            sent = [0]

            def rows_until(stop):
                while sent[0] < stop:
                    n = sent[0]
                    kind, *what = ROWS[n][1]
                    if n >= RSLOTS:
                        pool.wait_ge(*after("row", n - RSLOTS))
                    if kind == "mod":
                        l, s, m = what
                        for q in range(2):
                            pool.wait_ge(mods_stored[q], 16 * (l * NMOD + m + 1))
                        src = mods[l, s * NMOD + m:s * NMOD + m + 1, :]
                    else:
                        src = A["gains"][what[0]:what[0] + 1, :]
                    pool.dma_start(rring[:, n % RSLOTS, :], src.broadcast_to([P, D])).then_inc(r_landed[n % RSLOTS], 16)
                    sent[0] += 1

            for l in range(LAYERS):
                rows_until(1 + max(n for n, (name, _) in enumerate(ROWS) if name[0] == l))
                if l == 1:
                    pool.wait_ge(*after("xn", 1, 1))
                    pool.dma_start(H[:, 0:2, :], A["ctx2"]).then_inc(ctx2_landed, 16)
                pool.wait_ge(*after("ring_room", l))
                for r, i in [(r, i) for r in ROUNDS_OF[l] for i in range(2)]:
                    q0 = r * ROUND_HEADS + i * PH
                    with pool.Fori(0, PH // 2) as it:
                        for e in range(2):
                            pool.wait_ge(topk_done, it * 2 + (q0 + r + e + 1))
                            pool.nop(nofuse=True)
                            for j in range(GPH):
                                pool.wait_ge(slots_free, it * (2 * GPH) + (q0 * GPH + e * GPH + j + 1))
                                pool.nop(nofuse=True)
                                for x in range(GROUP):
                                    k = GROUP * j + x
                                    pool.indirect_dma_start(
                                        out=ring[:, j % SLOTS, x, :], out_offset=None, in_=A[f"uv{l}"],
                                        in_offset=bass.IndirectOffsetOnAxis(ap=idx[:, e, k:k + 1], axis=0),
                                    ).then_inc(ring_landed[j % SLOTS], 16)

        @block.tensor
        def _(pe):
            mm_ = nc.tensor.matmul
            free = {b: None for b in range(8)}
            turn = [0]
            kept = set()
            seen = set()

            def new_bank(*key):
                while turn[0] % 7 in kept:
                    turn[0] += 1
                b = turn[0] % 7
                turn[0] += 1
                if free[b] is not None:
                    pe.wait_ge(*after(*free[b]))
                free[b] = ("ev",) + key
                st.at[("bank",) + key] = b
                return b

            def weights(name, k):
                n = BLOCK_AT[name]
                if n not in seen:
                    seen.add(n)
                    pe.wait_ge(w_landed[SLOT[n][0]], 16 * SLOT[n][1])
                return n, block_ap(n, k)

            def transposes(key, t, src, n=8, per=4):
                for half in range((n + per - 1) // per):
                    b = new_bank(*key, t, half)
                    m = min(per, n - half * per)
                    for k in range(m):
                        ins = nc.tensor.transpose(bank[:, b, k * P:(k + 1) * P],
                                                  src[:, (half * per + k) * P:(half * per + k + 1) * P], ident)
                    ins.then_inc(sems["pe"], done("pe", ("mm",) + key + (t, half)))

            def natural(l, name, tiles, src, k, width, cols=None, part=0, last=True, beside=None):
                n, w = weights((l, name), k)
                c0, c1 = cols or (0, width)
                for t in tiles:
                    if beside is not None and t == tiles[len(tiles) // 2]:
                        take_beside(beside)
                    b = new_bank(l, name, t, part)
                    for kk in range(k):
                        ins = mm_(bank[:, b, 0:c1 - c0], src(kk, t), w[:, kk, c0:c1], start=kk == 0, stop=kk == k - 1)
                    ev = [("mm", l, name, t, part)]
                    if t == tiles[-1] and c1 == width and last:
                        ev.append(("w", n))
                    ins.then_inc(sems["pe"], done("pe", *ev))

            def feature(l, name, chunks, src, k, ncols, last=True):
                n, w = weights((l, *name) if isinstance(name, tuple) else (l, name), k)
                for c in range(chunks):
                    b = new_bank(l, name, c)
                    for kk in range(k):
                        ins = mm_(bank[:, b, 0:ncols], w[:, kk, c * P:(c + 1) * P], src(kk), start=kk == 0, stop=kk == k - 1)
                    ev = [("mm", l, name, c)]
                    if c == chunks - 1:
                        ev.append(("w", n))
                    ins.then_inc(sems["pe"], done("pe", *ev))

            def modulations(blocks):
                for kind, (l, nb) in mod_pieces(blocks):
                    if kind == "sum":
                        pe.wait_ge(*after("parts", l, nb))
                        b = new_bank("mod", l, nb)
                        mm_(bank[0:2, b, :], const("add4"), modparts[:, :], start=True, stop=True)\
                            .then_inc(sems["pe"], done("pe", ("mm", "mod", l, nb)))
                        yield
                        continue
                    n, w = weights((l, "mod", nb), KC)
                    mb = MOD_ORDER.index((l, nb))
                    if kind == "low" and mb:
                        pe.wait_ge(*after("parts", *MOD_ORDER[mb - 1]))
                    for j in range(4):
                        kk = j + (4 if kind == "high" else 0)
                        cond = silc[:, 4 * kk + 2 * (l // 2):][:, 0:32]
                        mm_(bank[32 * j:32 * j + 32, 7, :], cond, w[:, kk, :], start=kind == "low", stop=False, skip_group_check=True)
                    if kind == "high":
                        for j in range(4):
                            ch = PT_["mod_b"][0] + l * MODC + 4 * nb + j
                            ins = mm_(bank[32 * j:32 * j + 32, 7, j * P:(j + 1) * P], params[:, ch:ch + 1].broadcast_to([P, 32]), ident,
                                      start=False, stop=True, skip_group_check=True)
                        ins.then_inc(sems["pe"], done("pe", ("mm", "parts", l, nb), ("w", n)))
                    yield

            pe.wait_ge(consts_landed, 16)
            pe.wait_ge(*after("silc"))
            for _ in modulations(MODS_FIRST):
                pass

            for l in range(LAYERS):
                tiles = LT[l]
                for t in tiles:
                    pe.wait_ge(*after("xn", l, t))
                    transposes((l, "xT"), t, xn[:, t, :])
                pe.wait_ge(*after("ev", l, "xT", tiles[-1], 0))
                pe.wait_ge(*after("ev", l, "xT", tiles[-1], 1))
                xs = lambda kk, t: xT[:, kk, t * P:(t + 1) * P]
                beside = modulations(MODS_BESIDE[l]) if l < 3 else None

                def take_beside(step):
                    if step < len(MOD_SHARE[l]):
                        for _ in range(MOD_SHARE[l][step]):
                            next(beside)

                if l == 0:
                    feature(0, "qk", 4, lambda kk: xT[:, kk, :], KC, TOK)
                    n, w = weights((0, "gates"), KC)
                    b = new_bank(0, "gnat")
                    for t in tiles:
                        for kk in range(KC):
                            ins = mm_(bank[:, b, t * 16:t * 16 + 16], xT[:, kk, t * P:(t + 1) * P], w[:, kk, :], start=kk == 0, stop=kk == KC - 1)
                    ins.then_inc(sems["pe"], done("pe", ("mm", 0, "gnat"), ("w", n)))
                    natural(0, "v", tiles, xs, KC, 512, beside=0)
                    pe.wait_ge(*after("ev", 0, "gnat"))
                    for g in range(4):
                        b = new_bank(0, "gates", g)
                        for t in tiles:
                            ins = nc.tensor.transpose(bank[0:4, b, t * P:(t + 1) * P], gnat[:, t, 4 * g:4 * g + 4], ident)
                        ins.then_inc(sems["pe"], done("pe", ("mm", 0, "gates", g)))
                    for n_, name in enumerate(("o", "dq", "dk", "dv")):
                        natural(0, name, tiles, xs, KC, 512, beside=1 + n_)
                    dqn = xn
                    for t in tiles:
                        pe.wait_ge(*after("roped", t))
                        transposes((0, "dqkT"), t, dqn[:, t, :])
                    pe.wait_ge(*after("gate_rows"))
                    b = new_bank(0, "gcols")
                    i = 0
                    for q in range(2):
                        for d in range(2):
                            rows_ = arena[0:4, (GW + 3072 if q else GW + 2048) + d * 512:][:, 0:512]
                            for t in range(4):
                                ins = nc.tensor.transpose(bank[:, b, i * 4:i * 4 + 4], rows_[:, t * P:(t + 1) * P], ident[0:4, 0:4])
                                i += 1
                    ins.then_inc(sems["pe"], done("pe", ("mm", 0, "gcols")))
                    qk = v3(QKT, 4, TOK)
                    vml = v4(VML, 4, 4, 129)
                    mrow = arena[0:4, MROW:MROW + 1024].rearrange("p (a b) -> p a b", a=2)
                    selr = consts[0:4, CT["sel"][0]:CT["sel"][0] + 512].rearrange("p (h c) -> p h c", h=4)
                    pe.wait_ge(*after("qkT", 3))
                    pe.wait_ge(*after("vml_ones"))
                    pe.wait_ge(*after("ev", 0, "v", 3, 0))
                    for h in range(4):
                        o = 64 * (h % 2)
                        for s in range(4):
                            b = new_bank(0, "A", h, s)
                            mm_(bank[:, b, :], qk[o:o + 64, 2 + h // 2, s * P:(s + 1) * P], qk[o:o + 64, h // 2, :], start=True, stop=True)\
                                .then_inc(sems["pe"], done("pe", ("mm", 0, "A", h, s)))
                        for d in range(2):
                            b = new_bank(0, "M", h, d)
                            mm_(bank[:, b, :], selr[:, h, :], mrow[:, d, :], start=True, stop=True)\
                                .then_inc(sems["pe"], done("pe", ("mm", 0, "M", h, d)))
                        for d in range(2):
                            wt = v3(EW1 if d else EW0, 4, TOK)
                            take_beside(5 + 2 * h + d)
                            pe.wait_ge(*after("WT", h, d))
                            for tp in range(2):
                                b = new_bank(0, "N", h, d, tp)
                                for t in (2 * tp, 2 * tp + 1):
                                    src = SOURCES[d][t]
                                    for s in src:
                                        ins = mm_(bank[:, b, (t % 2) * 129:(t % 2) * 129 + 129], wt[:, s, t * P:(t + 1) * P],
                                                  vml[:, s, h, :], start=s == src[0], stop=s == src[-1])
                                ins.then_inc(sems["pe"], done("pe", ("mm", 0, "N", h, d, tp)))
                    dqT, dkT = v3(DQT, 4, TOK), v3(DKT, 4, TOK)
                    dv = v3(DV, 4, 512)
                    pe.wait_ge(*after("ev", 0, "dqkT", 3, 0))
                    pe.wait_ge(*after("ev", 0, "dqkT", 3, 1))
                    pe.wait_ge(*after("ev", 0, "dv", 3, 0))
                    for step in range(16 + 4):
                        if step < 16:
                            i = step
                            t, h = i // 4, i % 4
                            nkt = 2 if t < 2 else 4
                            for m in range(2):
                                b = new_bank(0, "S", t, h, m)
                                mm_(bank[:, b, 0:nkt * P], dqT[64 * m:64 * m + 64, h, t * P:(t + 1) * P],
                                    dkT[64 * m:64 * m + 64, h, 0:nkt * P], start=True, stop=True)\
                                    .then_inc(sems["pe"], done("pe", ("mm", 0, "S", t, h, m)))
                        take_beside(13 + step)
                        if 0 <= step - 3 < 16:
                            i = step - 3
                            nkt = 2 if i < 8 else 4
                            pe.wait_ge(*after("Pr", 0, i))
                            b = new_bank(0, "PT", i)
                            pr = v(ATS + (i % 3) * 1024, 512)
                            for kk in range(nkt):
                                ins = nc.tensor.transpose(bank[:, b, kk * P:(kk + 1) * P], pr[:, kk * P:(kk + 1) * P], ident)
                            ins.then_inc(sems["pe"], done("pe", ("mm", 0, "PT", i)))
                        if 0 <= step - 4 < 16:
                            i = step - 4
                            h = i % 4
                            nkt = 2 if i < 8 else 4
                            b = new_bank(0, "O", i)
                            pe.wait_ge(*after("ev", 0, "PT", i))
                            prT = v3(ATS + 3072 + (i % 2) * 512, 4, P)
                            for kk in range(nkt):
                                ins = mm_(bank[:, b, 0:P], prT[:, kk, :], dv[:, kk, h * P:(h + 1) * P], start=kk == 0, stop=kk == nkt - 1)
                            ins.then_inc(sems["pe"], done("pe", ("mm", 0, "O", i)))
                    assert next(beside, None) is None
                    mix_off = MIX
                if l == 1:
                    natural(1, "q0", LAT, xs, KC, 512, beside=0)
                    natural(1, "q1", LAT, xs, KC, 512, beside=1)
                    natural(1, "kv", tiles, xs, KC, 512, beside=2)
                    qn, kn = v3(L1_QN, 2, 1024), v3(L1_KN, 4, 256)
                    for t in LAT:
                        pe.wait_ge(*after("q_roped", t))
                        transposes((1, "qT"), t, qn[:, t - 2, :])
                    for t in tiles:
                        pe.wait_ge(*after("k_roped", t))
                        transposes((1, "kT"), t, kn[:, t, :], n=2)
                    qT1, kT1, v1 = v3(L1_QT, 8, 256), v3(L1_KT, 2, TOK), v3(L1_V, 4, 256)
                    pe.wait_ge(*after("ev", 1, "qT", 3, 1))
                    pe.wait_ge(*after("ev", 1, "qT", 3, 0))
                    pe.wait_ge(*after("ev", 1, "kT", 3, 0))
                    for step in range(32 + 3):
                        if step < 32:
                            i = step
                            t, c, sd = i // 16, (i % 16) // 2, i % 2
                            b = new_bank(1, "S", i)
                            mm_(bank[:, b, :], qT1[64 * sd:64 * sd + 64, c, t * P:(t + 1) * P], kT1[64 * sd:64 * sd + 64, c // 4, :],
                                start=True, stop=True).then_inc(sems["pe"], done("pe", ("mm", 1, "S", i)))
                            take_beside(3 + step)
                        if 0 <= step - 2 < 32:
                            i = step - 2
                            pe.wait_ge(*after("ev", 1, "S", i))
                            b = new_bank(1, "PT", i)
                            pr = v(L1_P + (i % 2) * 512, 512)
                            for kk in range(4):
                                ins = nc.tensor.transpose(bank[:, b, kk * P:(kk + 1) * P], pr[:, kk * P:(kk + 1) * P], ident)
                            ins.then_inc(sems["pe"], done("pe", ("mm", 1, "PT", i)))
                        if 0 <= step - 3 < 32:
                            i = step - 3
                            c, sd = (i % 16) // 2, i % 2
                            kvh = 2 * (c // 4) + sd
                            b = new_bank(1, "O", i)
                            pe.wait_ge(*after("ev", 1, "PT", i))
                            prT = v3(L1_PT + (i % 2) * 512, 4, P)
                            for kk in range(4):
                                ins = mm_(bank[:, b, 0:64], prT[:, kk, :], v1[:, kk, kvh * 64:kvh * 64 + 64], start=kk == 0, stop=kk == 3)
                            ins.then_inc(sems["pe"], done("pe", ("mm", 1, "O", i)))
                    assert next(beside, None) is None
                    mix_off = MIX
                if l == 2:
                    natural(2, "zq", LAT, xs, KC, 384, beside=0)
                    natural(2, "zkv", tiles, xs, KC, 320, beside=1)
                    z = v3(L2_Z, 4, 704)
                    for t in tiles:
                        if t in LAT:
                            pe.wait_ge(*after("zq_n", t))
                            transposes((2, "cqT"), t, z[:, t, 0:384], n=3)
                        pe.wait_ge(*after("zkv_n", t))
                        transposes((2, "ckvT"), t, z[:, t, 384:640], n=2)
                        pe.wait_ge(*after("kr", t))
                        transposes((2, "krT"), t, v3(L2_QR, 4, P)[:, t, :], n=1)
                    cqT, ckvT = v3(L2_CQT, 3, 256), v3(L2_CKVT, 2, TOK)
                    for t in tiles:
                        if t in LAT:
                            pe.wait_ge(*after("ev", 2, "cqT", t, 0))
                        pe.wait_ge(*after("ev", 2, "ckvT", t, 0))
                        pe.wait_ge(*after("ev", 2, "krT", t, 0))
                    feature(2, "uqn", 8, lambda kk: cqT[:, kk, :], 3, 256)
                    take_beside(2)
                    natural(2, "uqr", LAT, lambda kk, t: cqT[:, kk, (t - 2) * P:(t - 1) * P], 3, 512)
                    feature(2, "ukn", 8, lambda kk: ckvT[:, kk, :], 2, TOK)
                    for part in range(2):
                        natural(2, "uv", tiles, lambda kk, t: ckvT[:, kk, t * P:(t + 1) * P], 2, 1024,
                                cols=(part * 512, part * 512 + 512), part=part)
                    qr = v3(L2_QR, 2, 512)
                    for t in LAT:
                        pe.wait_ge(*after("qr_roped", t))
                        transposes((2, "qrT"), t, qr[:, t - 2, :], n=4)
                    qnT, qrT, knT, krT, v2 = (v3(L2_QNT, 8, 256), v3(L2_QRT, 4, 256), v3(L2_KNT, 8, TOK),
                                              v(L2_KRT, TOK), v3(L2_V, 4, 1024))
                    pe.wait_ge(*after("ev", 2, "qrT", 3, 0))
                    for ev in (("uqn", 6), ("uqn", 7), ("ukn", 6), ("ukn", 7)):
                        pe.wait_ge(*after("ev", 2, *ev))
                    for t_ in tiles:
                        pe.wait_ge(*after("ev", 2, "uv", t_, 1))
                        pe.wait_ge(*after("ev", 2, "uv", t_, 0))
                    for step in range(16 + 3):
                        if step < 16:
                            i = step
                            t, h = i // 8, i % 8
                            b = new_bank(2, "S", i)
                            o = 64 * (h % 2)
                            mm_(bank[:, b, :], qnT[:, h, t * P:(t + 1) * P], knT[:, h, :], start=True, stop=False)
                            mm_(bank[:, b, :], qrT[o:o + 64, h // 2, t * P:(t + 1) * P], krT[o:o + 64, :], start=False, stop=True)\
                                .then_inc(sems["pe"], done("pe", ("mm", 2, "S", i)))
                            take_beside(3 + step)
                        if 0 <= step - 2 < 16:
                            i = step - 2
                            pe.wait_ge(*after("ev", 2, "S", i))
                            b = new_bank(2, "PT", i)
                            pr = v(L2_P + (i % 2) * 512, 512)
                            for kk in range(4):
                                ins = nc.tensor.transpose(bank[:, b, kk * P:(kk + 1) * P], pr[:, kk * P:(kk + 1) * P], ident)
                            ins.then_inc(sems["pe"], done("pe", ("mm", 2, "PT", i)))
                        if 0 <= step - 3 < 16:
                            i = step - 3
                            h = i % 8
                            b = new_bank(2, "O", i)
                            pe.wait_ge(*after("ev", 2, "PT", i))
                            prT = v3(L2_PT + (i % 2) * 512, 4, P)
                            for kk in range(4):
                                ins = mm_(bank[:, b, 0:P], prT[:, kk, :], v2[:, kk, h * P:(h + 1) * P], start=kk == 0, stop=kk == 3)
                            ins.then_inc(sems["pe"], done("pe", ("mm", 2, "O", i)))
                    assert next(beside, None) is None
                    mix_off = L2_MIX
                out_tiles = MIX_TILES[l]
                if l < 3:
                    m0 = 0 if l == 0 else 2
                    mixv = v3(mix_off, len(out_tiles), D)
                    for t in out_tiles:
                        pe.wait_ge(*after("mix", l, t))
                        transposes((l, "mT"), t, mixv[:, t - m0, :])
                    for t in out_tiles:
                        pe.wait_ge(*after("ev", l, "mT", t, 0))
                        pe.wait_ge(*after("ev", l, "mT", t, 1))
                    ms = lambda kk, t: mixT[:, kk, t * P:(t + 1) * P]
                else:
                    for j in range(2):
                        natural(3, f"in{j}", LAT, xs, KC, 512)
                    z3, pT, yT = v3(L3_Z, 2, 1024), v3(L3_POOLT, 8, 256), v3(L3_YT, 8, 256)
                    n, w = weights((3, "band"), 2)
                    for t in LAT:
                        for j in range(2):
                            pe.wait_ge(*after("ev", 3, f"in{j}", t, 0))
                    for c in range(8):
                        b = new_bank(3, "pool", c)
                        for kk in range(2):
                            ins = mm_(bank[:, b, 0:256], z3[:, kk, c * P:(c + 1) * P], w[:, kk, (c // 2) * 256:(c // 2) * 256 + 256],
                                      start=kk == 0, stop=kk == 1)
                        ev = [("mm", 3, "pool", c)] + ([("w", n)] if c == 7 else [])
                        ins.then_inc(sems["pe"], done("pe", *ev))
                    n, w = weights((3, "grp"), 8)
                    pe.wait_ge(*after("ev", 3, "pool", 6))
                    pe.wait_ge(*after("ev", 3, "pool", 7))
                    for c in range(8):
                        b = new_bank(3, "yT", c)
                        g = c // 2
                        for kk in range(2):
                            ins = mm_(bank[:, b, 0:256], w[:, 2 * g + kk, (c % 2) * P:(c % 2) * P + P], pT[:, 2 * g + kk, :],
                                      start=kk == 0, stop=kk == 1)
                        ev = [("mm", 3, "yT", c)] + ([("w", n)] if c == 7 else [])
                        ins.then_inc(sems["pe"], done("pe", *ev))
                    pe.wait_ge(*after("ev", 3, "yT", 6))
                    pe.wait_ge(*after("ev", 3, "yT", 7))
                    ms = lambda kk, t: yT[:, kk, (t - 2) * P:(t - 1) * P]
                if l == 0:
                    for j in range(2):
                        natural(l, f"out{j}", CTX, ms, KC, 512, last=False)
                for j in range(2):
                    natural(l, f"out{j}", LAT, ms, KC, 512)

                def peer_input(r, tiles):
                    for t in tiles:
                        pe.wait_ge(*after("xnat", l, t))
                        transposes((r, "xT2"), t, xnat_of(r, t))

                def query_chunk(r, hp):
                    j, c = divmod(hp, 4)
                    n, w = weights((l, "wq", j, r), KC)
                    b = new_bank(r, "q", hp)
                    for kk in range(KC):
                        ins = mm_(bank[:, b, 0:2 * P], w[:, kk, c * P:(c + 1) * P], xT2[:, kk, :], start=kk == 0, stop=kk == KC - 1)
                        if (r, hp, kk) == (0, 0, 0):
                            ins.then_inc(slots_free, SLOTS)
                    ins.then_inc(sems["pe"], done("pe", ("mm", r, "q", hp), *([("w", n)] if c == 3 else [])))

                def key_scores(r, j):
                    for q in range(4):
                        pe.wait_ge(*after("ev", r, "q", 4 * j + q))
                    for i in range(2):
                        b = new_bank(r, "sc", i, j)
                        for q in range(4):
                            hp = 4 * j + q
                            ins = mm_(bank[:, b, q * P:(q + 1) * P], qT[:, hp % 8, i * P:(i + 1) * P], keys_sb[:, hp, :],
                                      start=True, stop=True)
                        ins.then_inc(sems["pe"], done("pe", ("mm", r, "sc", i, j)))

                def first_scores(r, tiles):
                    for t in tiles:
                        pe.wait_ge(*after("ev", r, "xT2", t, 0))
                        pe.wait_ge(*after("ev", r, "xT2", t, 1))
                    for j in range(2):
                        for c in range(4):
                            query_chunk(r, 4 * j + c)
                        if j == 0:
                            pe.wait_ge(keys_landed, 16 * (l + 1))
                        key_scores(r, j)

                def peer_sum(r, i):
                    q0 = r * ROUND_HEADS + i * PH
                    yb = 2 * i
                    for hf in range(2):
                        pe.wait_ge(*after(*free[yb + hf]))
                        free[yb + hf] = ("y_taken", r, i)
                        mm_(bank[:, yb + hf, :], ident, const("zero"), start=True, stop=False, skip_group_check=True)

                    def two_heads(it, then=None):
                        for e in range(2):
                            for j in range(GPH):
                                pe.wait_ge(diag_done, it * (2 * GPH) + (q0 * GPH + e * GPH + j + 1))
                                for x in range(GROUP):
                                    for hf in range(2):
                                        ins = mm_(bank[:, yb + hf, :], diag[:, j % SLOTS, x, :],
                                                  ring[:, j % SLOTS, x, D + hf * 512:D + hf * 512 + 512],
                                                  start=False, stop=True, skip_group_check=True)
                                ins.then_inc(slots_free, 1)
                                if then:
                                    then(e * GPH + j)

                    def later_scores(g):
                        if g < 8:
                            query_chunk(r, 8 + g)
                        if g in SCORES_AFTER:
                            key_scores(r, SCORES_AFTER[g])

                    if i == 0:
                        kept.update((yb, yb + 1))
                        two_heads(0, later_scores)
                        kept.clear()
                    with pe.Fori(1 - i, PH // 2) as it:
                        two_heads(it)

                peer_input(ROUNDS_OF[l][0], ROUNDS[ROUNDS_OF[l][0]][1])
                for r in ROUNDS_OF[l]:
                    first_scores(r, ROUNDS[r][1])
                    peer_sum(r, 0)
                    if r == 0:
                        peer_input(1, LAT)
                    peer_sum(r, 1)

        @block.scalar
        def _(act):
            a = nc.scalar
            AF = a.activation

            def b_(*key):
                act.wait_ge(*after("mm", *key))
                return known.get(("bank",) + key, 0)

            def ev(ins, *key):
                ins.then_inc(sems["act"], done("act", ("ev",) + key))

            def copy_T(key, t, dst, half, n=4):
                b = b_(*key, t, half)
                ev(a.copy(dst, bank3(b, n, P)), *key, t, half)

            act.wait_ge(params_landed, 16)
            AF(silc[:, :], par("cond"), ACT.Silu).then_inc(sems["act"], done("act", ("silc",)))

            def take_mod(kind, lb):
                l, nb = lb
                mb = MOD_ORDER.index((l, nb))
                if kind == "high":
                    act.wait_ge(*after("mm", "parts", l, nb))
                    a.copy(modparts[:, :], bank[:, 7, :]).then_inc(sems["act"], done("act", ("parts", l, nb)))
                if kind == "sum":
                    b = b_("mod", l, nb)
                    if mb >= 2:
                        act.wait_ge(mods_stored[mb % 2], 16 * (mb // 2))
                    ev(a.copy(modst[:, mb % 2, :], bank[0:2, b, :]), "mod", l, nb)
                    act.wait_ge(*after("ev", "mod", l, nb))
                    dst = mods[l, :, :].rearrange("(s m) d -> s (m d)", s=2)[:, nb * 512:(nb + 1) * 512]
                    act.dma_start(dst, modst[:, mb % 2, :]).then_inc(mods_stored[mb % 2], 16)

            for kind, m in mod_pieces(MODS_FIRST):
                take_mod(kind, m)
            act.wait_ge(*after("lam_dots"))
            AF(lamc[:, 0:2], lamc[:, 0:2], ACT.Exp).then_inc(sems["act"], done("act", ("lam_exp",)))
            for l in range(LAYERS):
                tiles = LT[l]

                def follow(step):
                    if step < len(MOD_SHARE[l]):
                        for piece in mod_ready(l, step):
                            take_mod(*piece)

                for t in tiles:
                    copy_T((l, "xT"), t, xT[:, 0:4, t * P:(t + 1) * P], 0)
                if l == 0:
                    raw = v4(RAW, 4, 2, 258)
                    qk = v3(QKT, 4, TOK)
                    for c in range(4):
                        act.wait_ge(*after("conv", c))
                        AF(qk[:, c, :], qk[:, c, :], ACT.Silu).then_inc(sems["act"], done("act", ("qkT", c)))
                    vml = v4(VML, 4, 4, 129)
                    for t in tiles:
                        b = b_(0, "v", t, 0)
                        ev(a.copy(vml[:, t, :, 0:128], bank3(b, 4, P)), 0, "v", t, 0)
                    follow(0)
                    tmp = arena[0:4, GW + 2048:GW + 3072]
                    act.wait_ge(*after("absz"))
                    AF(tmp, tmp, ACT.Exp, scale=-1.0)
                    act.drain()
                    AF(tmp, tmp, ACT.Ln, bias=1.0).then_inc(sems["act"], done("act", ("softplus",)))
                    for t in tiles:
                        b = b_(0, "o", t, 0)
                        ev(AF(v(OSIG + t * 512, 512), bank[:, b, :], ACT.Sigmoid), 0, "o", t, 0)
                    for step in (1, 2, 3):
                        follow(step)
                    for t in tiles:
                        b = b_(0, "dv", t, 0)
                        ev(a.copy(v(DV + t * 512, 512), bank[:, b, :]), 0, "dv", t, 0)
                    follow(4)
                    for t in tiles:
                        copy_T((0, "dqkT"), t, v3(DQT, 4, TOK)[:, :, t * P:(t + 1) * P], 0)
                    act.wait_ge(*after("m_rows"))
                    AF(arena[0:4, GW + 3072:GW + 4096], arena[0:4, GW + 1024:GW + 2048], ACT.Exp, scale=-1.0)\
                        .then_inc(sems["act"], done("act", ("floor_rows",)))
                    ats = v3(ATS, 4, TOK)
                    for h in range(4):
                        for s in range(4):
                            b = b_(0, "A", h, s)
                            if s == 0:
                                if h:
                                    act.wait_ge(*after("WT", h - 1, 1))
                                else:
                                    act.wait_ge(*after("ev", 0, "gcols"))
                            ev(AF(ats[:, s, :], bank[:, b, :], ACT.Copy, scale=SCALE64), 0, "A", h, s)
                        for d in range(2):
                            wt = v3(EW1 if d else EW0, 4, TOK)
                            dm = v3(DMASK, 4, P)
                            b = b_(0, "M", h, d)
                            act.wait_ge(*after("dmask", h, d))
                            if h:
                                act.wait_ge(*after("mm", 0, "N", h - 1, d, 1))
                            for s in range(4):
                                bias = gcols[:, (d * 4 + s) * 4 + h:(d * 4 + s) * 4 + h + 1]
                                ins = AF(wt[:, s, s * P:(s + 1) * P], dm[:, s, :], ACT.Exp, bias=bias)
                                for t0, t1 in OFF_DIAGONAL[d][s]:
                                    ins = AF(wt[:, s, t0 * P:t1 * P], bank[:, b, t0 * P:t1 * P], ACT.Exp, bias=bias)
                            ins.then_inc(sems["act"], done("act", ("ev", 0, "M", h, d), ("E", h, d)))
                            follow(5 + 2 * h + d)
                    for step in range(16 + 4):
                        if 0 <= step - 1 < 16:
                            i = step - 1
                            t, h = i // 4, i % 4
                            nk = 256 if t < 2 else 512
                            act.wait_ge(*after("smax", 0, i))
                            for m in range(2):
                                b = b_(0, "S", t, h, m)
                                c = 8 * (i % 4) + m
                                ev(AF(v(ATS + (i % 3) * 1024 + m * 512, nk), bank[:, b, 0:nk], ACT.Exp, bias=small[:, c:c + 1],
                                      scale=SCALE64, accum_out=small[:, c + 2:c + 3]), 0, "S", t, h, m)
                        follow(13 + step)
                        if 0 <= step - 3 < 16:
                            i = step - 3
                            nk = 256 if i < 8 else 512
                            b = b_(0, "PT", i)
                            ev(a.copy(v(ATS + 3072 + (i % 2) * 512, nk), bank[:, b, 0:nk]), 0, "PT", i)
                        if 0 <= step - 4 < 16:
                            i = step - 4
                            t, h = i // 4, i % 4
                            b = b_(0, "O", i)
                            ev(a.copy(v3(MIX, 4, D)[:, t, 512 + h * P:512 + (h + 1) * P], bank[:, b, 0:P]), 0, "O", i)
                if l == 1:
                    follow(0)
                    follow(1)
                    for t in tiles:
                        b = b_(1, "kv", t, 0)
                        act.wait_ge(*after("k_roped", t))
                        ev(a.copy(v3(L1_V, 4, 256)[:, t, :], bank[:, b, 256:512]), 1, "kv", t, 0)
                    follow(2)
                    for t in LAT:
                        copy_T((1, "qT"), t, v3(L1_QT, 8, 256)[:, 0:4, (t - 2) * P:(t - 1) * P], 0)
                    for t in tiles:
                        copy_T((1, "kT"), t, v3(L1_KT, 2, TOK)[:, :, t * P:(t + 1) * P], 0, n=2)

                    for step in range(32 + 3):
                        if 0 <= step - 1 < 32:
                            i = step - 1
                            b = b_(1, "S", i)
                            act.wait_ge(*after("smax", 1, i))
                            c = 8 * (i % 4)
                            if i >= 2:
                                act.wait_ge(*after("mm", 1, "PT", i - 2))
                            AF(v(L1_P + (i % 2) * 512, 512), bank[:, b, :], ACT.Exp, bias=small[:, c:c + 1], scale=SCALE64,
                               accum_out=small[:, c + 1:c + 2])
                            hq = head_of(i)
                            ev(AF(small[:, c + 2:c + 3], par("sink")[:, hq:hq + 1], ACT.Exp, bias=small[:, c:c + 1]), 1, "S", i)
                        if step < 32:
                            follow(3 + step)
                        if 0 <= step - 2 < 32:
                            i = step - 2
                            b = b_(1, "PT", i)
                            ev(a.copy(v(L1_PT + (i % 2) * 512, 512), bank[:, b, :]), 1, "PT", i)
                if l == 2:
                    follow(0)
                    follow(1)
                    for c in range(8):
                        if c % 2 == 0:
                            b = b_(2, "uqn", c)
                            ev(a.copy(v3(L2_QNT, 8, 256)[:, c, :], bank[:, b, 0:256]), 2, "uqn", c)
                    follow(2)
                    for c in range(8):
                        if c % 2 == 0:
                            b = b_(2, "ukn", c)
                            ev(a.copy(v3(L2_KNT, 8, TOK)[:, c, :], bank[:, b, :]), 2, "ukn", c)
                    for part in range(2):
                        for t in tiles:
                            if t % 2 == 0:
                                b = b_(2, "uv", t, part)
                                ev(a.copy(v3(L2_V, 4, 1024)[:, t, part * 512:part * 512 + 512], bank[:, b, :]), 2, "uv", t, part)

                    for step in range(16 + 3):
                        if 0 <= step - 1 < 16:
                            i = step - 1
                            b = b_(2, "S", i)
                            act.wait_ge(*after("smax", 2, i))
                            c = 8 * (i % 4)
                            if i >= 2:
                                act.wait_ge(*after("mm", 2, "PT", i - 2))
                            ev(AF(v(L2_P + (i % 2) * 512, 512), bank[:, b, :], ACT.Exp, bias=small[:, c:c + 1], scale=SCALE_MLA,
                                  accum_out=small[:, c + 1:c + 2]), 2, "S", i)
                        if step < 16:
                            follow(3 + step)
                        if 0 <= step - 2 < 16:
                            i = step - 2
                            b = b_(2, "PT", i)
                            ev(a.copy(v(L2_PT + (i % 2) * 512, 512), bank[:, b, :]), 2, "PT", i)
                if l == 3:
                    for t in LAT:
                        b = b_(3, "in0", t, 0)
                        ev(a.copy(v3(L3_Z, 2, 1024)[:, t - 2, 0:512], bank[:, b, :]), 3, "in0", t, 0)
                    for c in range(0, 8, 2):
                        b = b_(3, "pool", c)
                        ev(a.copy(v3(L3_POOLT, 8, 256)[:, c, :], bank[:, b, 0:256]), 3, "pool", c)
                    for c in range(0, 8, 2):
                        b = b_(3, "yT", c)
                        ev(AF(v3(L3_YT, 8, 256)[:, c, :], bank[:, b, 0:256], ACT.Copy, scale=par("pool_scale")[:, c:c + 1]), 3, "yT", c)
                out_tiles = MIX_TILES[l]
                if l < 3:
                    for t in out_tiles:
                        copy_T((l, "mT"), t, mixT[:, 0:4, t * P:(t + 1) * P], 0)

                def peer_input(r, tiles):
                    for t in tiles:
                        copy_T((r, "xT2"), t, xT2[:, 0:4, (t % 2) * P:(t % 2 + 1) * P], 0)

                def exps(wait):
                    act.wait_ge(topk_done, wait)
                    act.nop(nofuse=True)
                    AF(ex[:, :], cv[:, :], ACT.Exp, bias=neg[:, :], accum_out=es[:, :]).then_inc(exp_done, 1)

                def take_query(r, hp):
                    if hp % 2 == 0:
                        b = b_(r, "q", hp)
                        ev(a.copy(qT[:, hp % 8, :], bank[:, b, 0:2 * P]), r, "q", hp)

                def take_scores(r, j):
                    b = b_(r, "sc", 0, j)
                    ev(a.copy(scores[:, 2 * j:2 * j + 2, :].rearrange("p a b -> p (a b)"), bank[:, b, :]), r, "sc", 0, j)

                def first_scores(r):
                    for j in range(2):
                        if r == 1 and j == 1:
                            act.wait_ge(*after("xnat_moved"))
                        for c in range(4):
                            take_query(r, 4 * j + c)
                        take_scores(r, j)
                        if j == 0:
                            act.wait_ge(*after("ev", r, "sc", 0, 0))
                            a.copy(head_scores[:, :], scores[:, 0, :]).then_inc(head_copied, 1)
                    exps(r * ROUND_HEADS + r + 1)
                    act.wait_ge(*after("ev", r, "sc", 0, 1))

                def peer_weights(r, i):
                    q0 = r * ROUND_HEADS + i * PH

                    def two_heads(it, then=None):
                        for e in range(2):
                            act.wait_ge(topk_done, it * 2 + (q0 + r + e + 1))
                            act.nop(nofuse=True)
                            a.copy(head_scores[:, :], scores[:, ds(it * 2 + (i * PH + e + 1), 1), :].rearrange("p a b -> p (a b)"))\
                                .then_inc(head_copied, 1)
                            for j in range(GPH):
                                s = j % SLOTS
                                act.wait_ge(dots_done, it * (2 * GPH) + (q0 * GPH + e * GPH + j + 1))
                                act.nop(nofuse=True)
                                AF(gel[:, s, :], dot[:, s, :], ACT.Gelu)
                                act.drain()
                                for x in range(GROUP):
                                    AF(wgt[:, s, x:x + 1], gel[:, s, x:x + 1], ACT.Copy, scale=gate[:, e, GROUP * j + x:GROUP * j + x + 1])
                                act.drain()
                                for x in range(GROUP):
                                    ins = AF(diag[:, s, x, :], ident, ACT.Copy, scale=wgt[:, s, x:x + 1])
                                ins.then_inc(diag_done, 1)
                                if j == 1:
                                    exps(it * 2 + (q0 + r + e + 2))
                                if then:
                                    then(e * GPH + j)

                    def later_scores(g):
                        if 0 <= g - CHUNK_LAG < 8:
                            take_query(r, 8 + g - CHUNK_LAG)
                        if g - SCORES_LAG in SCORES_AFTER:
                            take_scores(r, SCORES_AFTER[g - SCORES_LAG])

                    if i == 0:
                        two_heads(0, later_scores)
                        act.wait_ge(*after("ev", r, "sc", 0, 3))
                        act.wait_ge(*after("ev", r, "sc", 1, 3))
                        act.wait_ge(*after("pad_scores", r))
                    with act.Fori(1 - i, PH // 2) as it:
                        two_heads(it)

                peer_input(ROUNDS_OF[l][0], ROUNDS[ROUNDS_OF[l][0]][1])
                for r in ROUNDS_OF[l]:
                    first_scores(r)
                    peer_weights(r, 0)
                    if r == 0:
                        peer_input(1, LAT)
                    peer_weights(r, 1)

        @block.vector
        def _(dve):
            V = nc.vector

            def b_(*key):
                dve.wait_ge(*after("mm", *key))
                return known.get(("bank",) + key, 0)

            def ev(ins, *key, more=()):
                ins.then_inc(sems["dve"], done("dve", ("ev",) + key, *more))

            def sig(ins, *events):
                ins.then_inc(sems["dve"], done("dve", *events))

            def row(l, name, s):
                n = ROW_AT[(l, name, s)]
                dve.wait_ge(r_landed[n % RSLOTS], 16 * (n // RSLOTS + 1))
                return n, rring[:, n % RSLOTS, :]

            def squares(src, sq, ss):
                V.tensor_tensor_reduce(out=sq, in0=src, in1=src, scale=1.0, scalar=0.0, op0=ALU.mult, op1=ALU.add, accum_out=ss)

            def rsqrt(x, scale, eps):
                n = x.shape[-1]
                y, t_ = newton[:, 0:n], newton[:, 32:32 + n]
                dve.drain()
                V.tensor_scalar(x, x, scale, eps, ALU.mult, ALU.add)
                dve.drain()
                V.tensor_scalar(t_.bitcast(U32), x.bitcast(U32), 1, None, ALU.logical_shift_right)
                dve.drain()
                V.tensor_scalar(y.bitcast(U32), t_.bitcast(U32), -1.0, float(0x5F3759DF), ALU.mult, ALU.add)
                dve.drain()
                for step in range(3):
                    V.scalar_tensor_tensor(out=t_, in0=y, scalar=-0.5, in1=y, op0=ALU.mult, op1=ALU.mult)
                    dve.drain()
                    V.tensor_tensor(t_, t_, x, ALU.mult)
                    dve.drain()
                    V.scalar_tensor_tensor(out=y if step < 2 else x, in0=t_, scalar=1.5, in1=y, op0=ALU.add, op1=ALU.mult)
                    dve.drain()

            def modulated(l, tiles, s, names, dst, event, norm):
                g_, sc_, sh_ = names
                rows_ = []
                if norm:
                    dve.drain()
                    for t in tiles:
                        squares(H[:, t, :], dst[t - tiles[0]], small[:, 32 + t:33 + t])
                    rsqrt(small[:, 32 + tiles[0]:33 + tiles[-1]], 1.0 / D, EPS)
                if norm:
                    ng, g = row(l, g_, s)
                    rows_.append(ng)
                nsc, sc = row(l, sc_, s)
                nsh, sh = row(l, sh_, s)
                rows_ += [nsc, nsh]
                if norm:
                    V.scalar_tensor_tensor(out=sc, in0=sc, scalar=1.0, in1=g, op0=ALU.add, op1=ALU.mult)
                else:
                    V.tensor_scalar(sc, sc, 1.0, None, ALU.add)
                dve.drain()
                for t in tiles:
                    y = dst[t - tiles[0]]
                    if norm:
                        V.scalar_tensor_tensor(out=y, in0=H[:, t, :], scalar=small[:, 32 + t:33 + t], in1=sc, op0=ALU.mult, op1=ALU.mult)
                    else:
                        V.tensor_tensor(y, H[:, t, :], sc, ALU.mult)
                    dve.drain()
                    evs = [(event, l, t)]
                    if t == tiles[-1]:
                        evs += [("row", n) for n in rows_]
                    sig(V.tensor_tensor(y, y, sh, ALU.add), *evs)

            def layernorm(l, which):
                ng, g = row(l, "lng", which)
                nb, b2 = row(l, "lnb", which)
                for t in LAT:
                    for c in range(2):
                        V.bn_stats(small[:, 40 + 6 * c:46 + 6 * c], H[:, t, c * 512:(c + 1) * 512])
                    dve.drain()
                    V.bn_aggr(small[:, 32 + 2 * (t - 2):34 + 2 * (t - 2)], small[:, 40:52])
                    dve.drain()
                V.tensor_copy(small[:, 56:58], small[:, 33:37:2])
                rsqrt(small[:, 56:58], 1.0, LN_EPS)
                for t in LAT:
                    x = H[:, t, :]
                    V.tensor_scalar(x, x, small[:, 32 + 2 * (t - 2):33 + 2 * (t - 2)], small[:, 54 + t:55 + t], ALU.subtract, ALU.mult)
                    dve.drain()
                    V.tensor_tensor(x, x, g, ALU.mult)
                    dve.drain()
                    evs = [("ln", l, which, t)] + ([("row", ng), ("row", nb)] if t == 3 else [])
                    sig(V.tensor_tensor(x, x, b2, ALU.add), *evs)
                dve.drain()

            def rope(dst, src, t, groups, tmp):
                cos = const("cos")[:, (t - 2) * 32:(t - 1) * 32].unsqueeze(1).broadcast_to([P, groups, 32])
                sin = const("sin")[:, (t - 2) * 32:(t - 1) * 32].unsqueeze(1).broadcast_to([P, groups, 32])
                ta, tb = tmp
                V.tensor_tensor(dst[:, :, 0, :], src[:, :, 0, :], cos, ALU.mult)
                V.tensor_tensor(ta, src[:, :, 1, :], sin, ALU.mult)
                V.tensor_tensor(dst[:, :, 1, :], src[:, :, 0, :], sin, ALU.mult)
                V.tensor_tensor(tb, src[:, :, 1, :], cos, ALU.mult)
                dve.drain()
                V.tensor_tensor(dst[:, :, 0, :], dst[:, :, 0, :], ta, ALU.subtract)
                return V.tensor_tensor(dst[:, :, 1, :], dst[:, :, 1, :], tb, ALU.add)

            def groups32(ap):
                return ap.rearrange("p (g a b) -> p g a b", a=2, b=32)

            def copy_T(key, t, dst, half, n=4):
                b = b_(*key, t, half)
                ev(V.tensor_copy(dst, bank3(b, n, P)), *key, t, half)

            dve.wait_ge(params_landed, 16)
            lam = par("lam").rearrange("p (a b) -> p a b", a=4)
            for q in range(2):
                V.tensor_tensor_reduce(out=left[:, q * 64:(q + 1) * 64], in0=lam[:, 2 * q, :], in1=lam[:, 2 * q + 1, :], scale=1.0,
                                       scalar=0.0, op0=ALU.mult, op1=ALU.add, accum_out=lamc[:, q:q + 1])
            sig(dve.drain(), ("lam_dots",))
            dve.wait_ge(consts_landed, 16)
            dve.wait_ge(hidden_landed, 16)

            for l in range(LAYERS):
                tiles = LT[l]
                norm = l < 2
                if l == 2:
                    dve.wait_ge(ctx2_landed, 16)
                if l != 3:
                    modulated(l, CTX, 1, ("g1", "sc1", "sh1"), [xn[:, t, :] for t in CTX], "xn", norm)
                modulated(l, LAT, 0, ("g1", "sc1", "sh1"), [xn[:, t, :] for t in LAT], "xn", norm)
                for t in tiles:
                    copy_T((l, "xT"), t, xT[:, 4:8, t * P:(t + 1) * P], 1)
                if l == 0:
                    raw = v4(RAW, 4, 2, 258)
                    qk = v3(QKT, 4, TOK)
                    V.memset(raw[:, :, :, 0:1], 0.0)
                    V.memset(raw[:, :, :, 257:258], 0.0)
                    sig(V.memset(v4(VML, 4, 4, 129)[:, :, :, 128:129], 1.0), ("vml_ones",))
                    cw = par("conv_w").rearrange("p (c j) -> p c j", c=4)
                    for c in range(4):
                        b = b_(0, "qk", c)
                        ev(V.tensor_copy(raw[:, c, :, 1:257], bank3(b, 2, 256)), 0, "qk", c)
                        dve.drain()
                        y = qk[:, c, :].rearrange("p (a b) -> p a b", a=2)
                        V.tensor_scalar(y, raw[:, c, :, 0:256], cw[:, c, 0:1], par("conv_b")[:, c:c + 1], ALU.mult, ALU.add)
                        dve.drain()
                        V.scalar_tensor_tensor(out=y, in0=raw[:, c, :, 1:257], scalar=cw[:, c, 1:2], in1=y, op0=ALU.mult, op1=ALU.add)
                        dve.drain()
                        sig(V.scalar_tensor_tensor(out=y, in0=raw[:, c, :, 2:258], scalar=cw[:, c, 2:3], in1=y, op0=ALU.mult,
                                                   op1=ALU.add), ("conv", c))
                    b = b_(0, "gnat")
                    ev(V.tensor_tensor(gnat[:, :, :], bank3(b, 4, 16), par("gate_b").unsqueeze(1).broadcast_to([P, 4, 16]), ALU.add), 0, "gnat")
                    gw = arena[0:4, GW:GW + 4096].rearrange("p (q d t) -> p q d t", q=4, d=2)
                    zi, zf, tmp, fl = (gw[:, q, :, :] for q in range(4))
                    mrow = arena[0:4, MROW:MROW + 1024].rearrange("p (a b) -> p a b", a=2)
                    for g in range(4):
                        b = b_(0, "gates", g)
                        dst = (zi, zf)[g % 2]
                        if g < 2:
                            ins = V.tensor_copy(dst[:, 0, :], bank[0:4, b, :])
                        else:
                            V.tensor_copy(dst[:, 1, 0:256], bank[0:4, b, rev(0)])
                            ins = V.tensor_copy(dst[:, 1, 256:512], bank[0:4, b, rev(256)])
                        ev(ins, 0, "gates", g)
                    dve.drain()
                    sig(V.scalar_tensor_tensor(out=tmp, in0=zf, scalar=-1.0, in1=zf, op0=ALU.mult, op1=ALU.max), ("absz",))
                    V.tensor_scalar(zf, zf, 0.0, None, ALU.min)
                    dve.wait_ge(*after("softplus"))
                    dve.drain()
                    V.tensor_tensor(zf, zf, tmp, ALU.subtract)
                    V.memset(fl, 1.0)
                    dve.drain()
                    for d in range(2):
                        V.tensor_tensor_scan(tmp[:, d, :], fl[:, d, :], zf[:, d, :], 0.0, ALU.mult, ALU.add)
                    dve.drain()
                    V.tensor_tensor(zi, zi, tmp, ALU.subtract)
                    dve.drain()
                    for d in range(2):
                        V.tensor_tensor_scan(fl[:, d, :], zi[:, d, :], zi[:, d, :], 0.0, ALU.max, ALU.max)
                    dve.drain()
                    V.tensor_tensor(tmp, tmp, fl, ALU.add)
                    dve.drain()
                    V.tensor_copy(zf[:, 0, :], tmp[:, 0, :])
                    V.tensor_scalar(mrow[:, 0, :], fl[:, 0, :], -1.0, None, ALU.mult)
                    for c0 in (0, 256):
                        V.tensor_copy(zf[:, 1, c0:c0 + 256], tmp[:, 1, rev(c0)])
                        V.tensor_scalar(mrow[:, 1, c0:c0 + 256], fl[:, 1, rev(c0)], -1.0, None, ALU.mult)
                    dve.drain()
                    V.tensor_copy(tmp[:, 0, :], zi[:, 0, :])
                    V.tensor_copy(tmp[:, 1, 0:256], zi[:, 1, rev(0)])
                    sig(V.tensor_copy(tmp[:, 1, 256:512], zi[:, 1, rev(256)]), ("m_rows",))
                    rt = (v3(DMASK, 8, 32), v3(DMASK + 256, 8, 32))
                    for q, name in enumerate(("dq", "dk")):
                        for t in tiles:
                            b = b_(0, name, t, 0)
                            dst = xn[:, t, q * 512:(q + 1) * 512]
                            if t < 2:
                                ins = V.tensor_copy(dst, bank[:, b, :])
                            else:
                                ins = rope(groups32(dst), groups32(bank[:, b, :]), t, 8, rt)
                                dve.drain()
                            if q:
                                ev(ins, 0, name, t, 0, more=(("roped", t),))
                            else:
                                ev(ins, 0, name, t, 0)
                    for t in tiles:
                        copy_T((0, "dqkT"), t, v3(DKT, 4, TOK)[:, :, t * P:(t + 1) * P], 1)
                    dve.wait_ge(*after("floor_rows"))
                    sig(dve.drain(), ("gate_rows",))
                    b = b_(0, "gcols")
                    ev(V.tensor_copy(gcols[:, :], bank[:, b, 0:64]), 0, "gcols")
                    dve.drain()
                    ats = v3(ATS, 4, TOK)
                    mix = v3(MIX, 4, D)

                    def masked(h, d):
                        b = b_(0, "M", h, d)
                        if h or d:
                            dve.wait_ge(*after("E", *((h, 0) if d else (h - 1, 1))))
                        tri = const("tri")[:, d * P:(d + 1) * P].unsqueeze(1).broadcast_to([P, 4, P])
                        sig(V.tensor_tensor(v3(DMASK, 4, P), bank3(b, 4, P), tri, ALU.add), ("dmask", h, d))

                    for h in range(4):
                        for d in range(2):
                            wt = v3(EW1 if d else EW0, 4, TOK)
                            masked(h, d)
                            for s in range(4):
                                dve.wait_ge(*after("ev", 0, "A", h, s))
                            dve.wait_ge(*after("E", h, d))
                            for s in range(4):
                                for t0, t1 in [(s, s + 1)] + OFF_DIAGONAL[d][s]:
                                    ins = V.tensor_tensor(wt[:, s, t0 * P:t1 * P], wt[:, s, t0 * P:t1 * P],
                                                          ats[:, s, t0 * P:t1 * P], ALU.mult)
                            sig(ins, ("WT", h, d))
                        for d in range(2):
                            for tp in range(2):
                                b = b_(0, "N", h, d, tp)
                                nd = bank[:, b, 0:258].rearrange("p (a n) -> p a n", a=2)
                                den = small[:, 8 * tp:8 * tp + 2]
                                c = 32 + (d * 4 + 2 * tp) * 4 + h
                                V.tensor_copy(den, nd[:, :, 128])
                                dve.drain()
                                V.scalar_tensor_tensor(out=den, in0=den, scalar=-1.0, in1=den, op0=ALU.mult, op1=ALU.max)
                                dve.drain()
                                V.tensor_tensor(den, den, gcols[:, c:c + 5:4], ALU.max)
                                dve.drain()
                                V.reciprocal(den, den)
                                dve.drain()
                                for q in range(2):
                                    t = 2 * tp + q
                                    dst = mix[:, t, h * P:(h + 1) * P]
                                    if d == 0:
                                        ins = V.tensor_scalar(dst, nd[:, q, 0:128], den[:, q:q + 1], None, ALU.mult)
                                    else:
                                        ins = V.scalar_tensor_tensor(out=dst, in0=nd[:, q, 0:128], scalar=den[:, q:q + 1], in1=dst,
                                                                     op0=ALU.mult, op1=ALU.add)
                                ev(ins, 0, "N", h, d, tp)
                    dve.wait_ge(*after("lam_exp"))
                    V.tensor_tensor(lamc[:, 2:3], lamc[:, 1:2], lamc[:, 0:1], ALU.subtract)
                    dve.drain()
                    V.tensor_scalar(lamc[:, 3:4], lamc[:, 2:3], LAM_INIT, None, ALU.subtract)
                    dve.drain()

                    nh, hg = row(0, "headg", 0)

                    def heads_of(t, half):
                        return mix[:, t, 512 * half:512 * half + 512]

                    def head_squares(t, half):
                        if half:
                            dve.wait_ge(*after("ev", 0, "O", 4 * t + 3))
                        for h in range(4):
                            squares(heads_of(t, half)[:, h * P:(h + 1) * P], v(RAW + h * P, P), head_ss(t, half)[:, h:h + 1])

                    def head_ss(t, half, n=1):
                        return gcols[:, 16 * half + 4 * t:16 * half + 4 * (t + n)]

                    def head_norm(t, half):
                        x4 = heads_of(t, half)
                        x = x4.rearrange("p (h c) -> p h c", h=4)
                        gain = hg[:, 512 * half:512 * half + 512]
                        V.tensor_tensor(x, x, head_ss(t, half).unsqueeze(2).broadcast_to([P, 4, P]), ALU.mult)
                        dve.drain()
                        if half:
                            ins = V.scalar_tensor_tensor(out=x4, in0=x4, scalar=1.0 - LAM_INIT, in1=gain, op0=ALU.mult, op1=ALU.mult)
                            sig(ins, *([("mix", 0, t)] + ([("row", nh)] if t == 3 else [])))
                        else:
                            V.tensor_tensor(x4, x4, gain, ALU.mult)
                            dve.drain()
                            dve.wait_ge(*after("ev", 0, "o", t, 0))
                            V.tensor_tensor(x4, x4, v(OSIG + t * 512, 512), ALU.mult)

                    for step in range(16 + 2):
                        if step < 16:
                            i = step
                            t, h = i // 4, i % 4
                            nk = 256 if t < 2 else 512
                            c = 8 * (i % 4)
                            for m in range(2):
                                b = b_(0, "S", t, h, m)
                                V.tensor_reduce(small[:, c + 4 + m:c + 5 + m], bank[:, b, 0:nk], AX_X, ALU.max)
                            dve.drain()
                            sig(V.tensor_scalar(small[:, c:c + 2], small[:, c + 4:c + 6], -SCALE64, None, ALU.mult), ("smax", 0, i))
                        if 0 <= step - 2 < 16:
                            i = step - 2
                            t, h = i // 4, i % 4
                            nk = 256 if t < 2 else 512
                            c = 8 * (i % 4)
                            dve.wait_ge(*after("ev", 0, "S", t, h, 1))
                            pr0, pr1 = v(ATS + (i % 3) * 1024, nk), v(ATS + (i % 3) * 1024 + 512, nk)
                            V.reciprocal(small[:, c + 2:c + 4], small[:, c + 2:c + 4])
                            dve.drain()
                            V.tensor_scalar(pr1, pr1, small[:, c + 3:c + 4], lamc[:, 3:4], ALU.mult, ALU.mult)
                            dve.drain()
                            sig(V.scalar_tensor_tensor(out=pr0, in0=pr0, scalar=small[:, c + 2:c + 3], in1=pr1, op0=ALU.mult,
                                                       op1=ALU.add), ("Pr", 0, i))
                        if step < 4:
                            head_squares(step, 0)
                        if step == 4:
                            rsqrt(head_ss(0, 0, 4), 1.0 / P, EPS)
                        if 4 <= step < 8:
                            head_norm(step - 4, 0)
                        if step in (8, 12, 16):
                            head_squares(step // 4 - 2, 1)
                        if step == 12:
                            rsqrt(head_ss(0, 1, 2), 1.0 / P, EPS)
                        if step in (12, 13):
                            head_norm(step - 12, 1)
                    head_squares(3, 1)
                    rsqrt(head_ss(2, 1, 2), 1.0 / P, EPS)
                    head_norm(2, 1)
                    head_norm(3, 1)
                if l == 1:
                    qn, kn = v3(L1_QN, 2, 1024), v3(L1_KN, 4, 256)
                    rt = (v3(L1_P, 8, 32), v3(L1_P + 256, 8, 32))
                    for q in range(2):
                        for t in LAT:
                            b = b_(1, f"q{q}", t, 0)
                            ins = rope(groups32(qn[:, t - 2, q * 512:(q + 1) * 512]), groups32(bank[:, b, :]), t, 8, rt)
                            dve.drain()
                            more = (("q_roped", t),) if q else ()
                            ev(ins, 1, f"q{q}", t, 0, more=more)
                    rt4 = (v3(L1_P, 4, 32), v3(L1_P + 128, 4, 32))
                    for t in tiles:
                        b = b_(1, "kv", t, 0)
                        if t < 2:
                            ins = V.tensor_copy(kn[:, t, :], bank[:, b, 0:256])
                        else:
                            ins = rope(groups32(kn[:, t, :]), groups32(bank[:, b, 0:256]), t, 4, rt4)
                            dve.drain()
                        sig(ins, ("k_roped", t))
                    for t in LAT:
                        copy_T((1, "qT"), t, v3(L1_QT, 8, 256)[:, 4:8, (t - 2) * P:(t - 1) * P], 1)
                    mix = v3(MIX, 2, D)
                    V.tensor_scalar(gcols[:, 0:16], par("sink"), 1.0 / SCALE64, None, ALU.mult)
                    dve.drain()

                    for step in range(32 + 3):
                        if step < 32:
                            i = step
                            t, c, hq = i // 16, 8 * (i % 4), head_of(i)
                            b = b_(1, "S", i)
                            off = 256 + (P if t == 0 else 0)
                            V.tensor_tensor(bank[:, b, off:off + P], bank[:, b, off:off + P], const("win")[:, t * P:(t + 1) * P], ALU.add)
                            dve.drain()
                            V.tensor_reduce(small[:, c + 4:c + 5], bank[:, b, :], AX_X, ALU.max)
                            dve.drain()
                            sig(V.tensor_scalar(small[:, c:c + 1], small[:, c + 4:c + 5], gcols[:, hq:hq + 1], -SCALE64, ALU.max, ALU.mult),
                                ("smax", 1, i))
                        if 0 <= step - 3 < 32:
                            i = step - 3
                            t, c, hq = i // 16, 8 * (i % 4), head_of(i)
                            b = b_(1, "O", i)
                            V.tensor_tensor(small[:, c + 3:c + 4], small[:, c + 1:c + 2], small[:, c + 2:c + 3], ALU.add)
                            dve.drain()
                            V.reciprocal(small[:, c + 3:c + 4], small[:, c + 3:c + 4])
                            dve.drain()
                            ev(V.tensor_scalar(mix[:, t, hq * 64:hq * 64 + 64], bank[:, b, 0:64], small[:, c + 3:c + 4],
                                               None, ALU.mult), 1, "O", i)
                    dve.drain()
                    sig(dve.drain(), ("mix", 1, 2), ("mix", 1, 3))
                if l == 2:
                    z = v3(L2_Z, 4, 704)
                    nm, mg = row(2, "mlag", 0)
                    kr = v3(L2_QR, 4, P)
                    for t in LAT:
                        b = b_(2, "zq", t, 0)
                        ev(V.tensor_copy(z[:, t, 0:384], bank[:, b, 0:384]), 2, "zq", t, 0)
                        dve.drain()
                        squares(z[:, t, 0:384], v(L2_PT, 384), small[:, 32:33])
                        rsqrt(small[:, 32:33], 1.0 / 384, EPS)
                        sig(V.scalar_tensor_tensor(out=z[:, t, 0:384], in0=z[:, t, 0:384], scalar=small[:, 32:33], in1=mg[:, 0:384],
                                                   op0=ALU.mult, op1=ALU.mult), ("zq_n", t))
                    rt1 = (v3(L2_P + 512, 1, 32), v3(L2_P + 544, 1, 32))
                    for t in tiles:
                        b = b_(2, "zkv", t, 0)
                        ev(V.tensor_copy(z[:, t, 384:704], bank[:, b, 0:320]), 2, "zkv", t, 0)
                        dve.drain()
                        squares(z[:, t, 384:640], v(L2_PT, 256), small[:, 32:33])
                        rsqrt(small[:, 32:33], 1.0 / 256, EPS)
                        evs = [("zkv_n", t)] + ([("row", nm)] if t == 3 else [])
                        sig(V.scalar_tensor_tensor(out=z[:, t, 384:640], in0=z[:, t, 384:640], scalar=small[:, 32:33],
                                                   in1=mg[:, 384:640], op0=ALU.mult, op1=ALU.mult), *evs)
                        if t < 2:
                            V.tensor_copy(kr[:, t, 0:64], z[:, t, 640:704])
                        else:
                            rope(groups32(kr[:, t, 0:64]), groups32(z[:, t, 640:704]), t, 1, rt1)
                        dve.drain()
                        sig(V.tensor_copy(kr[:, t, 64:128], kr[:, t, 0:64]), ("kr", t))
                    for t in tiles:
                        if t in LAT:
                            copy_T((2, "cqT"), t, v3(L2_CQT, 3, 256)[:, :, (t - 2) * P:(t - 1) * P], 0, n=3)
                        copy_T((2, "ckvT"), t, v3(L2_CKVT, 2, TOK)[:, :, t * P:(t + 1) * P], 0, n=2)
                        copy_T((2, "krT"), t, v3(L2_KRT, 1, TOK)[:, :, t * P:(t + 1) * P], 0, n=1)
                    for c in range(1, 8, 2):
                        b = b_(2, "uqn", c)
                        ev(V.tensor_copy(v3(L2_QNT, 8, 256)[:, c, :], bank[:, b, 0:256]), 2, "uqn", c)
                    qr = v3(L2_QR, 2, 512)
                    rt = (v3(L2_P, 8, 32), v3(L2_P + 256, 8, 32))
                    for t in LAT:
                        b = b_(2, "uqr", t, 0)
                        ins = rope(groups32(qr[:, t - 2, :]), groups32(bank[:, b, :]), t, 8, rt)
                        dve.drain()
                        ev(ins, 2, "uqr", t, 0, more=(("qr_roped", t),))
                    for c in range(1, 8, 2):
                        b = b_(2, "ukn", c)
                        ev(V.tensor_copy(v3(L2_KNT, 8, TOK)[:, c, :], bank[:, b, :]), 2, "ukn", c)
                    for part in range(2):
                        for t in tiles:
                            if t % 2:
                                b = b_(2, "uv", t, part)
                                ev(V.tensor_copy(v3(L2_V, 4, 1024)[:, t, part * 512:part * 512 + 512], bank[:, b, :]), 2, "uv", t, part)
                    for t in LAT:
                        copy_T((2, "qrT"), t, v3(L2_QRT, 4, 256)[:, :, (t - 2) * P:(t - 1) * P], 0)
                    mix = v3(L2_MIX, 2, D)

                    for step in range(16 + 3):
                        if step < 16:
                            i = step
                            c = 8 * (i % 4)
                            b = b_(2, "S", i)
                            V.tensor_reduce(small[:, c + 4:c + 5], bank[:, b, :], AX_X, ALU.max)
                            dve.drain()
                            sig(V.tensor_scalar(small[:, c:c + 1], small[:, c + 4:c + 5], -SCALE_MLA, None, ALU.mult), ("smax", 2, i))
                        if 0 <= step - 3 < 16:
                            i = step - 3
                            t, h, c = i // 8, i % 8, 8 * (i % 4)
                            b = b_(2, "O", i)
                            V.reciprocal(small[:, c + 3:c + 4], small[:, c + 1:c + 2])
                            dve.drain()
                            ev(V.tensor_scalar(mix[:, t, h * P:(h + 1) * P], bank[:, b, 0:P], small[:, c + 3:c + 4],
                                               None, ALU.mult), 2, "O", i)
                    dve.drain()
                    sig(dve.drain(), ("mix", 2, 2), ("mix", 2, 3))
                if l == 3:
                    for t in LAT:
                        b = b_(3, "in1", t, 0)
                        ev(V.tensor_copy(v3(L3_Z, 2, 1024)[:, t - 2, 512:1024], bank[:, b, :]), 3, "in1", t, 0)
                    for c in range(1, 8, 2):
                        b = b_(3, "pool", c)
                        ev(V.tensor_copy(v3(L3_POOLT, 8, 256)[:, c, :], bank[:, b, 0:256]), 3, "pool", c)
                    for c in range(1, 8, 2):
                        b = b_(3, "yT", c)
                        ev(V.tensor_scalar(v3(L3_YT, 8, 256)[:, c, :], bank[:, b, 0:256], par("pool_scale")[:, c:c + 1], None, ALU.mult),
                           3, "yT", c)
                out_tiles = MIX_TILES[l]
                t0 = out_tiles[0]
                if l < 3:
                    for t in out_tiles:
                        copy_T((l, "mT"), t, mixT[:, 4:8, t * P:(t + 1) * P], 1)
                gates_ = {s: row(l, "gate1", s) for s in ((1, 0) if l == 0 else (0,))}

                def residual(y, t, c0, c1, g, tmp_, events, post):
                    V.tensor_tensor(tmp_, y, g[:, c0:c1], ALU.mult)
                    dve.drain()
                    x = H[:, t, c0:c1]
                    if post:
                        ins = V.scalar_tensor_tensor(out=x, in0=x, scalar=ALPHA, in1=tmp_, op0=ALU.mult, op1=ALU.add)
                    else:
                        ins = V.tensor_tensor(x, x, tmp_, ALU.add)
                    sig(ins, *events)

                tmpr = v(RESID, 1024)

                def mixer_residual(tiles):
                    for j in range(2):
                        for t in tiles:
                            b = b_(l, f"out{j}", t, 0)
                            ng, g = gates_[1 if t < 2 else 0]
                            evs = [("ev", l, f"out{j}", t, 0)]
                            if j == 1 and t in (1, 3):
                                evs.append(("row", ng))
                            residual(bank[:, b, :], t, j * 512, j * 512 + 512, g, tmpr[:, (t % 2) * 512:(t % 2) * 512 + 512], evs, l >= 2)

                def peer_input(r, tiles):
                    for t in tiles:
                        copy_T((r, "xT2"), t, xT2[:, 4:8, (t % 2) * P:(t % 2 + 1) * P], 1)

                if l == 0:
                    mixer_residual(CTX)
                    modulated(l, CTX, 1, ("g2", "sc2", "sh2"), [xnat_of(0, t) for t in CTX], "xnat", True)
                mixer_residual(LAT)
                sig(dve.drain(), ("ring_room", l))
                if l >= 2:
                    layernorm(l, 0)
                if l:
                    modulated(l, LAT, 0, ("g2", "sc2", "sh2"), [xnat_of(ROUNDS_OF[l][0], t) for t in LAT], "xnat", norm)

                def topk(wait, e):
                    dve.wait_ge(head_copied, wait)
                    dve.nop(nofuse=True)
                    hs = head_scores[:, :].rearrange("p (a b) -> p a b", a=2)
                    lf = left[:, :].rearrange("p (a b) -> p a b", a=2)
                    for q in range(2):
                        V.max(topv[:, q, 0:8], hs[:, q, :])
                    dve.drain()
                    for q in range(2):
                        V.max_index(topi[:, q, 0:8], topv[:, q, 0:8], hs[:, q, :])
                    for q in range(2):
                        V.match_replace(lf[:, q, :], topv[:, q, 0:8], hs[:, q, :], NEG)
                    dve.drain()
                    for q in range(2):
                        V.max(topv[:, q, 8:16], lf[:, q, :])
                    dve.drain()
                    for q in range(2):
                        V.max_index(topi[:, q, 8:16], topv[:, q, 8:16], lf[:, q, :])
                    cand = head_cand
                    V.tensor_tensor(cand.rearrange("p (a b) -> p a b", a=16), topv[:, 0, :].unsqueeze(2).broadcast_to([P, 16, 16]),
                                    topv[:, 1, :].unsqueeze(1).broadcast_to([P, 16, 16]), ALU.add)
                    dve.drain()
                    V.tensor_copy(topf[:, :, :], topi[:, :, :])
                    V.max(cv[:, 0:8], cand)
                    dve.drain()
                    V.max_index(ci[:, 0:8], cv[:, 0:8], cand)
                    V.match_replace(left[:, :], cv[:, 0:8], cand, NEG)
                    dve.drain()
                    V.max(cv[:, 8:16], left[:, :])
                    V.tensor_scalar(neg[:, :], cv[:, 0:1], -1.0, None, ALU.mult)
                    dve.drain()
                    V.max_index(ci[:, 8:16], cv[:, 8:16], left[:, :])
                    dve.drain()
                    V.tensor_scalar(ab[:, 0, :], ci[:, :], 4, None, ALU.logical_shift_right)
                    V.tensor_scalar(ab[:, 1, :], ci[:, :], 15, None, ALU.bitwise_and)
                    dve.drain()
                    V.tensor_copy(abf[:, :, :], ab[:, :, :])
                    dve.drain()
                    V.tensor_tensor(eq[:, :, :, :].rearrange("p a k m -> p (a k) m"),
                                    abf[:, :, :].rearrange("p a k -> p (a k)").unsqueeze(2).broadcast_to([P, 32, 16]),
                                    const("iota").unsqueeze(1).broadcast_to([P, 32, 16]), ALU.is_equal)
                    dve.drain()
                    for q in range(2):
                        V.tensor_tensor(eq[:, q, :, :], eq[:, q, :, :], topf[:, q, :].unsqueeze(1).broadcast_to([P, 16, 16]), ALU.mult)
                    dve.drain()
                    V.tensor_reduce(selv[:, :, :].rearrange("p a k -> p (a k)"), eq[:, :, :, :].rearrange("p a k m -> p (a k) m"),
                                    AX_X, ALU.add)
                    dve.drain()
                    V.scalar_tensor_tensor(out=ef[:, :], in0=selv[:, 0, :], scalar=float(NK), in1=selv[:, 1, :], op0=ALU.mult, op1=ALU.add)
                    dve.drain()
                    V.tensor_copy(idx[:, e, :], ef[:, :]).then_inc(topk_done, 1)

                def gates(wait, wait_free, e):
                    dve.wait_ge(exp_done, wait)
                    dve.nop(nofuse=True)
                    if wait_free is not None:
                        dve.wait_ge(diag_done, wait_free)
                        dve.nop(nofuse=True)
                    V.reciprocal(neg[:, :], es[:, :])
                    dve.drain()
                    V.tensor_scalar(gate[:, e, :], ex[:, :], neg[:, :], None, ALU.mult)

                head_cand = eq[:, 0, :, :].rearrange("p k m -> p (k m)")

                def take_query(r, hp):
                    if hp % 2:
                        b = b_(r, "q", hp)
                        ev(V.tensor_copy(qT[:, hp % 8, :], bank[:, b, 0:2 * P]), r, "q", hp)

                def take_scores(r, j):
                    b = b_(r, "sc", 1, j)
                    ev(V.tensor_copy(scores[:, PH + 2 * j:PH + 2 * j + 2, :].rearrange("p a b -> p (a b)"), bank[:, b, :]),
                       r, "sc", 1, j)

                def first_scores(r):
                    sig(V.memset(scores[:, ROUND_HEADS, :], 0.0), ("pad_scores", r))
                    k0 = r * ROUND_HEADS + r
                    for j in range(2):
                        for c in range(4):
                            take_query(r, 4 * j + c)
                        if j == 0:
                            topk(k0 + 1, 0)
                        take_scores(r, j)
                    gates(k0 + 1, None, 0)

                def peer_dots(r, i):
                    q0 = r * ROUND_HEADS + i * PH

                    def two_heads(it, then=None):
                        for e in range(2):
                            for j in range(GPH):
                                s = j % SLOTS
                                dve.wait_ge(ring_landed[s], it * (2 * GPH // SLOTS * GROUP * 16)
                                            + ((q0 * GPH + e * GPH + j) // SLOTS + 1) * GROUP * 16)
                                for x in range(GROUP):
                                    ins = V.tensor_tensor_reduce(out=ring[:, s, x, 0:D], in0=ring[:, s, x, 0:D], in1=xnat[:, i, :],
                                                                 scale=1.0, scalar=0.0, op0=ALU.mult, op1=ALU.add,
                                                                 accum_out=dot[:, s, x:x + 1])
                                ins.then_inc(dots_done, 1)
                                if j == 1:
                                    topk(it * 2 + (q0 + r + e + 2), (e + 1) % 2)
                                if j == 4:
                                    gates(it * 2 + (q0 + r + e + 2), it * (2 * GPH) + (q0 * GPH + e * GPH + 1), (e + 1) % 2)
                                if then:
                                    then(e * GPH + j)

                    def later_scores(g):
                        if 0 <= g - CHUNK_LAG < 8:
                            take_query(r, 8 + g - CHUNK_LAG)
                        if g - SCORES_LAG in SCORES_AFTER:
                            take_scores(r, SCORES_AFTER[g - SCORES_LAG])

                    if i == 0:
                        two_heads(0, later_scores)
                    with dve.Fori(1 - i, PH // 2) as it:
                        two_heads(it)

                def peer_residual(r, i):
                    dve.wait_ge(slots_free, SLOTS + (r * ROUND_HEADS + (i + 1) * PH) * GPH)
                    t = ROUNDS[r][1][i]
                    y = bank[:, 2 * i:2 * i + 2, :].rearrange("p a b -> p (a b)")
                    ng, g = row(l, "gate2", 1 if t < 2 else 0)
                    evs = [("y_taken", r, i)]
                    if i == 1:
                        evs.append(("row", ng))
                    residual(y, t, 0, D, g, xnat[:, i, :], evs, l >= 2)
                    dve.drain()

                peer_input(ROUNDS_OF[l][0], ROUNDS[ROUNDS_OF[l][0]][1])
                for r in ROUNDS_OF[l]:
                    first_scores(r)
                    peer_dots(r, 0)
                    peer_residual(r, 0)
                    if r == 0:
                        modulated(l, LAT, 0, ("g2", "sc2", "sh2"), [xnat_of(1, t) for t in LAT], "xnat", norm)
                        peer_input(1, LAT)
                    peer_dots(r, 1)
                    peer_residual(r, 1)
                    if r == 0:
                        sig(V.tensor_copy(xnat[:, 1, :], xnat_of(1, 3)), ("xnat_moved",))
                        dve.drain()
                if l == 1:
                    nf, fg = row(1, "final", 0)
                    for t in LAT:
                        squares(H[:, t, :], xnat[:, t - 2, :], small[:, 32 + t:33 + t])
                    rsqrt(small[:, 34:36], 1.0 / D, EPS)
                    for t in LAT:
                        evs = [("final1", t)] + ([("row", nf)] if t == 3 else [])
                        sig(V.scalar_tensor_tensor(out=H[:, t, :], in0=H[:, t, :], scalar=small[:, 32 + t:33 + t], in1=fg, op0=ALU.mult,
                                                   op1=ALU.mult), *evs)
                    dve.drain()
                if l >= 2:
                    layernorm(l, 1)
            sig(dve.drain(), ("final_out",))
        return st.at




def _blocks(inp, f32):
    def tiled(w, k=KC):
        return w.reshape(k, P, -1).transpose(1, 0, 2).reshape(P, -1)

    def cut(w, j, k=KC):
        return tiled(w[:, 512 * j:512 * (j + 1)], k)

    out = np.zeros((len(BLOCKS), P, WCOLS), f32)

    all_keys = np.zeros((LAYERS, P, 2 * PH * NK), f32)

    def put(name, a):
        n = BLOCK_AT[name]
        assert a.shape == (P, BLOCKS[n][1]), (name, a.shape)
        out[n, :, :a.shape[1]] = a

    for l in range(LAYERS):
        w = (inp["mod_w"] if l < 2 else inp["w_mod_2"])[l % 2]
        for n in range(MODC // 4):
            put((l, "mod", n), cut(w, n))
        wq = (inp["pr_w_q"] if l < 2 else inp["peer_w_q_2"])[l % 2]
        for r in ROUNDS_OF[l]:
            for n in range(4):
                put((l, "wq", n, r), cut(wq, n))
        if l < 2:
            keys = inp["pr_keys"][l]
        else:
            keys = np.stack([inp["peer_k1_2"][l - 2], inp["peer_k2_2"][l - 2]], axis=1)
        all_keys[l] = keys.reshape(2 * PH, NK, P).transpose(2, 0, 1).reshape(P, -1)
    w = inp["ev_w_in"][0]
    put((0, "qk"), tiled(w[:, 0:512]))
    put((0, "v"), tiled(w[:, 512:1024]))
    put((0, "o"), tiled(w[:, 1024:1536]))
    put((0, "gates"), tiled(w[:, 1536:1552]))
    for j, n in enumerate(("dq", "dk", "dv")):
        put((0, n), tiled(w[:, 1552 + 512 * j:2064 + 512 * j]))
    w = inp["od_w_in"][0]
    order = [head_of(i) for i in range(16)]
    wq = w[:, :1024].reshape(D, 16, 64)[:, order].reshape(D, 1024)
    put((1, "q0"), cut(wq, 0))
    put((1, "q1"), cut(wq, 1))
    put((1, "kv"), tiled(w[:, 1024:]))
    w = inp["mla_w_in_2"][0]
    put((2, "zq"), tiled(w[:, :384]))
    put((2, "zkv"), tiled(w[:, 384:]))
    uq = inp["mla_w_uq_2"][0].reshape(384, 8, 192)
    put((2, "uqn"), tiled(uq[:, :, :128].reshape(384, 1024), 3))
    put((2, "uqr"), tiled(uq[:, :, 128:].reshape(384, 512), 3))
    ukv = inp["mla_w_ukv_2"][0].reshape(256, 8, 256)
    put((2, "ukn"), tiled(ukv[:, :, :128].reshape(256, 1024), 2))
    put((2, "uv"), tiled(ukv[:, :, 128:].reshape(256, 1024), 2))
    put((3, "in0"), cut(inp["pool_w_in_2"][0], 0))
    put((3, "in1"), cut(inp["pool_w_in_2"][0], 1))
    band = np.zeros((SEQ, 4, SEQ), f32)
    for g, win in enumerate((2, 4, 8, 16)):
        for t in range(SEQ):
            lo, hi = max(t - win // 2, 0), min(t + win // 2, SEQ)
            band[lo:hi, g, t] = 1.0 / (hi - lo)
            band[t, g, t] -= 1.0
    put((3, "band"), tiled(band.reshape(SEQ, -1), 2))
    put((3, "grp"), inp["pool_w_grp_2"][0].reshape(4, 2, P, 256).transpose(2, 0, 1, 3).reshape(P, -1))
    for l, w in enumerate((inp["ev_w_out"][0], inp["od_w_out"][0], inp["mla_w_o_2"][0], inp["pool_w_out_2"][0])):
        put((l, "out0"), cut(w, 0))
        put((l, "out1"), cut(w, 1))
    return out, all_keys


def _consts(f32):
    c = np.zeros((P, CT_COLS), f32)
    p, j = np.arange(P)[:, None], np.arange(P)[None, :]

    def at(name):
        o, n = CT[name]
        return c[:, o:o + n]

    at("ident")[:] = np.eye(P)
    at("tri")[:, :P] = np.where(p <= j, 0, MASK)
    at("tri")[:, P:] = np.where(p >= j, 0, MASK)
    at("win")[:, :P] = np.where(j <= p, 0, MASK)
    at("win")[:, P:] = np.where(j >= p, 0, MASK)
    pos = np.arange(SEQ)
    inv = (10000.0 ** (-np.arange(16, dtype=np.float64) / 16))
    ang = np.concatenate([(pos // 64)[:, None] * inv, (pos % 64)[:, None] * inv], axis=1)
    at("cos")[:] = np.cos(ang).reshape(2, P, 32).transpose(1, 0, 2).reshape(P, 64)
    at("sin")[:] = np.sin(ang).reshape(2, P, 32).transpose(1, 0, 2).reshape(P, 64)
    at("iota")[:] = np.arange(16)[None]
    for h in range(4):
        at("sel")[h, h * P:(h + 1) * P] = 1
    at("add4")[:] = (p % 32) == np.arange(2)
    return c


def _params(inp, f32):
    c = np.zeros((P, PT_COLS), f32)

    def at(name, rows=P):
        o, n = PT_[name]
        return c[:rows, o:o + n]

    at("conv_w")[:] = inp["ev_ml_conv_w"][0].reshape(3, 4, P).transpose(2, 1, 0).reshape(P, 12)
    at("conv_b")[:] = inp["ev_ml_conv_b"][0].reshape(4, P).T
    at("gate_b")[:] = inp["ev_ml_gate_b"][0].reshape(1, 16)
    at("lam")[:] = inp["ev_da_lam"][0].reshape(1, 256)
    at("sink")[:] = inp["od_sink"][0].reshape(1, 16)
    at("pool_scale")[:] = inp["pool_scale_2"][0].reshape(8, P).T
    cond = np.stack([inp["c"][0], inp["c_ctx"], inp["c_2"][0], inp["c_ctx_2"]])
    at("cond")[:, 0:32] = cond.reshape(4, KC, P).transpose(2, 1, 0).reshape(P, 32)
    mb = np.concatenate([inp["mod_b"], inp["b_mod_2"]])
    at("mod_b")[:] = mb.reshape(LAYERS, MODC, P).transpose(2, 0, 1).reshape(P, -1)
    return c


def _gains(inp, f32):
    g = np.zeros((15, D), f32)
    for l in range(2):
        g[GAIN[("norm1", l)]] = inp["norm1_g"][l]
        g[GAIN[("norm2", l)]] = inp["norm2_g"][l]
        for s in range(2):
            g[GAIN[("lng", l + 2, s)]] = inp["ln_g_2"][l, s]
            g[GAIN[("lnb", l + 2, s)]] = inp["ln_b_2"][l, s]
    g[GAIN["headg"]] = np.concatenate([inp["ev_ml_norm_g"][0], inp["ev_da_norm_g"][0]])
    g[GAIN["final"]] = inp["final_g"]
    g[GAIN["mlag"], :384] = inp["mla_q_norm_2"][0]
    g[GAIN["mlag"], 384:640] = inp["mla_kv_norm_2"][0]
    return g


def layout(inputs):
    inp = {k: np.asarray(a) for k, a in inputs.items()}
    f32 = np.float32

    def tok(a):
        return a[0].reshape(2, P, D).transpose(1, 0, 2)

    arrays = {
        "hidden": np.ascontiguousarray(np.concatenate([tok(inp["ctx"]), tok(inp["x"])], axis=1)),
        "ctx2": np.ascontiguousarray(tok(inp["ctx_2"])),
        "consts": _consts(f32),
        "params": _params(inp, f32),
        "gains": _gains(inp, f32),
    }
    arrays["weights"], arrays["keys"] = _blocks(inp, f32)
    for l in range(LAYERS):
        u = inp["pr_u" if l < 2 else "peer_u_2"][l % 2]
        v = inp["pr_v" if l < 2 else "peer_v_2"][l % 2]
        arrays[f"uv{l}"] = np.concatenate([u, v], axis=1)
    return arrays


def build(make, arrays):
    known = {}
    for _ in range(2):
        nc = make()
        A = {n: nc.dram_tensor(n, a.shape, mybir.dt.from_np(a.dtype), kind="ExternalInput").ap() for n, a in arrays.items()}
        A["out"] = nc.dram_tensor("out", (P, 2, D), F32, kind="ExternalOutput").ap()
        known = program(nc, A, known)
    return nc


def kernel(**inputs):
    import concourse.bacc as bacc
    from concourse.bass_utils import run_bass_kernel_spmd

    arrays = layout(inputs)
    nc = build(lambda: bacc.Bacc("TRN2", target_bir_lowering=False, num_devices=1), arrays)
    r = run_bass_kernel_spmd(nc, [arrays], core_ids=[0])
    out = r.results[0]["out"]
    return np.ascontiguousarray(out.transpose(1, 0, 2).reshape(1, SEQ, D))
```
